# Optimizing a Trainium2 kernel written in Bass

```python
import math
import jax
import jax.numpy as jnp
from jax import lax
import numpy as np

D_MODEL = 1024
BATCH = 1
SEQ = 128
DEPTH = 1
DEC_BATCH = 1
DEC_SEQ = 256
PAST_LEN = 128

GRID_W = 64
POS_BASE = 10000.0
EPS = 1e-6
CONV_W = 5
N_MOD = 6
SSD_HEADS = 16
SSD_HEAD_DIM = 64
SSD_WIDTH = SSD_HEADS * SSD_HEAD_DIM
SSD_GROUPS = 2
SSD_STATE = 64
SSD_CHUNK = 128
SSD_XBC = SSD_WIDTH + 2 * SSD_GROUPS * SSD_STATE
DN_HEADS = 8
DN_HEAD_DIM = 128
DN_WIDTH = DN_HEADS * DN_HEAD_DIM
DN_CHUNK = 64
MIX_WIDTH = SSD_WIDTH + DN_WIDTH
IN_COLS = SSD_WIDTH + SSD_XBC + 2 * SSD_HEADS + 3 * DN_WIDTH + DN_WIDTH + 2 * DN_HEADS + 2 * DN_HEADS
N_EXPERT_GROUPS = 4
EXPERTS_PER_GROUP = 8
N_EXPERTS = N_EXPERT_GROUPS * EXPERTS_PER_GROUP
TOP_K = 2
D_FF_EXPERT = 512

kernel_name = 'hybrid_ssd_deltanet_hmoe_diffusion_step'

def rmsnorm(x, w):
    xf = x.astype(jnp.float32)
    y = xf * lax.rsqrt(jnp.mean(xf * xf, axis=-1, keepdims=True) + EPS)
    return (y * w.astype(jnp.float32)).astype(x.dtype)

def l2norm(x):
    xf = x.astype(jnp.float32)
    return xf * lax.rsqrt(jnp.sum(xf * xf, axis=-1, keepdims=True) + EPS)

def rev(t):
    return jnp.flip(t, axis=1)

def grid_sincos_2d(n_tokens):
    rows = n_tokens // GRID_W
    quarter = D_MODEL // 4
    omega = 1.0 / (POS_BASE ** (jnp.arange(quarter, dtype=jnp.float32) / quarter))
    r = jnp.broadcast_to(jnp.arange(rows, dtype=jnp.float32)[:, None], (rows, GRID_W)).reshape(-1)
    col = jnp.broadcast_to(jnp.arange(GRID_W, dtype=jnp.float32)[None, :], (rows, GRID_W)).reshape(-1)
    ar = r[:, None] * omega
    ac = col[:, None] * omega
    return jnp.concatenate([jnp.sin(ar), jnp.cos(ar), jnp.sin(ac), jnp.cos(ac)], axis=-1)

def centred_dwconv(x, w, b):
    ch = x.shape[-1]
    y = lax.conv_general_dilated(x, w[:, None, :].astype(x.dtype), window_strides=(1,),
                                 padding=((CONV_W // 2, CONV_W // 2),),
                                 dimension_numbers=('NWC', 'WIO', 'NWC'),
                                 feature_group_count=ch)
    return y + b.astype(x.dtype)

def ssd_chunked(x, dt, a_neg, bmat, cmat, h0):
    f32 = jnp.float32
    bsz, seqlen, nh, hp = x.shape
    ng, ns = bmat.shape[2], bmat.shape[3]
    hg = nh // ng
    q = SSD_CHUNK
    nc = seqlen // q
    x = x.astype(f32).reshape(bsz, nc, q, ng, hg, hp)
    dt = dt.astype(f32).reshape(bsz, nc, q, ng, hg)
    bmat = bmat.astype(f32).reshape(bsz, nc, q, ng, ns)
    cmat = cmat.astype(f32).reshape(bsz, nc, q, ng, ns)
    acum = jnp.cumsum(dt * a_neg.astype(f32).reshape(ng, hg), axis=2)
    lower = jnp.tril(jnp.ones((q, q), bool))
    seg = acum[:, :, :, None] - acum[:, :, None]
    decay = jnp.exp(jnp.where(lower[:, :, None, None], seg, -jnp.inf))
    cb = jnp.einsum('bcign,bcjgn->bcijg', cmat, bmat)
    xdt = x * dt[..., None]
    y_diag = jnp.einsum('bcijgh,bcjghp->bcighp', cb[..., None] * decay, xdt)
    end_decay = jnp.exp(acum[:, :, -1:] - acum)
    states = jnp.einsum('bcjgn,bcjghp->bcghpn', bmat, xdt * end_decay[..., None])
    chunk_decay = jnp.exp(acum[:, :, -1])

    def step(h, inp):
        s_c, d_c = inp
        return h * d_c[..., None, None] + s_c, h

    h_last, h_prev = lax.scan(step, h0.astype(f32).reshape(bsz, ng, hg, hp, ns),
                              (jnp.moveaxis(states, 1, 0), jnp.moveaxis(chunk_decay, 1, 0)))
    h_prev = jnp.moveaxis(h_prev, 0, 1)
    y_off = jnp.einsum('bcign,bcghpn->bcighp', cmat, h_prev) * jnp.exp(acum)[..., None]
    y = (y_diag + y_off).reshape(bsz, seqlen, nh, hp)
    return y, h_last.reshape(bsz, nh, hp, ns)

def gated_delta_chunked(q, k, v, g, beta, s0):
    f32 = jnp.float32
    bsz, seqlen, nh, dk = q.shape
    dv = v.shape[-1]
    c = DN_CHUNK
    nc = seqlen // c

    def chunks(t):
        return t.astype(f32).reshape(bsz, nc, c, nh, -1).transpose(0, 1, 3, 2, 4)

    q = chunks(q) * (dk ** -0.5)
    k = chunks(k)
    v = chunks(v)
    g = g.astype(f32).reshape(bsz, nc, c, nh).transpose(0, 1, 3, 2)
    beta = beta.astype(f32).reshape(bsz, nc, c, nh).transpose(0, 1, 3, 2)
    gc = jnp.cumsum(g, axis=-1)
    incl = jnp.tril(jnp.ones((c, c), bool))
    strict = jnp.tril(jnp.ones((c, c), bool), -1)
    decay = jnp.exp(jnp.where(incl, gc[..., :, None] - gc[..., None, :], -jnp.inf))
    kk = jnp.einsum('bnhik,bnhjk->bnhij', k, k)
    t_mat = jnp.where(strict, kk * decay * beta[..., None], 0.0) + jnp.eye(c, dtype=f32)
    rhs = jnp.concatenate([v * beta[..., None], k * (beta * jnp.exp(gc))[..., None]], axis=-1)
    sol = lax.linalg.triangular_solve(t_mat, rhs, left_side=True, lower=True, unit_diagonal=True)
    u = sol[..., :dv]
    w = sol[..., dv:]
    qk = jnp.einsum('bnhik,bnhjk->bnhij', q, k) * decay
    q_dec = q * jnp.exp(gc)[..., None]
    k_dec = k * jnp.exp(gc[..., -1:] - gc)[..., None]
    cdec = jnp.exp(gc[..., -1])

    def step(s, inp):
        qk_i, qd_i, kd_i, u_i, w_i, cd_i = inp
        v_new = u_i - jnp.einsum('bhck,bhkv->bhcv', w_i, s)
        o = jnp.einsum('bhck,bhkv->bhcv', qd_i, s) + jnp.einsum('bhij,bhjv->bhiv', qk_i, v_new)
        s = s * cd_i[..., None, None] + jnp.einsum('bhck,bhcv->bhkv', kd_i, v_new)
        return s, o

    xs = (jnp.moveaxis(qk, 1, 0), jnp.moveaxis(q_dec, 1, 0), jnp.moveaxis(k_dec, 1, 0),
          jnp.moveaxis(u, 1, 0), jnp.moveaxis(w, 1, 0), jnp.moveaxis(cdec, 1, 0))
    s_last, o = lax.scan(step, s0.astype(f32), xs)
    o = jnp.moveaxis(o, 0, 1).transpose(0, 1, 3, 2, 4).reshape(bsz, seqlen, nh, dv)
    return o, s_last

def hybrid_mixer(h, lp, init):
    f32 = jnp.float32
    bsz, seqlen, _ = h.shape
    proj = h @ lp['w_in']
    cuts = [SSD_WIDTH, SSD_XBC, 2 * SSD_HEADS, 3 * DN_WIDTH, DN_WIDTH, 2 * DN_HEADS]
    z_s, xbc, dt_s, qkv, z_d, a_d, b_d = jnp.split(proj, list(np.cumsum(cuts)), axis=-1)

    xbc = jax.nn.silu(centred_dwconv(xbc, lp['conv_ssd_w'], lp['conv_ssd_b']))
    xs, bm, cm = jnp.split(xbc, [SSD_WIDTH, SSD_WIDTH + SSD_GROUPS * SSD_STATE], axis=-1)
    xs = xs.reshape(bsz, seqlen, SSD_HEADS, SSD_HEAD_DIM)
    bm = bm.reshape(bsz, seqlen, SSD_GROUPS, SSD_STATE)
    cm = cm.reshape(bsz, seqlen, SSD_GROUPS, SSD_STATE)
    dt = jax.nn.softplus(dt_s.astype(f32).reshape(bsz, seqlen, 2, SSD_HEADS) + lp['ssd_dt_bias'].astype(f32))
    a_neg = -jnp.exp(lp['ssd_a_log'].astype(f32))
    y_f, s_f = ssd_chunked(xs, dt[:, :, 0], a_neg[0], bm, cm, init[0])
    y_b, s_b = ssd_chunked(rev(xs), rev(dt[:, :, 1]), a_neg[1], rev(bm), rev(cm), init[1])
    y = y_f + rev(y_b) + lp['ssd_d'].astype(f32)[:, None] * xs.astype(f32)
    y = y.reshape(bsz, seqlen, SSD_WIDTH) * jax.nn.silu(z_s.astype(f32))
    y_ssd = rmsnorm(y, lp['ssd_norm_w']).astype(h.dtype)

    qkv = jax.nn.silu(centred_dwconv(qkv, lp['conv_dn_w'], lp['conv_dn_b']))
    q, k, v = jnp.split(qkv, 3, axis=-1)
    q = l2norm(q.reshape(bsz, seqlen, DN_HEADS, DN_HEAD_DIM))
    k = l2norm(k.reshape(bsz, seqlen, DN_HEADS, DN_HEAD_DIM))
    v = v.reshape(bsz, seqlen, DN_HEADS, DN_HEAD_DIM)
    beta = jax.nn.sigmoid(b_d.astype(f32).reshape(bsz, seqlen, 2, DN_HEADS))
    g = -jnp.exp(lp['dn_a_log'].astype(f32)) * jax.nn.softplus(
        a_d.astype(f32).reshape(bsz, seqlen, 2, DN_HEADS) + lp['dn_dt_bias'].astype(f32))
    o_f, d_f = gated_delta_chunked(q, k, v, g[:, :, 0], beta[:, :, 0], init[2])
    o_b, d_b = gated_delta_chunked(rev(q), rev(k), rev(v), rev(g[:, :, 1]), rev(beta[:, :, 1]), init[3])
    o = rmsnorm(o_f + rev(o_b), lp['dn_norm_w']) * jax.nn.silu(
        z_d.astype(f32).reshape(bsz, seqlen, DN_HEADS, DN_HEAD_DIM))
    y_dn = o.reshape(bsz, seqlen, DN_WIDTH).astype(h.dtype)

    out = jnp.concatenate([y_ssd, y_dn], axis=-1) @ lp['w_out']
    return out, (s_f, s_b, d_f, d_b)

def hier_moe(h, lp):
    bsz, seqlen, d = h.shape
    t = h.reshape(bsz * seqlen, d)
    g_logits = (t @ lp['w_router_group'] + lp['b_router_group']).astype(jnp.float32)
    g_w, g_idx = lax.top_k(jax.nn.softmax(g_logits, axis=-1), 1)
    e_logits = (t @ lp['w_router_expert'] + lp['b_router_expert']).astype(jnp.float32)
    e_logits = e_logits.reshape(-1, N_EXPERT_GROUPS, EXPERTS_PER_GROUP)
    e_logits = jnp.einsum('tge,tg->te', e_logits,
                          jax.nn.one_hot(g_idx[:, 0], N_EXPERT_GROUPS, dtype=jnp.float32))
    e_w, e_idx = lax.top_k(jax.nn.softmax(e_logits, axis=-1), TOP_K)
    gate = g_w * e_w / jnp.sum(e_w, axis=-1, keepdims=True)
    ids = g_idx * EXPERTS_PER_GROUP + e_idx
    comb = jnp.einsum('tk,tke->te', gate,
                      jax.nn.one_hot(ids, N_EXPERTS, dtype=jnp.float32)).astype(h.dtype)
    out = jnp.zeros_like(t)
    for grp in range(N_EXPERT_GROUPS):
        sl = slice(grp * EXPERTS_PER_GROUP, (grp + 1) * EXPERTS_PER_GROUP)
        a = jnp.einsum('td,edf->tef', t, lp['w_gate'][sl])
        u = jnp.einsum('td,edf->tef', t, lp['w_up'][sl])
        act = jax.nn.silu(a) * u * comb[:, sl, None]
        out = out + jnp.einsum('tef,efd->td', act, lp['w_down'][sl])
    return out.reshape(bsz, seqlen, d)

def adaln_mod(cond, lp):
    m = jax.nn.silu(cond) @ lp['w_ada'] + lp['b_ada']
    return m.reshape(cond.shape[0], N_MOD, 1, D_MODEL)

def trunk_layer(x, mod, lp, init):
    mod = mod.astype(x.dtype)
    sh1, sc1, gt1, sh2, sc2, gt2 = (mod[:, i] for i in range(N_MOD))
    h = rmsnorm(x, lp['norm1_w']) * (1 + sc1) + sh1
    m, states = hybrid_mixer(h, lp, init)
    x = x + gt1 * m
    h = rmsnorm(x, lp['norm2_w']) * (1 + sc2) + sh2
    x = x + gt2 * hier_moe(h, lp)
    return x, states

def setup_inputs(seed: int = 0) -> dict:
    key = jax.random.key(seed)
    k = jax.random.split(key, 34)
    f32 = jnp.float32

    def nrm(kk, shape, scale):
        return scale * jax.random.normal(kk, shape, f32)

    def dt_bias(kk, shape):
        dt = jnp.exp(jax.random.uniform(kk, shape, f32, minval=math.log(1e-3), maxval=math.log(1e-1)))
        return dt + jnp.log(-jnp.expm1(-dt))

    def a_log(kk, shape):
        return jnp.log(jax.random.uniform(kk, shape, f32, minval=1.0, maxval=16.0))

    return {
        'x_prompt': nrm(k[0], (BATCH, SEQ, D_MODEL), 1.0),
        'x_sample': nrm(k[1], (DEC_BATCH, DEC_SEQ, D_MODEL), 1.0),
        'state_ssd_fwd': nrm(k[2], (DEC_BATCH, DEPTH, SSD_HEADS, SSD_HEAD_DIM, SSD_STATE), 0.1),
        'state_ssd_bwd': nrm(k[3], (DEC_BATCH, DEPTH, SSD_HEADS, SSD_HEAD_DIM, SSD_STATE), 0.1),
        'state_dn_fwd': nrm(k[4], (DEC_BATCH, DEPTH, DN_HEADS, DN_HEAD_DIM, DN_HEAD_DIM), 0.1),
        'state_dn_bwd': nrm(k[5], (DEC_BATCH, DEPTH, DN_HEADS, DN_HEAD_DIM, DN_HEAD_DIM), 0.1),
        'c': nrm(k[6], (DEC_BATCH, D_MODEL), 1.0),
        'c_ctx': nrm(k[7], (D_MODEL,), 1.0),
        'w_ada': nrm(k[8], (DEPTH, D_MODEL, N_MOD * D_MODEL), 0.5 * D_MODEL ** -0.5),
        'b_ada': nrm(k[9], (DEPTH, N_MOD * D_MODEL), 0.02),
        'norm1_w': 1.0 + nrm(k[10], (DEPTH, D_MODEL), 0.02),
        'w_in': nrm(k[11], (DEPTH, D_MODEL, IN_COLS), D_MODEL ** -0.5),
        'conv_ssd_w': nrm(k[12], (DEPTH, CONV_W, SSD_XBC), CONV_W ** -0.5),
        'conv_ssd_b': nrm(k[13], (DEPTH, SSD_XBC), 0.02),
        'conv_dn_w': nrm(k[14], (DEPTH, CONV_W, 3 * DN_WIDTH), CONV_W ** -0.5),
        'conv_dn_b': nrm(k[15], (DEPTH, 3 * DN_WIDTH), 0.02),
        'ssd_dt_bias': dt_bias(k[16], (DEPTH, 2, SSD_HEADS)),
        'ssd_a_log': a_log(k[17], (DEPTH, 2, SSD_HEADS)),
        'ssd_d': 1.0 + nrm(k[18], (DEPTH, SSD_HEADS), 0.02),
        'ssd_norm_w': 1.0 + nrm(k[19], (DEPTH, SSD_WIDTH), 0.02),
        'dn_dt_bias': dt_bias(k[20], (DEPTH, 2, DN_HEADS)),
        'dn_a_log': a_log(k[21], (DEPTH, 2, DN_HEADS)),
        'dn_norm_w': 1.0 + nrm(k[22], (DEPTH, DN_HEAD_DIM), 0.02),
        'w_out': nrm(k[23], (DEPTH, MIX_WIDTH, D_MODEL), MIX_WIDTH ** -0.5),
        'norm2_w': 1.0 + nrm(k[24], (DEPTH, D_MODEL), 0.02),
        'w_router_group': nrm(k[25], (DEPTH, D_MODEL, N_EXPERT_GROUPS), D_MODEL ** -0.5),
        'b_router_group': nrm(k[26], (DEPTH, N_EXPERT_GROUPS), 0.01),
        'w_router_expert': nrm(k[27], (DEPTH, D_MODEL, N_EXPERTS), D_MODEL ** -0.5),
        'b_router_expert': nrm(k[28], (DEPTH, N_EXPERTS), 0.01),
        'w_gate': nrm(k[29], (DEPTH, N_EXPERTS, D_MODEL, D_FF_EXPERT), D_MODEL ** -0.5),
        'w_up': nrm(k[30], (DEPTH, N_EXPERTS, D_MODEL, D_FF_EXPERT), D_MODEL ** -0.5),
        'w_down': nrm(k[31], (DEPTH, N_EXPERTS, D_FF_EXPERT, D_MODEL), D_FF_EXPERT ** -0.5),
        'final_norm_w': 1.0 + nrm(k[32], (D_MODEL,), 0.02),
    }

def reference(x_prompt, x_sample, state_ssd_fwd, state_ssd_bwd, state_dn_fwd, state_dn_bwd, c, c_ctx,
              w_ada, b_ada, norm1_w, w_in, conv_ssd_w, conv_ssd_b, conv_dn_w, conv_dn_b,
              ssd_dt_bias, ssd_a_log, ssd_d, ssd_norm_w, dn_dt_bias, dn_a_log, dn_norm_w, w_out,
              norm2_w, w_router_group, b_router_group, w_router_expert, b_router_expert,
              w_gate, w_up, w_down, final_norm_w):
    nb = x_prompt.shape[0]
    zero_init = (jnp.zeros((nb, SSD_HEADS, SSD_HEAD_DIM, SSD_STATE), jnp.float32),
                 jnp.zeros((nb, SSD_HEADS, SSD_HEAD_DIM, SSD_STATE), jnp.float32),
                 jnp.zeros((nb, DN_HEADS, DN_HEAD_DIM, DN_HEAD_DIM), jnp.float32),
                 jnp.zeros((nb, DN_HEADS, DN_HEAD_DIM, DN_HEAD_DIM), jnp.float32))
    xc = x_prompt
    xl = x_sample + grid_sincos_2d(x_sample.shape[1]).astype(x_sample.dtype)
    ctx_states = ([], [], [], [])
    for layer in range(DEPTH):
        lp = {
            'w_ada': w_ada[layer], 'b_ada': b_ada[layer], 'norm1_w': norm1_w[layer],
            'w_in': w_in[layer], 'conv_ssd_w': conv_ssd_w[layer], 'conv_ssd_b': conv_ssd_b[layer],
            'conv_dn_w': conv_dn_w[layer], 'conv_dn_b': conv_dn_b[layer],
            'ssd_dt_bias': ssd_dt_bias[layer], 'ssd_a_log': ssd_a_log[layer], 'ssd_d': ssd_d[layer],
            'ssd_norm_w': ssd_norm_w[layer], 'dn_dt_bias': dn_dt_bias[layer], 'dn_a_log': dn_a_log[layer],
            'dn_norm_w': dn_norm_w[layer], 'w_out': w_out[layer], 'norm2_w': norm2_w[layer],
            'w_router_group': w_router_group[layer], 'b_router_group': b_router_group[layer],
            'w_router_expert': w_router_expert[layer], 'b_router_expert': b_router_expert[layer],
            'w_gate': w_gate[layer], 'w_up': w_up[layer], 'w_down': w_down[layer],
        }
        xc, st = trunk_layer(xc, adaln_mod(c_ctx[None, :], lp), lp, zero_init)
        for lst, s in zip(ctx_states, st):
            lst.append(s)
        lat_init = (state_ssd_fwd[:, layer], state_ssd_bwd[:, layer],
                    state_dn_fwd[:, layer], state_dn_bwd[:, layer])
        xl, _ = trunk_layer(xl, adaln_mod(c, lp), lp, lat_init)
    y_prompt = rmsnorm(xc, final_norm_w)
    y_sample = rmsnorm(xl, final_norm_w)
    new_ssd_fwd = jnp.stack(ctx_states[0], axis=1).astype(x_prompt.dtype)
    new_ssd_bwd = jnp.stack(ctx_states[1], axis=1).astype(x_prompt.dtype)
    new_dn_fwd = jnp.stack(ctx_states[2], axis=1).astype(x_prompt.dtype)
    new_dn_bwd = jnp.stack(ctx_states[3], axis=1).astype(x_prompt.dtype)
    return (y_prompt, y_sample, new_ssd_fwd, new_ssd_bwd, new_dn_fwd, new_dn_bwd)


_drawn_inputs = setup_inputs


def setup_inputs(seed=0):
    import zlib

    import numpy as np

    out = dict(_drawn_inputs(seed))
    spreads = {}
    factors = {'state_ssd_fwd': 3.633,
     'state_dn_fwd': 6.855,
     'state_dn_bwd': 3.337,
     'ssd_d': 8.0,
     'ssd_norm_w': 8.0,
     'dn_norm_w': 8.0,
     'norm2_w': 6.366,
     'b_router_group': 8.0,
     'b_router_expert': 8.0,
     'final_norm_w': 2.733}
    for name, (base, spread) in spreads.items():
        noise = np.random.default_rng([zlib.crc32(name.encode()), seed]).standard_normal(out[name].shape)
        drawn = base * np.exp(spread * noise) if base else spread * noise
        out[name] = jnp.asarray(drawn.astype(out[name].dtype))
    for name, factor in factors.items():
        out[name] = (out[name] * factor).astype(out[name].dtype)
    return out
```

```python
import concourse.bass as bass
from concourse import mybir
from contextlib import ExitStack

P = 128
D_MODEL = 1024
KD = D_MODEL // P
SEQ, DEC_SEQ = 128, 256
TOK = SEQ + DEC_SEQ
TT = TOK // P
SEGS = ((0, SEQ), (SEQ, TOK))
EPS = 1e-6
CONV_W = 5
N_MOD = 6
NBM = N_MOD * KD
SSD_HEADS, SSD_HEAD_DIM, SSD_STATE, SSD_GROUPS = 16, 64, 64, 2
SSD_WIDTH = SSD_HEADS * SSD_HEAD_DIM
SSD_XBC = SSD_WIDTH + 2 * SSD_GROUPS * SSD_STATE
DN_HEADS, DN_HEAD_DIM, DN_CHUNK = 8, 128, 64
DN_WIDTH = DN_HEADS * DN_HEAD_DIM
N_GROUPS, PER_GROUP = 4, 8
N_EXPERTS = N_GROUPS * PER_GROUP
N_ROUTE = N_GROUPS + N_EXPERTS
F_EXP = 512
FK = F_EXP // P
CHUNK_COLS = 512

XBC0 = SSD_WIDTH
DT0 = XBC0 + SSD_XBC
QKV0 = DT0 + 2 * SSD_HEADS
ZD0 = QKV0 + 3 * DN_WIDTH
AB0 = ZD0 + DN_WIDTH
N_DT = 2 * SSD_HEADS
N_AB = 4 * DN_HEADS
CONV_BLOCKS = (SSD_XBC + 3 * DN_WIDTH) // P

_cols, PC = 0, {}
for _name, _n in (("c", 2 * KD), ("b_ada", NBM), ("norm1", KD), ("norm2", KD), ("final", KD),
                  ("ssd_norm", KD), ("dn_norm", 1), ("ssd_d", KD), ("conv_w", CONV_BLOCKS * CONV_W),
                  ("conv_b", CONV_BLOCKS), ("gate_bias", 48), ("a_log", 48), ("route_bias", N_ROUTE), ("desc8", 8), ("tok_id", TT)):
    PC[_name] = (_cols, _cols + _n)
    _cols += _n
N_PC = _cols

LEVELS = (1, 2, 4, 8, 16, 32)
MASKS = ["ident", "ones", "upper", "lower", "upper64", "lower64", "ones64", "first64", "last64", "strict_up"] + \
        [f"lev{d}_{m}" for d in (0, 1) for m in LEVELS] + ["iota", "eps"]
MI = {n: i for i, n in enumerate(MASKS)}


def hybrid_step(nc, x_t, xs_t, pos_t, params, masks, w_ada, w_in, w_out, h0_ssd, s0_dn, router, w_gate, w_up, w_down,
                h2_dram, outs):
    fp32 = mybir.dt.float32
    ALU = mybir.AluOpType
    ACT = mybir.ActivationFunctionType
    ctx = ExitStack()
    with ctx:
        def sb(name, shape, dt=fp32):
            return ctx.enter_context(nc.sbuf_tensor(name, shape, dt))

        def sem(name):
            return ctx.enter_context(nc.semaphore(name))

        RING = 4
        ring = sb("ring", [P, RING, KD, CHUNK_COLS])
        buf_h = sb("buf_h", [P, KD * TOK])
        mix = sb("mix", [P, 2 * KD, TOK])
        x_ssd = sb("x_ssd", [P, KD, TOK])
        bc = sb("bc", [P, 2, TOK])
        q_t = sb("q_t", [P, KD, TOK])
        kv = sb("kv", [P, 2 * KD, TOK])
        k_t, v_t = kv[:, 0:KD, :], kv[:, KD:2 * KD, :]
        masks_sb = sb("masks_sb", [P, len(MASKS), P])
        pc = sb("pc", [P, N_PC])
        mod = sb("mod", [P, NBM, 2])
        amp1 = sb("amp1", [P, KD, 2])
        silu_c = sb("silu_c", [P, 2 * KD])
        w_ab = sb("w_ab", [P, KD, N_AB])
        gates = sb("gates", [P, TT, 256])
        cums = sb("cums", [P, TT, P])
        b_tok = sb("b_tok", [P, TT, P])
        temp = sb("temp", [P, 8704])

        def carve(start, *dims):
            n = 1
            for d in dims:
                n *= d
            v = temp[:, start:start + n]
            if len(dims) == 1:
                return v
            names = "abcd"[:len(dims)]
            return v.rearrange(f"p ({' '.join(names)}) -> p {' '.join(names)}", **{c: d for c, d in zip(names[1:], dims[1:])})

        ps = ctx.enter_context(nc.psum_tensor("ps", [P, 8, 512], fp32))

        def mask(name):
            return masks_sb[:, MI[name], :]

        def col(name, i=0):
            a = PC[name][0] + i
            return pc[:, a:a + 1]

        def cols(name):
            a, b = PC[name]
            return pc[:, a:b]

        x0_t = q_t
        h1_t = buf_h[:, :].rearrange("p (k t) -> p k t", k=KD)
        x_tok = buf_h[:, :].rearrange("p (t c) -> p t c", t=TT)
        k_tok = x_tok
        v_tok = x_ssd[:, :, :].rearrange("p k t -> p (k t)").rearrange("p (t c) -> p t c", t=TT)
        o_t = v_t
        g_log, g_dt, g_beta = gates[:, :, 0:48], gates[:, :, 48:80], gates[:, :, 80:96]
        g_dte, g_be, g_nec, g_tot = gates[:, :, 96:128], gates[:, :, 128:144], gates[:, :, 144:160], gates[:, :, 160:240]

        wi = w_in.rearrange("(k p) n -> p k n", p=P)
        wa = w_ada.rearrange("(k p) n -> p k n", p=P)
        wo = w_out.rearrange("(k p) n -> p k n", p=P)
        ada = lambda g: [(wa[:, :, c * 512:(c + 1) * 512], 512) for c in range(4 * g, 4 * g + 4)]
        proj_cols = [(XBC0, 512), (XBC0 + 512, 512), (XBC0 + 1024, 288)] + \
                    [(QKV0 + 512 * c, 512) for c in range(6)] + [(0, 512), (512, 512), (ZD0, 512), (ZD0 + 512, 512)]
        loads = ada(0) + [(wi[:, :, a:a + n], n) for a, n in proj_cols] + ada(1) + ada(2) + \
            [(wo[:, kh * KD:(kh + 1) * KD, dh * 512:(dh + 1) * 512], 512) for dh in range(2) for kh in range(2)]
        LOAD_PROJ, LOAD_ADA1, LOAD_ADA2, LOAD_OUT = 4, 17, 21, 25
        blocks = []
        for n, (a, w) in enumerate(proj_cols):
            for b in range(w // P):
                i = len(blocks)
                blocks.append((LOAD_PROJ + n, b * P, "conv" if i < CONV_BLOCKS else "z", i if i < CONV_BLOCKS else i - CONV_BLOCKS))
        NB = len(blocks)

        def conv_dest(i):
            if i < 8:
                return x_ssd[:, i, :]
            if i < 10:
                return bc[:, i - 8, :]
            return (q_t, k_t, v_t)[(i - 10) // KD][:, (i - 10) % KD, :]

        pc_in = sem("pc_in")
        x_in = sem("x_in")
        masks_in = sem("masks_in")
        wab_in = sem("wab_in")
        h0_in = sem("h0_in")
        s0_in = sem("s0_in")
        w_in_sem = [sem(f"w_ready{i}") for i in range(RING)]
        dve_step = sem("dve_step")
        act_step = sem("act_step")
        silu_ready = sem("silu_ready")
        x_ready = sem("x_ready")
        sq_ready = sem("sq_ready")
        stat_ready = sem("stat_ready")
        rs_ready = sem("rs_ready")
        ada_mm = sem("ada_mm")
        row_ready = sem("row_ready")
        modp_ready = sem("modp_ready")
        mod_ready = sem("mod_ready")
        h1_ready = sem("h1_ready")
        block_mm = sem("block_mm")
        block_out = sem("block_out")
        pad_ready = sem("pad_ready")
        conv_done = sem("conv_done")
        conv_out = sem("conv_out")
        tok_mm = sem("tok_mm")
        na_ready = sem("na_ready")
        ln_ready = sem("ln_ready")
        log_ready = sem("log_ready")
        cum_mm = sem("cum_mm")
        cum_ready = sem("cum_ready")
        exps_ready = sem("exps_ready")
        gates_ready = sem("gates_ready")
        qk_sq = sem("qk_sq")
        qk_sum = sem("qk_sum")
        qk_rs = sem("qk_rs")
        qk_ready = sem("qk_ready")
        xt_mm = sem("xt_mm")
        xt_ready = sem("xt_ready")
        xe_ready = sem("xe_ready")
        st_mm = sem("st_mm")
        st_out = sem("st_out")
        h_ready = sem("h_ready")
        cb_mm = sem("cb_mm")
        cb_ready = sem("cb_ready")
        seg_mm = sem("seg_mm")
        seg_ready = sem("seg_ready")
        dec_ready = sem("dec_ready")
        m_ready = sem("m_ready")
        y_mm = sem("y_mm")
        y_ready = sem("y_ready")
        ynorm_ready = sem("ynorm_ready")
        states_out = sem("states_out")
        out_mm = sem("out_mm")
        kvt_mm = sem("kvt_mm")
        kvt_ready = sem("kvt_ready")
        s_zero = sem("s_zero")
        two = lambda name: [sem(f"{name}_fwd"), sem(f"{name}_bwd")]
        dseg_mm = two("dseg_mm")
        kq_mm = two("kq_mm")
        dseg_ready = two("dseg_ready")
        e_ready = two("e_ready")
        dec_exp = two("dec_exp")
        qe_ready = two("qe_ready")
        lev_in = two("lev_in")
        lev_mm1 = two("lev_mm1")
        lev_p = two("lev_p")
        lev_mm2 = two("lev_mm2")
        ks_mm = two("ks_mm")
        r_ready = two("r_ready")
        vn_mm = two("vn_mm")
        vn_ready = two("vn_ready")
        ds_mm = two("ds_mm")
        s_ready = two("s_ready")
        o_mm = two("o_mm")
        o_out = two("o_out")
        o_sq = sem("o_sq")
        o_sum = sem("o_sum")
        o_rs = sem("o_rs")
        o_ready = sem("o_ready")
        done = sem("done")

        pad = carve(0, 2, 392)
        conv_acc = carve(784, 2, 388)
        mod_row = carve(1600, 4, 512)
        rs1 = carve(3700, TOK)
        sg = carve(0, 6, TT, 48)
        sq = carve(1024, 2, TOK)
        rs = carve(1792, 2, TOK)
        x_end = carve(0, 4, SSD_WIDTH)
        seg = [carve(1024 * i, 2, 4, P) for i in range(3)]
        c_dec = carve(3072, 2, 2, 4 * P).rearrange("p n d (h i) -> p n d h i", h=4)
        st_stage = carve(5120, 2, KD, SSD_STATE)
        h_st = carve(6144, 4, 512)
        cbm = carve(8192, 2, 2, P)
        y_tmp = w_ab[:, :, :].rearrange("p k n -> p (k n)").rearrange("p (b i) -> p b i", b=2)
        y_sq = carve(0, KD, TOK)
        y_rs = carve(8192, TOK)

        PAIRS = [(hq, kind) for hq in range(2) for kind in range(3)]
        CAP = 64
        NPAIR = N_EXPERTS // 2
        x1_t, h2_t = q_t, h1_t
        x1_tok = x_ssd[:, :, :].rearrange("p k t -> p (k t)").rearrange("p (t c) -> p t c", t=TT)
        h2_tok = carve(0, TT, D_MODEL)
        rs2 = carve(8192, TOK)
        amp2 = amp1
        kv_flat = kv[:, :, :].rearrange("p k t -> p (k t)")
        mix_flat = mix[:, :, :].rearrange("p k t -> p (k t)")
        slots = [ring[:, i, :, :] for i in range(RING)] + [m[:, 0:KD * 512].rearrange("p (k n) -> p k n", k=KD) for m in (mix_flat, kv_flat)]
        down = [m.rearrange("p k n -> p (k n)").rearrange("p (f n) -> p f n", f=FK) for m in slots]
        slot_in = w_in_sem + [sem("w_ready4"), sem("w_ready5")]
        n_loads = [sum(1 for i in range(len(loads)) if i % RING == s) for s in range(RING)] + [0, 0]
        router_sb = bc[:, :, :].rearrange("p k t -> p (k t)")[:, 0:KD * N_ROUTE].rearrange("p (k n) -> p k n", k=KD)
        rt = kv_flat[:, 4096:4096 + TT * 600].rearrange("p (t n) -> p t n", t=TT)
        take = [0]

        def field(n):
            take[0] += n
            return rt[:, :, take[0] - n:take[0]]

        lg, gmax, geq, gpick, g_exp, g_w = field(N_ROUTE), field(1), field(4), field(4), field(4), field(1)
        es, es_rest, e_top, e_eq, e_pick, pick1, pick2 = field(8), field(8), field(2), field(8), field(1), field(8), field(8)
        e_p2, e_w1, e_w2, wsum = field(1), field(1), field(1), field(8)
        spread, a1, a2, any_e, comb, rank, rank_only, over = [field(N_EXPERTS) for _ in range(8)]
        tg = field(3 * NPAIR)
        sel = mix[:, :, :].rearrange("p k t -> p (k t)").rearrange("p (t e c) -> p t e c", t=TT, e=N_EXPERTS)
        slot_info = sb("slot_info", [P, NPAIR, 3])
        slot_gate = sb("slot_gate", [P, NPAIR])
        slot_tok = sb("slot_tok", [P, NPAIR], mybir.dt.uint32)
        cur_tok = sb("cur_tok", [P, 1], mybir.dt.uint32)
        xg = carve(3072, D_MODEL)
        xg_t = carve(4096, KD, P)
        e_silu = carve(5120, F_EXP)
        e_act = carve(5632, F_EXP)
        e_act_t = carve(6144, FK, P)
        e_y = carve(6656, D_MODEL)
        sel_t = carve(7680, TOK)
        iota_w = carve(8192, TOK)
        y_acc = carve(0, TT, D_MODEL)
        x2_sq = carve(4096, D_MODEL)
        ss, most_f, counts = cums[:, 0, 0:8], cums[:, 0, 8:9], cums[:, 0, 16:48]
        gt2_row = q_t[:, :, :].rearrange("p k t -> p (k t)")[:, 0:2048].rearrange("p (c d) -> p c d", c=2)
        final_row = q_t[:, :, :].rearrange("p k t -> p (k t)")[:, 2048:3072]
        most = sb("most", [P, 2], mybir.dt.int32)
        o_scaled = carve(4096, D_MODEL)
        most_ready = sem("most_ready")
        rest_in = [sem(f"rest_{n}_in") for n in ("gate", "up", "down")]
        rest_up_mm = sem("rest_up_mm")
        rest_silu = sem("rest_silu")
        rest_act = sem("rest_act")
        rest_at_mm = sem("rest_at_mm")
        rest_at = sem("rest_at")
        rest_down_mm = sem("rest_down_mm")
        rest_scaled = sem("rest_scaled")
        rest_added = sem("rest_added")
        router_in = sem("router_in")
        h2_stored = sem("h2_stored")
        mix_done = sem("mix_done")
        x1_ready = sem("x1_ready")
        h2_ready = sem("h2_ready")
        lg_mm = sem("lg_mm")
        h2t_mm = sem("h2t_mm")
        h2t_ready = sem("h2t_ready")
        x1t_mm = sem("x1t_mm")
        x1t_ready = sem("x1t_ready")
        gd_ready = sem("gd_ready")
        gexp_ready = sem("gexp_ready")
        ed_ready = sem("ed_ready")
        eexp_ready = sem("eexp_ready")
        any_ready = sem("any_ready")
        rank_mm = sem("rank_mm")
        sel_ready = sem("sel_ready")
        info_mm = sem("info_mm")
        slots_ready = sem("slots_ready")
        rows_mm = sem("rows_mm")
        rows_ready = sem("rows_ready")
        cur_ready = sem("cur_ready")
        gather_go = sem("gather_go")
        xg_in = sem("xg_in")
        xgt_mm = sem("xgt_mm")
        xgt_ready = sem("xgt_ready")
        gate_mm = sem("gate_mm")
        up_mm = sem("up_mm")
        silu_done = sem("silu_done")
        hact_ready = sem("hact_ready")
        at_mm = sem("at_mm")
        at_ready = sem("at_ready")
        down_mm = sem("down_mm")
        y_half = sem("y_half")
        spread_mm = sem("spread_mm")
        acc_added = sem("acc_added")
        x2_ready = sem("x2_ready")
        x2_rs = sem("x2_rs")
        out_ready = sem("out_ready")
        out_stored = sem("out_stored")
        TILE = ((0, 0), (1, 2), (2, 1))
        LAST_DIR_ADDS = ((False, True), (False, False), (True, True))
        dn = [[carve(3072 * a + 512 * i, 4, P) for i in range(4)] for a in range(2)]
        dn_m, dn_e, dn_qk, dn_o = [[dn[a][i] for a in range(2)] for i in range(4)]
        dn_d = [carve(3072 * a + 2048, 2, 4, P) for a in range(2)]
        dn_s = carve(6144, 2, 2, 4 * P)
        mod_row2 = carve(6144, 4, 512)
        o_sq_t = carve(0, 2, TOK)
        o_rs_t = carve(1024, 2, TOK)

        SSD_UNITS = [(t, u) for t in range(TT) for u in range(4)]
        ENDS = [(0, 0), (0, 1), (1, 0), (2, 1)]

        block = ctx.enter_context(nc.Block())

        def consumed(i):
            if i < LOAD_PROJ:
                return ada_mm, 1
            if i < LOAD_ADA1:
                return (tok_mm, 1) if i == LOAD_PROJ + 2 else (block_mm, 1 + max(n for n, b in enumerate(blocks) if b[0] == i))
            if i < LOAD_OUT:
                return ada_mm, 2 + (i - LOAD_ADA1) // 4
            return out_mm, KD

        def more_than_cap(eng):
            eng.wait_ge(most_ready, 1)
            return eng.value_load(most[0:1, 0:1], min_val=0, max_val=TOK) > CAP

        @block.sync
        def _(sp):
            sp.dma_start(pc[:, :], params).then_inc(pc_in, 16)
            sp.dma_start(x0_t[:, :, 0:SEQ], x_t.rearrange("(k p) t -> p k t", p=P)).then_inc(x_in, 16)
            sp.dma_start(x0_t[:, :, SEQ:TOK], xs_t.rearrange("(k p) t -> p k t", p=P)).then_inc(x_in, 16)
            sp.dma_start(k_t[:, :, 0:DEC_SEQ], pos_t.rearrange("(k p) t -> p k t", p=P)).then_inc(x_in, 16)
            for i, (src, n) in enumerate(loads):
                if i >= RING:
                    sp.wait_ge(*consumed(i - RING))
                sp.dma_start(ring[:, i % RING, :, 0:n], src).then_inc(w_in_sem[i % RING], 16)
                if i == 3:
                    sp.dma_start(masks_sb[:, :, :], masks).then_inc(masks_in, 16)
                    sp.dma_start(w_ab[:, :, :], wi[:, :, AB0:AB0 + N_AB]).then_inc(wab_in, 16)

            for a in range(2):
                sp.wait_ge(o_mm[a], len(PAIRS))
            sp.dma_start(x0_t[:, :, 0:SEQ], x_t.rearrange("(k p) t -> p k t", p=P)).then_inc(x_in, 16)
            sp.dma_start(x0_t[:, :, SEQ:TOK], xs_t.rearrange("(k p) t -> p k t", p=P)).then_inc(x_in, 16)
            sp.dma_start(k_t[:, :, 0:DEC_SEQ], pos_t.rearrange("(k p) t -> p k t", p=P)).then_inc(x_in, 16)

            def expert_load(e, s):
                src = (w_gate, w_gate, w_up, w_up, w_down, w_down)[s]
                e = e + s % 2
                src = src[e, :, :] if isinstance(e, int) else src[bass.ds(e, 1), :, :].rearrange("a d f -> (a d) f")
                dst = slots[s] if s < 4 else down[s]
                sp.dma_start(dst, src.rearrange("(k p) n -> p k n", p=P)).then_inc(slot_in[s], 16)

            for s in range(6):
                if s < RING:
                    sp.wait_ge(out_mm, KD)
                elif s == 4:
                    for t in range(TT):
                        sp.wait_ge(h2t_ready, t + 1)
                        sp.dma_start(h2_dram[t * P:(t + 1) * P, :], h2_tok[:, t, :]).then_inc(h2_stored, 16)
                    sp.wait_ge(info_mm, 1)
                else:
                    sp.wait_ge(stat_ready, 3)
                    sp.wait_ge(x_ready, 2)
                expert_load(0, s)
            with sp.Fori(1, NPAIR) as i:
                for s in range(6):
                    sp.wait_ge((gate_mm, up_mm, down_mm)[s // 2], i)
                    expert_load(2 * i, s)
            with sp.If(more_than_cap(sp)):
                sp.wait_ge(down_mm, NPAIR)
                with sp.Fori(0, N_EXPERTS) as e:
                    sp.wait_ge(rest_added, e * TT + 1)
                    for n, src in enumerate((w_gate, w_up, w_down)):
                        dst = down[2] if n == 2 else slots[n]
                        sp.dma_start(dst, src[bass.ds(e, 1), :, :].rearrange("a (k p) n -> p (a k) n", p=P)).then_inc(rest_in[n], 16)
            for t in range(TT):
                sp.wait_ge(out_ready, t + 1)
                dst = outs[0] if t == 0 else outs[1][(t - 1) * P:t * P, :]
                sp.dma_start(dst, y_acc[:, t, :]).then_inc(out_stored, 16)
            sp.wait_ge(out_stored, 16 * TT)
        @block.gpsimd
        def _(pool):
            pool.wait_ge(qk_ready, 2 * KD)
            for d in range(2):
                pool.dma_start(h_st[:, 2 * d, :], h0_ssd[d]).then_inc(h0_in, 16)
            for d in range(2):
                pool.wait_ge(st_out, d + 1)
                pool.dma_start(outs[2 + d].rearrange("(b q) n -> q b n", q=P), st_stage[:, d, :, :]).then_inc(states_out, 16)
            for hq in range(2):
                pool.wait_ge(modp_ready, 2 + hq)
                if hq:
                    for d in range(2):
                        pool.wait_ge(s_ready[d], 6)
                for d in range(2):
                    pool.dma_start(dn_s[:, 1, d, :], s0_dn[d, :, 4 * hq:4 * hq + 4, :].rearrange("k h v -> k (h v)")).then_inc(s0_in, 16)
                for d in range(2):
                    pool.wait_ge(s_ready[d], 6 * hq + 2)
                    pool.dma_start(outs[4 + d][:, 4 * hq:4 * hq + 4, :].rearrange("k h v -> k (h v)"), dn_s[:, 0, d, :]).then_inc(states_out, 16)
                pool.wait_ge(states_out, 64 + 32 * hq)
            pool.wait_ge(m_ready, len(SSD_UNITS))
            pool.dma_start(router_sb, router).then_inc(router_in, 16)

            def gather():
                pool.indirect_dma_start(out=xg, out_offset=None, in_=h2_dram,
                                        in_offset=bass.IndirectOffsetOnAxis(ap=cur_tok[:, 0:1], axis=0)).then_inc(xg_in, 16)

            pool.wait_ge(slots_ready, 1)
            pool.wait_ge(h2_stored, 16 * TT)
            nc.gpsimd.tensor_copy(cur_tok[:, :], slot_tok[:, 0:1]).then_inc(cur_ready, 1)
            pool.wait_ge(cur_ready, 1)
            gather()
            with pool.Fori(1, NPAIR) as i:
                pool.wait_ge(xg_in, i * 16)
                nc.gpsimd.tensor_copy(cur_tok[:, :], slot_tok[:, bass.ds(i, 1)]).then_inc(cur_ready, 1)
                pool.wait_ge(cur_ready, i + 1)
                pool.wait_ge(xgt_mm, i)
                pool.sem_inc(gather_go, 1)
                gather()

        @block.tensor
        def _(pe):
            def ready(i):
                pe.wait_ge(w_in_sem[i % RING], 16 * (i // RING + 1))

            def ada_part(g, first, bank, rows):
                if g:
                    pe.wait_ge(mod_ready, g)
                for j in range(4):
                    ready(first + j)
                if g == 0:
                    pe.wait_ge(silu_ready, 1)
                for k in range(KD):
                    for j in range(4):
                        last = nc.tensor.matmul(ps[32 * j:32 * j + 2, bank, :], silu_c[:, 2 * k:2 * k + 2],
                                                ring[:, (first + j) % RING, k, :], start=(k == 0), stop=(k == KD - 1), tile_position=(0, 32 * j))
                last.then_inc(ada_mm, 1)
                pe.wait_ge(row_ready, g + 1)
                for j in range(4):
                    for b in range(4):
                        m = 16 * g + 4 * j + b
                        last = nc.tensor.matmul(ps[:, 7, 2 * m:2 * m + 2], rows[0:2, j, b * P:(b + 1) * P],
                                                masks_sb[0:2, MI["ident"], 0:2],
                                                start=True, stop=True)
                last.then_inc(modp_ready, 1)

            pe.wait_ge(masks_in, 16)
            pe.wait_ge(sq_ready, 1)
            for k in range(KD):
                last = nc.tensor.matmul(ps[:, 1, 0:TOK], mask("ones"), v_t[:, k, :], start=(k == 0), stop=(k == KD - 1))
            last.then_inc(stat_ready, 1)
            ada_part(0, 0, 0, mod_row)

            pe.wait_ge(h1_ready, 1)
            for n, (load, c, kind, i) in enumerate(blocks):
                if c == 0:
                    ready(load)
                if n >= 3:
                    pe.wait_ge(block_out, n - 2)
                for k in range(KD):
                    last = nc.tensor.matmul(ps[:, 2 + n % 3, 0:TOK], ring[:, load % RING, k, c:c + P], h1_t[:, k, :],
                                            start=(k == 0), stop=(k == KD - 1))
                last.then_inc(block_mm, 1)
                if n == 9:
                    pe.wait_ge(wab_in, 16)
                    for t in range(TT):
                        for w, n_w, o in ((ring[:, load % RING, :, 256:256 + N_DT], N_DT, 0), (w_ab[:, :, :], N_AB, N_DT)):
                            for k in range(KD):
                                last = nc.tensor.matmul(ps[:, 5, 64 * t + o:64 * t + o + n_w], h1_t[:, k, t * P:(t + 1) * P],
                                                        w[:, k, :], start=(k == 0), stop=(k == KD - 1))
                    last.then_inc(tok_mm, 1)

            pe.wait_ge(log_ready, 1)
            for t in range(TT):
                for m, a, b, o in (("upper", 0, 16, 0), ("lower", 16, 32, 16), ("upper64", 32, 40, 32), ("lower64", 40, 48, 40),
                                   ("ones", 0, 32, 48), ("ones64", 32, 48, 80), ("first64", 32, 48, 96), ("last64", 32, 48, 112)):
                    last = nc.tensor.matmul(ps[:, 6, t * P + o:t * P + o + b - a], mask(m), g_log[:, t, a:b], start=True, stop=True)
            last.then_inc(cum_mm, 1)

            for i in range(2 * KD):
                pe.wait_ge(qk_sq, i + 1)
                nc.tensor.matmul(ps[:, i % 2, 0:TOK], mask("ones"), sq[:, i % 2, :], start=True, stop=True).then_inc(qk_sum, 1)

            for t in range(TT):
                if t:
                    pe.wait_ge(xt_ready, t)
                for b in range(KD):
                    nc.tensor.transpose(ps[:, 2 + b // 4, (b % 4) * P:(b % 4 + 1) * P], x_ssd[:, b, t * P:(t + 1) * P], mask("ident"))
                nc.tensor.transpose(ps[:, 4, 0:P], bc[:, 0, t * P:(t + 1) * P], mask("ident")).then_inc(xt_mm, 1)

            pe.wait_ge(xe_ready, 4)
            for d in range(2):
                for b in range(KD):
                    g = b // 4
                    last = nc.tensor.matmul(ps[:, 5 + d, b * 64:(b + 1) * 64], x_end[:, d, b * P:(b + 1) * P],
                                            b_tok[:, 0, 64 * g:64 * g + 64], start=True, stop=True)
                last.then_inc(st_mm, 1)
            for d in range(2):
                for g in range(SSD_GROUPS):
                    last = nc.tensor.matmul(ps[64 * g:64 * g + 64, d, :], b_tok[:, 1 + d, 64 * g:64 * g + 64],
                                            x_end[:, 2 + d, g * 512:(g + 1) * 512], start=True, stop=True, tile_position=(0, 64 * g))
                last.then_inc(st_mm, 1)

            def seg_products(n):
                t, u = SSD_UNITS[n]
                if n == 0:
                    pe.wait_ge(h_ready, 1)
                    pe.wait_ge(st_out, 2)
                if n >= 2:
                    pe.wait_ge(dec_ready, n - 1)
                if u == 0:
                    if t:
                        pe.wait_ge(cb_ready, t)
                    for g in range(2):
                        last = nc.tensor.matmul(ps[:, 6 + g, 0:P], bc[64 * g:64 * g + 64, 0, t * P:(t + 1) * P],
                                                bc[64 * g:64 * g + 64, 1, t * P:(t + 1) * P], start=True, stop=True, tile_position=(64 * g, 0))
                    last.then_inc(cb_mm, 1)
                for d in range(2):
                    for h in range(4):
                        hh = 16 * d + 4 * u + h
                        last = nc.tensor.matmul(ps[:, 2 * (n % 2) + d, h * P:(h + 1) * P],
                                                g_log[:, t, hh:hh + 1].to_broadcast([P, P]), mask(("upper", "lower")[d]),
                                                start=True, stop=True)
                last.then_inc(seg_mm, 1)

            def y_products(n):
                t, u = SSD_UNITS[n]
                g = u // 2
                pe.wait_ge(m_ready, n + 1)
                if n >= 2:
                    pe.wait_ge(y_ready, n - 1)
                for b in range(2):
                    for d in range(2):
                        for e in range(2):
                            h = 2 * b + e
                            out = ps[64 * e:64 * e + 64, 4 + n % 2, b * P:(b + 1) * P]
                            head = 4 * u + h
                            last = nc.tensor.matmul(out, x_tok[:, t, 64 * head:64 * head + 64], seg[n % 3][:, d, h, :],
                                                    start=(d == 0), stop=(d == 1 and t == 0), tile_position=(0, 64 * e))
                        if t:
                            for e in range(2):
                                h = 2 * b + e
                                out = ps[64 * e:64 * e + 64, 4 + n % 2, b * P:(b + 1) * P]
                                st = 2 * d + (t - 1 if d == 0 else 2 - t)
                                lo = (4 * u + h) % 8
                                last = nc.tensor.matmul(out, h_st[64 * g:64 * g + 64, st, 64 * lo:64 * lo + 64],
                                                        c_dec[64 * g:64 * g + 64, n % 2, d, h, :], start=False, stop=(d == 1),
                                                        tile_position=(64 * g, 64 * e))
                last.then_inc(y_mm, 1)

            for n in range(len(SSD_UNITS) + 2):
                if n < len(SSD_UNITS):
                    seg_products(n)
                if n >= 2:
                    y_products(n - 2)
            pe.wait_ge(sq_ready, 2)
            for k in range(KD):
                last = nc.tensor.matmul(ps[:, 6, 0:TOK], mask("ones"), y_sq[:, k, :], start=(k == 0), stop=(k == KD - 1))
            last.then_inc(stat_ready, 1)

            ada_part(1, LOAD_ADA1, 5, mod_row2)

            for t in range(TT):
                if t:
                    pe.wait_ge(kvt_ready, t)
                for i, src in enumerate((k_t, v_t)):
                    for b in range(KD):
                        last = nc.tensor.transpose(ps[:, 2 * i + b // 4, (b % 4) * P:(b % 4 + 1) * P], src[:, b, t * P:(t + 1) * P], mask("ident"))
                last.then_inc(kvt_mm, 1)

            def dn_head(p):
                hq, kind = PAIRS[p]
                for a in range(2):
                    t = TILE[kind][a]
                    tok = slice(t * P, (t + 1) * P)
                    if p:
                        pe.wait_ge(s_ready[a], 2 * p)
                    for h in range(4):
                        c = 32 + 8 * a + 4 * hq + h
                        last = nc.tensor.matmul(ps[:, a, h * P:(h + 1) * P], g_log[:, t, c:c + 1].to_broadcast([P, P]),
                                                mask(("upper64", "lower64")[a]), start=True, stop=True)
                    last.then_inc(dseg_mm[a], 1)
                    for i, x in enumerate((k_t, q_t)):
                        for h in range(4):
                            last = nc.tensor.matmul(ps[:, 2 + 2 * a + i, h * P:(h + 1) * P], k_t[:, 4 * hq + h, tok], x[:, 4 * hq + h, tok],
                                                    start=True, stop=True)
                    last.then_inc(kq_mm[a], 1)

            def dn_level(p, lev):
                for a in range(2):
                    pe.wait_ge(lev_in[a], 7 * p + lev + 1)
                    for h in range(4):
                        rhs = mask("ident") if lev == 0 else dn_d[a][:, 0, h, :]
                        last = nc.tensor.matmul(ps[:, a, h * P:(h + 1) * P], dn_o[a][:, h, :], rhs, start=True, stop=True)
                    last.then_inc(lev_mm1[a], 1)
                if lev == 0:
                    return
                for a in range(2):
                    pe.wait_ge(lev_p[a], 5 * p + lev)
                    if lev < 5:
                        for h in range(4):
                            nc.tensor.matmul(ps[:, 2 + 2 * a, h * P:(h + 1) * P], dn_d[a][:, 1, h, :], dn_o[a][:, h, :], start=True, stop=True)
                    for h in range(4):
                        last = nc.tensor.matmul(ps[:, 3 + 2 * a, h * P:(h + 1) * P], dn_o[a][:, h, :], dn_d[a][:, 1, h, :], start=True, stop=True)
                    last.then_inc(lev_mm2[a], 1)

            def dn_chunk(p, step):
                hq, kind = PAIRS[p]
                for a in range(2):
                    t, c = TILE[kind][a], (step if a == 0 else 1 - step)
                    rows = slice(64 * c, 64 * c + 64)
                    if step:
                        pe.wait_ge(s_ready[a], 2 * p + 1)
                    elif kind == 0:
                        pe.wait_ge(s_zero, hq + 1)
                    elif kind == 1:
                        pe.wait_ge(s0_in, 32 * (hq + 1))
                    if step == 0:
                        pe.wait_ge(lev_in[a], 7 * p + 7)
                        if p:
                            pe.wait_ge(o_out[a], p)
                    st = dn_s[:, min(kind, 1), a, :]
                    for h in range(4):
                        last = nc.tensor.matmul(ps[rows, a, h * P:(h + 1) * P], k_t[:, 4 * hq + h, t * P + 64 * c:t * P + 64 * c + 64],
                                                st[:, h * P:(h + 1) * P], start=True, stop=True)
                    last.then_inc(ks_mm[a], 1)
                    for h in range(4):
                        nc.tensor.matmul(ps[:, 6 + a, h * P + 64 * c:h * P + 64 * c + 64], st[:, h * P:(h + 1) * P], dn_e[a][:, h, rows],
                                         start=(step == 0 and h == 0), stop=False, skip_group_check=True)
                for a in range(2):
                    c = step if a == 0 else 1 - step
                    rows = slice(64 * c, 64 * c + 64)
                    pe.wait_ge(r_ready[a], 2 * p + step + 1)
                    for h in range(4):
                        last = nc.tensor.matmul(ps[rows, 2 + 2 * a, h * P:(h + 1) * P], dn_d[a][rows, 1, h, rows], dn_m[a][rows, h, :],
                                                start=True, stop=True)
                    last.then_inc(vn_mm[a], 1)
                for a in range(2):
                    t, c = TILE[kind][a], (step if a == 0 else 1 - step)
                    rows = slice(64 * c, 64 * c + 64)
                    pe.wait_ge(vn_ready[a], 2 * p + step + 1)
                    for h in range(4):
                        last = nc.tensor.matmul(ps[:, 3 + 2 * a, h * P:(h + 1) * P], k_tok[rows, t, (4 * hq + h) * P:(4 * hq + h + 1) * P],
                                                dn_d[a][rows, 0, h, :], start=True, stop=True)
                    last.then_inc(ds_mm[a], 1)

            for p in range(len(PAIRS)):
                if p == 0:
                    pe.wait_ge(kvt_ready, TT)
                if p == 3:
                    for a in range(2):
                        pe.wait_ge(s_ready[a], 6)
                        pe.wait_ge(o_out[a], 3)
                    ada_part(2, LOAD_ADA2, 5, mod_row2)
                dn_head(p)
                for lev in range(6):
                    dn_level(p, lev)
                for step in range(2):
                    dn_chunk(p, step)
                for a in range(2):
                    for h in range(4):
                        last = nc.tensor.matmul(ps[:, 6 + a, h * P:(h + 1) * P], dn_o[a][:, h, :], dn_qk[a][:, h, :],
                                                start=False, stop=(h == 3), skip_group_check=True)
                    last.then_inc(o_mm[a], 1)
            for i in range(KD):
                pe.wait_ge(o_sq, i + 1)
                nc.tensor.matmul(ps[:, i % 2, 0:TOK], mask("ones"), o_sq_t[:, i % 2, :], start=True, stop=True).then_inc(o_sum, 1)

            pe.wait_ge(o_ready, KD)
            pe.wait_ge(ynorm_ready, 1)
            for b in range(KD):
                dh = b // 4
                if b % 4 == 0:
                    ready(LOAD_OUT + 2 * dh)
                    ready(LOAD_OUT + 2 * dh + 1)
                if b >= 2:
                    pe.wait_ge(x1_ready, b - 1)
                for k in range(2 * KD):
                    w = ring[:, (LOAD_OUT + 2 * dh + k // KD) % RING, k % KD, (b % 4) * P:(b % 4 + 1) * P]
                    last = nc.tensor.matmul(ps[:, b % 2, 0:TOK], w, mix[:, k, :], start=(k == 0), stop=(k == 2 * KD - 1))
                last.then_inc(out_mm, 1)
            pe.wait_ge(sq_ready, 3)
            for k in range(KD):
                last = nc.tensor.matmul(ps[:, 2, 0:TOK], mask("ones"), v_t[:, k, :], start=(k == 0), stop=(k == KD - 1))
            last.then_inc(stat_ready, 1)
            pe.wait_ge(h2_ready, 1)
            pe.wait_ge(router_in, 16)
            for t in range(TT):
                for k in range(KD):
                    last = nc.tensor.matmul(ps[:, 7, t * N_ROUTE:(t + 1) * N_ROUTE], h2_t[:, k, t * P:(t + 1) * P], router_sb[:, k, :],
                                            start=(k == 0), stop=(k == KD - 1))
            last.then_inc(lg_mm, 1)
            for t in range(TT):
                if t:
                    pe.wait_ge(h2t_ready, t)
                for b in range(KD):
                    last = nc.tensor.transpose(ps[:, 3 + b // 4, (b % 4) * P:(b % 4 + 1) * P], h2_t[:, b, t * P:(t + 1) * P], mask("ident"))
                last.then_inc(h2t_mm, 1)
            pe.wait_ge(any_ready, 1)
            for t in range(TT + 1):
                for u in range(min(t + 1, TT)):
                    last = nc.tensor.matmul(ps[:, 7, t * N_EXPERTS:(t + 1) * N_EXPERTS], mask("strict_up" if u == t else "ones"), any_e[:, u, :],
                                            start=(u == 0), stop=(u == min(t, TT - 1)))
            last.then_inc(rank_mm, 1)
            pe.wait_ge(sel_ready, 1)
            for j in range(NPAIR):
                for t in range(TT):
                    last = nc.tensor.matmul(ps[:, 0, 3 * j:3 * j + 3], sel[:, t, 2 * j:2 * j + 2, :].rearrange("p e c -> p (e c)"),
                                            tg[:, t, 3 * j:3 * j + 3], start=(t == 0), stop=(t == TT - 1))
            last.then_inc(info_mm, 1)

            for t in range(TT):
                if t:
                    pe.wait_ge(x1t_ready, t)
                for b in range(KD):
                    last = nc.tensor.transpose(ps[:, 5 + b // 4, (b % 4) * P:(b % 4 + 1) * P], x1_t[:, b, t * P:(t + 1) * P], mask("ident"))
                last.then_inc(x1t_mm, 1)
            pe.wait_ge(slots_ready, 1)
            pe.wait_ge(x1t_ready, TT)
            for i in range(3):
                for k in range(KD):
                    src = mod[:, 5 * KD + k, i:i + 1] if i < 2 else col("final", k)
                    last = nc.tensor.matmul(ps[:, 2 * i + k // 4, (k % 4) * P:(k % 4 + 1) * P], src.to_broadcast([P, P]), mask("ident"),
                                            start=True, stop=True)
            last.then_inc(rows_mm, 1)
            def turn_rows(i):
                pe.wait_ge(xg_in, i * 16 + 16)
                for b in range(KD):
                    last = nc.tensor.transpose(ps[:, b // 4, (b % 4) * P:(b % 4 + 1) * P], xg[:, b * P:(b + 1) * P], mask("ident"))
                last.then_inc(xgt_mm, 1)

            def expert_pair(i, more):
                pe.wait_ge(xgt_ready, i * 2 + 2)
                for n, done_sem in ((0, gate_mm), (1, up_mm)):
                    for e in range(2):
                        pe.wait_ge(slot_in[2 * n + e], i * 16 + 16 * (n_loads[2 * n + e] + 1))
                    for k in range(KD):
                        for e in range(2):
                            last = nc.tensor.matmul(ps[64 * e:64 * e + 64, 2 + n, :], xg_t[:, k, 64 * e:64 * e + 64], slots[2 * n + e][:, k, :],
                                                    start=(k == 0), stop=(k == KD - 1), tile_position=(0, 64 * e))
                    last.then_inc(done_sem, 1)
                if more:
                    turn_rows(i + 1)
                pe.wait_ge(hact_ready, i + 1)
                for f in range(FK):
                    last = nc.tensor.transpose(ps[:, 4, f * P:(f + 1) * P], e_act[:, f * P:(f + 1) * P], mask("ident"))
                last.then_inc(at_mm, 1)
                pe.wait_ge(at_ready, i + 1)
                for e in range(2):
                    pe.wait_ge(slot_in[4 + e], i * 16 + 16)
                for n in range(2):
                    for f in range(FK):
                        for e in range(2):
                            last = nc.tensor.matmul(ps[64 * e:64 * e + 64, 5 + n, :], e_act_t[:, f, 64 * e:64 * e + 64],
                                                    down[4 + e][:, f, n * 512:(n + 1) * 512], start=(f == 0), stop=(f == FK - 1),
                                                    tile_position=(0, 64 * e))
                last.then_inc(down_mm, 1)
                pe.wait_ge(y_half, i * 2 + 2)
                for m in range(2 * TT):
                    t, n = m // 2, m % 2
                    pe.wait_ge(acc_added, i * 6 + m + 1)
                    nc.tensor.matmul(ps[:, (7, 4)[n], :], sel_t[:, t * P:(t + 1) * P], e_y[:, n * 512:(n + 1) * 512],
                                     start=True, stop=True).then_inc(spread_mm, 1)

            pe.wait_ge(rows_ready, 1)
            turn_rows(0)
            with pe.Fori(0, NPAIR - 1) as i:
                expert_pair(i, True)
            expert_pair(NPAIR - 1, False)

            with pe.If(more_than_cap(pe)):
                with pe.Fori(0, N_EXPERTS) as e:
                    for t in range(TT):
                        if t == 0:
                            pe.wait_ge(rest_in[0], e * 16 + 16)
                            pe.wait_ge(rest_in[1], e * 16 + 16)
                        for n in range(2):
                            for k in range(KD):
                                last = nc.tensor.matmul(ps[:, n, :], h2_t[:, k, t * P:(t + 1) * P], slots[n][:, k, :], start=(k == 0), stop=(k == KD - 1))
                        last.then_inc(rest_up_mm, 1)
                        pe.wait_ge(rest_act, e * TT + t + 1)
                        for f in range(FK):
                            last = nc.tensor.transpose(ps[:, 2, f * P:(f + 1) * P], e_act[:, f * P:(f + 1) * P], mask("ident"))
                        last.then_inc(rest_at_mm, 1)
                        if t == 0:
                            pe.wait_ge(rest_in[2], e * 16 + 16)
                        pe.wait_ge(rest_at, e * TT + t + 1)
                        pe.wait_ge(rest_added, e * TT + t + 1)
                        for n in range(2):
                            for f in range(FK):
                                last = nc.tensor.matmul(ps[:, 3 + n, :], e_act_t[:, f, :], down[2][:, f, n * 512:(n + 1) * 512],
                                                        start=(f == 0), stop=(f == FK - 1))
                        last.then_inc(rest_down_mm, 1)

        @block.scalar
        def _(act):
            steps = [0]

            def link(ins):
                steps[0] += 1
                ins.then_inc(act_step, 1)
                act.wait_ge(act_step, steps[0])

            def rsqrt(out, in_, scale, tmp):
                link(nc.scalar.activation(tmp, in_, ACT.Ln, bias=eps_col, scale=scale))
                return nc.scalar.activation(out, tmp, ACT.Exp, scale=-0.5)

            def ada_rows(g, bank, rows):
                act.wait_ge(ada_mm, g + 1)
                for j in range(4):
                    last = nc.scalar.copy(rows[0:2, j, :], ps[32 * j:32 * j + 2, bank, :])
                last.then_inc(row_ready, 1)

            act.wait_ge(pc_in, 16)
            nc.scalar.activation(silu_c[:, :], cols("c"), ACT.Silu).then_inc(silu_ready, 1)
            act.wait_ge(x_ready, 1)
            eps_col = masks_sb[:, MI["eps"], 0:1]
            nc.scalar.activation(v_t[:, :, :], x0_t[:, :, :], ACT.Square).then_inc(sq_ready, 1)
            act.wait_ge(stat_ready, 1)
            rsqrt(rs1, ps[:, 1, 0:TOK], 1.0 / D_MODEL, rs1).then_inc(rs_ready, 1)
            ada_rows(0, 0, mod_row)

            def conv_silu(i):
                act.wait_ge(conv_done, i + 1)
                dest = conv_dest(i)
                nc.scalar.activation(dest[:, 0:SEQ], conv_acc[:, i % 2, 0:SEQ], ACT.Silu)
                nc.scalar.activation(dest[:, SEQ:TOK], conv_acc[:, i % 2, SEQ + 4:TOK + 4], ACT.Silu).then_inc(conv_out, 1)

            for n, (load, c, kind, i) in enumerate(blocks):
                act.wait_ge(block_mm, n + 1)
                bank = 2 + n % 3
                if kind == "conv":
                    if i >= 2:
                        act.wait_ge(conv_done, i - 1)
                    nc.scalar.copy(pad[:, i % 2, 2:2 + SEQ], ps[:, bank, 0:SEQ])
                    nc.scalar.copy(pad[:, i % 2, SEQ + 6:TOK + 6], ps[:, bank, SEQ:TOK]).then_inc(block_out, 1)
                    if i:
                        conv_silu(i - 1)
                else:
                    if i == 0:
                        conv_silu(CONV_BLOCKS - 1)
                    nc.scalar.activation(mix[:, i, :], ps[:, bank, 0:TOK], ACT.Silu).then_inc(block_out, 1)

            act.wait_ge(na_ready, 1)
            nc.scalar.preload_act_table_set("natural_log_exp_and_others")
            nc.scalar.activation(sg[:, 2, :, :], sg[:, 1, :, :], ACT.Exp)
            nc.scalar.activation(g_beta, ps[:, 5, 0:192].rearrange("p (t c) -> p t c", t=TT)[:, :, 48:64], ACT.Exp, scale=-1.0)
            link(nc.scalar.activation(sg[:, 4, 0, :], cols("a_log"), ACT.Exp))
            nc.scalar.activation(sg[:, 3, :, :], sg[:, 2, :, :], ACT.Ln, bias=1.0).then_inc(ln_ready, 1)
            act.wait_ge(cum_ready, 1)
            nc.scalar.activation(sg[:, 0, :, :], sg[:, 1, :, :], ACT.Exp)
            nc.scalar.activation(g_nec, cums[:, :, 32:48], ACT.Exp)
            nc.scalar.activation(g_tot, cums[:, :, 48:128], ACT.Exp).then_inc(exps_ready, 1)

            for i in range(2 * KD):
                src = (q_t, k_t)[i // KD][:, i % KD, :]
                if i >= 2:
                    act.wait_ge(qk_sum, i - 1)
                nc.scalar.activation(sq[:, i % 2, :], src, ACT.Square).then_inc(qk_sq, 1)
                if i:
                    def norm(i):
                        act.wait_ge(qk_sum, i + 1)
                        if i >= 2:
                            act.wait_ge(qk_ready, i - 1)
                        rsqrt(rs[:, i % 2, :], ps[:, i % 2, 0:TOK], 1.0, rs[:, i % 2, :]).then_inc(qk_rs, 1)
                    norm(i - 1)
            norm(2 * KD - 1)

            for t in range(TT):
                act.wait_ge(xt_mm, t + 1)
                nc.scalar.copy(x_tok[:, t, 0:512], ps[:, 2, :])
                nc.scalar.copy(x_tok[:, t, 512:1024], ps[:, 3, :])
                nc.scalar.copy(b_tok[:, t, :], ps[:, 4, 0:P]).then_inc(xt_ready, 1)
            for d in range(2):
                act.wait_ge(st_mm, d + 1)
                nc.scalar.copy(st_stage[:, d, :, :], ps[:, 5 + d, :].rearrange("p (b n) -> p b n", b=KD)).then_inc(st_out, 1)

            for n, (t, u) in enumerate(SSD_UNITS):
                g = u // 2
                act.wait_ge(seg_ready, n + 1)
                if t:
                    if n >= 2:
                        act.wait_ge(y_mm, n - 1)
                    for d in range(2):
                        nc.scalar.activation(c_dec[64 * g:64 * g + 64, n % 2, d, :, :],
                                             ps[64 * g:64 * g + 64, 2 * (n % 2) + d, :].rearrange("p (h i) -> p h i", h=4), ACT.Exp)
                nc.scalar.activation(seg[n % 3], seg[n % 3], ACT.Exp).then_inc(dec_ready, 1)
            act.wait_ge(y_ready, len(SSD_UNITS))
            nc.scalar.activation(y_sq, mix[:, 0:KD, :], ACT.Square).then_inc(sq_ready, 1)
            act.wait_ge(stat_ready, 2)
            rsqrt(y_rs, ps[:, 6, 0:TOK], 1.0 / SSD_WIDTH, y_rs).then_inc(rs_ready, 1)

            ada_rows(1, 5, mod_row2)
            for t in range(TT):
                act.wait_ge(kvt_mm, t + 1)
                for i, dst in enumerate((k_tok, v_tok)):
                    for b in range(2):
                        last = nc.scalar.copy(dst[:, t, b * 512:(b + 1) * 512], ps[:, 2 * i + b, :])
                last.then_inc(kvt_ready, 1)

            for p, (hq, kind) in enumerate(PAIRS):
                if p == 3:
                    act.wait_ge(states_out, 64)
                    ada_rows(2, 5, mod_row2)
                for a in range(2):
                    act.wait_ge(dseg_ready[a], p + 1)
                    if p:
                        act.wait_ge(o_mm[a], p)
                    nc.scalar.activation(dn_m[a], dn_m[a], ACT.Exp).then_inc(dec_exp[a], 1)
                    nc.scalar.activation(dn_e[a], ps[:, a, :].rearrange("p (h i) -> p h i", h=4), ACT.Exp).then_inc(e_ready[a], 1)
                for lev in range(1, 6):
                    for a in range(2):
                        act.wait_ge(lev_mm1[a], 6 * p + lev + 1)
                        nc.scalar.copy(dn_o[a], ps[:, a, :].rearrange("p (h i) -> p h i", h=4)).then_inc(lev_p[a], 1)
                for a in range(2):
                    if not LAST_DIR_ADDS[kind][a]:
                        t = TILE[kind][a]
                        act.wait_ge(o_mm[a], p + 1)
                        nc.scalar.copy(o_t[:, 4 * hq:4 * hq + 4, t * P:(t + 1) * P], ps[:, 6 + a, :].rearrange("p (h i) -> p h i", h=4)).then_inc(o_out[a], 1)
            for i in range(KD):
                if i == 0:
                    for a in range(2):
                        act.wait_ge(o_out[a], len(PAIRS))
                if i >= 2:
                    act.wait_ge(o_sum, i - 1)
                nc.scalar.activation(o_sq_t[:, i % 2, :], o_t[:, i, :], ACT.Square).then_inc(o_sq, 1)
                if i:
                    def o_norm(i):
                        act.wait_ge(o_sum, i + 1)
                        if i >= 2:
                            act.wait_ge(o_ready, i - 1)
                        rsqrt(o_rs_t[:, i % 2, :], ps[:, i % 2, 0:TOK], 1.0 / DN_HEAD_DIM, o_rs_t[:, i % 2, :]).then_inc(o_rs, 1)
                    o_norm(i - 1)
            o_norm(KD - 1)

            act.wait_ge(x1_ready, KD)
            act.wait_ge(o_ready, KD)
            nc.scalar.activation(v_t[:, :, :], x1_t[:, :, :], ACT.Square).then_inc(sq_ready, 1)
            act.wait_ge(stat_ready, 3)
            rsqrt(rs2, ps[:, 2, 0:TOK], 1.0 / D_MODEL, rs2).then_inc(rs_ready, 1)
            for t in range(TT):
                act.wait_ge(h2t_mm, t + 1)
                nc.scalar.copy(h2_tok[:, t, 0:512], ps[:, 3, :])
                nc.scalar.copy(h2_tok[:, t, 512:1024], ps[:, 4, :]).then_inc(h2t_ready, 1)
            act.wait_ge(gd_ready, 1)
            nc.scalar.activation(g_exp, g_exp, ACT.Exp).then_inc(gexp_ready, 1)
            act.wait_ge(ed_ready, 1)
            nc.scalar.activation(e_p2, e_p2, ACT.Exp).then_inc(eexp_ready, 1)
            for t in range(TT):
                act.wait_ge(x1t_mm, t + 1)
                nc.scalar.copy(x1_tok[:, t, 0:512], ps[:, 5, :])
                nc.scalar.copy(x1_tok[:, t, 512:1024], ps[:, 6, :]).then_inc(x1t_ready, 1)
            act.wait_ge(rows_mm, 1)
            for i in range(3):
                for n in range(2):
                    dst = gt2_row[:, i, n * 512:(n + 1) * 512] if i < 2 else final_row[:, n * 512:(n + 1) * 512]
                    last = nc.scalar.copy(dst, ps[:, 2 * i + n, :])
            last.then_inc(rows_ready, 1)
            def turned_half(i):
                act.wait_ge(xgt_mm, i + 1)
                nc.scalar.copy(xg_t[:, 4:8, :], ps[:, 1, :].rearrange("p (k i) -> p k i", k=4)).then_inc(xgt_ready, 1)

            def expert_pair(i, more):
                act.wait_ge(gate_mm, i + 1)
                nc.scalar.activation(e_silu, ps[:, 2, :], ACT.Silu).then_inc(silu_done, 1)
                if more:
                    turned_half(i + 1)
                act.wait_ge(at_mm, i + 1)
                nc.scalar.copy(e_act_t, ps[:, 4, :].rearrange("p (f i) -> p f i", f=FK)).then_inc(at_ready, 1)
                act.wait_ge(down_mm, i + 1)
                nc.scalar.copy(e_y[:, 512:1024], ps[:, 6, :]).then_inc(y_half, 1)

            turned_half(0)
            with act.Fori(0, NPAIR - 1) as i:
                expert_pair(i, True)
            expert_pair(NPAIR - 1, False)
            with act.If(more_than_cap(act)):
                with act.Fori(0, N_EXPERTS) as e:
                    for t in range(TT):
                        act.wait_ge(rest_up_mm, e * TT + t + 1)
                        nc.scalar.activation(e_silu, ps[:, 0, :], ACT.Silu).then_inc(rest_silu, 1)
                        act.wait_ge(rest_at_mm, e * TT + t + 1)
                        nc.scalar.copy(e_act_t, ps[:, 2, :].rearrange("p (f i) -> p f i", f=FK)).then_inc(rest_at, 1)
            for t in range(TT):
                act.wait_ge(x2_ready, t + 1)
                link(nc.scalar.activation(x2_sq, y_acc[:, t, :], ACT.Square, accum_out=ss[:, t:t + 1]))
                rsqrt(ss[:, 4 + t:5 + t], ss[:, t:t + 1], 1.0 / D_MODEL, ss[:, t:t + 1]).then_inc(x2_rs, 1)

        @block.vector
        def _(dve):
            steps = [0]

            def link(ins):
                steps[0] += 1
                ins.then_inc(dve_step, 1)
                dve.wait_ge(dve_step, steps[0])

            V = nc.vector
            link(V.memset(pad, 0.0))
            dve.wait_ge(x_in, 48)
            V.tensor_tensor(x0_t[:, :, SEQ:TOK], x0_t[:, :, SEQ:TOK], k_t[:, :, 0:DEC_SEQ], ALU.add).then_inc(x_ready, 1)
            dve.wait_ge(pc_in, 16)
            dve.wait_ge(rs_ready, 1)
            link(V.tensor_tensor(h1_t, x0_t[:, :, :], rs1.unsqueeze(1).to_broadcast([P, KD, TOK]), ALU.mult))

            def mod_columns(g):
                dve.wait_ge(modp_ready, g + 1)
                b_ada = cols("b_ada")[:, 16 * g:16 * g + 16].unsqueeze(2).to_broadcast([P, 16, 2])
                return V.tensor_tensor(mod[:, 16 * g:16 * g + 16, :], ps[:, 7, 32 * g:32 * g + 32].rearrange("p (m c) -> p m c", c=2), b_ada, ALU.add)

            mod_columns(0).then_inc(mod_ready, 1)
            dve.wait_ge(mod_ready, 1)
            link(V.scalar_tensor_tensor(amp1[:, :, :], mod[:, KD:2 * KD, :], 1.0, cols("norm1").unsqueeze(2).to_broadcast([P, KD, 2]), ALU.add, ALU.mult))
            for c, (a, b) in enumerate(SEGS):
                for k in range(KD):
                    last = V.tensor_scalar(h1_t[:, k, a:b], h1_t[:, k, a:b], amp1[:, k, c:c + 1], mod[:, k, c:c + 1], ALU.mult, ALU.add)
            last.then_inc(h1_ready, 1)

            W5 = TOK + 4
            for i in range(CONV_BLOCKS):
                dve.wait_ge(block_out, i + 1)
                if i >= 2:
                    dve.wait_ge(conv_out, i - 1)
                c_acc, row = conv_acc[:, i % 2, :], pad[:, i % 2, :]
                link(V.tensor_scalar(c_acc, row[:, 0:W5], col("conv_w", CONV_W * i), col("conv_b", i), ALU.mult, ALU.add))
                for j in range(1, CONV_W):
                    ins = V.scalar_tensor_tensor(c_acc, row[:, j:j + W5], col("conv_w", CONV_W * i + j), c_acc, ALU.mult, ALU.add)
                    if j < CONV_W - 1:
                        link(ins)
                ins.then_inc(conv_done, 1)

            dve.wait_ge(tok_mm, 1)
            dve.wait_ge(conv_out, CONV_BLOCKS)
            gp = ps[:, 5, 0:192].rearrange("p (t c) -> p t c", t=TT)
            link(V.tensor_tensor(sg[:, 0, :, :], gp[:, :, 0:48], cols("gate_bias").unsqueeze(1).to_broadcast([P, TT, 48]), ALU.add))
            V.scalar_tensor_tensor(sg[:, 1, :, :], sg[:, 0, :, :], -1.0, sg[:, 0, :, :], ALU.mult, ALU.min).then_inc(na_ready, 1)
            dve.wait_ge(ln_ready, 1)
            link(V.scalar_tensor_tensor(sg[:, 5, :, :], sg[:, 0, :, :], 0.0, sg[:, 3, :, :], ALU.max, ALU.add))
            V.tensor_copy(g_dt, sg[:, 5, :, 0:32])
            link(V.tensor_scalar(g_beta, g_beta, 1.0, None, ALU.add))
            link(V.reciprocal(g_beta, g_beta))
            V.scalar_tensor_tensor(g_log, sg[:, 5, :, :], -1.0, sg[:, 4, 0:1, :].to_broadcast([P, TT, 48]), ALU.mult, ALU.mult).then_inc(log_ready, 1)
            dve.wait_ge(cum_mm, 1)
            link(V.tensor_copy(cums[:, :, :], ps[:, 6, 0:TT * P].rearrange("p (t c) -> p t c", t=TT)))
            V.tensor_tensor(sg[:, 1, :, :], cums[:, :, 48:96], cums[:, :, 0:48], ALU.subtract).then_inc(cum_ready, 1)
            dve.wait_ge(exps_ready, 1)
            V.tensor_tensor(g_dte, g_dt, sg[:, 0, :, 0:32], ALU.mult)
            V.tensor_tensor(g_be, g_beta, sg[:, 0, :, 32:48], ALU.mult)
            link(V.tensor_scalar(g_nec, g_nec, -1.0, None, ALU.mult))

            for i in range(2 * KD):
                dve.wait_ge(qk_rs, i + 1)
                x = (q_t, k_t)[i // KD][:, i % KD, :]
                V.scalar_tensor_tensor(x, x, (DN_HEAD_DIM ** -0.5, 1.0)[i // KD], rs[:, i % 2, :], ALU.mult, ALU.mult).then_inc(qk_ready, 1)

            for n, (t, d) in enumerate(ENDS):
                dve.wait_ge(xt_ready, t + 1)
                if n == 0:
                    dve.wait_ge(qk_ready, 2 * KD)
                V.tensor_tensor(x_end[:, n, :].rearrange("p (h c) -> p h c", c=64), x_tok[:, t, :].rearrange("p (h c) -> p h c", c=64),
                                g_dte[:, t, 16 * d:16 * d + 16].unsqueeze(2).to_broadcast([P, 16, 64]), ALU.mult).then_inc(xe_ready, 1)
            dve.wait_ge(h0_in, 32)
            for d in range(2):
                for g in range(2):
                    sl = slice(64 * g, 64 * g + 64)
                    last = V.tensor_tensor(h_st[sl, 2 * d + 1, :].rearrange("p (h c) -> p h c", c=64), h_st[sl, 2 * d, :].rearrange("p (h c) -> p h c", c=64),
                                           g_tot[sl, 1 + d, 16 * d + 8 * g:16 * d + 8 * g + 8].unsqueeze(2).to_broadcast([64, 8, 64]), ALU.mult)
                link(last)
                dve.wait_ge(st_mm, 3 + d)
                last = V.tensor_tensor(h_st[:, 2 * d + 1, :], h_st[:, 2 * d + 1, :], ps[:, d, :], ALU.add)
            last.then_inc(h_ready, 1)

            def seg_part(n):
                t, u = SSD_UNITS[n]
                dve.wait_ge(seg_mm, n + 1)
                if n >= 3:
                    dve.wait_ge(y_mm, n - 2)
                for d in range(2):
                    for h in range(4):
                        hh = 16 * d + 4 * u + h
                        last = V.tensor_scalar(seg[n % 3][:, d, h, :], ps[:, 2 * (n % 2) + d, h * P:(h + 1) * P], cums[:, t, hh:hh + 1], 0.0,
                                               ALU.subtract, ALU.min)
                last.then_inc(seg_ready, 1)

            def m_part(n):
                t, u = SSD_UNITS[n]
                g = u // 2
                if u == 0:
                    dve.wait_ge(cb_mm, t + 1)
                    for d in range(2):
                        last = V.tensor_tensor(cbm[:, d, :, :], ps[:, 6:8, 0:P],
                                               mask(("upper", "lower")[d]).unsqueeze(1).to_broadcast([P, 2, P]), ALU.mult)
                    last.then_inc(cb_ready, 1)
                    dve.wait_ge(cb_ready, t + 1)
                dve.wait_ge(dec_ready, n + 1)
                for d in range(2):
                    for h in range(4):
                        hh = 16 * d + 4 * u + h
                        last = V.scalar_tensor_tensor(seg[n % 3][:, d, h, :], seg[n % 3][:, d, h, :], g_dt[:, t, hh:hh + 1], cbm[:, d, g, :],
                                                      ALU.mult, ALU.mult)
                    if t:
                        sl = slice(64 * g, 64 * g + 64)
                        last = V.tensor_tensor(c_dec[sl, n % 2, d, :, :], c_dec[sl, n % 2, d, :, :],
                                               bc[sl, 1, t * P:(t + 1) * P].unsqueeze(1).to_broadcast([64, 4, P]), ALU.mult)
                last.then_inc(m_ready, 1)

            def y_out(n):
                t, u = SSD_UNITS[n]
                dve.wait_ge(y_mm, n + 1)
                if n:
                    dve.wait_ge(y_ready, n)
                for b in range(2):
                    last = V.scalar_tensor_tensor(y_tmp[:, b, :], x_ssd[:, 2 * u + b, t * P:(t + 1) * P], col("ssd_d", 2 * u + b),
                                                  ps[:, 4 + n % 2, b * P:(b + 1) * P], ALU.mult, ALU.add)
                link(last)
                V.tensor_tensor(mix[:, 2 * u:2 * u + 2, t * P:(t + 1) * P], mix[:, 2 * u:2 * u + 2, t * P:(t + 1) * P], y_tmp,
                                ALU.mult).then_inc(y_ready, 1)

            seg_part(0)
            for n in range(len(SSD_UNITS)):
                if n + 1 < len(SSD_UNITS):
                    seg_part(n + 1)
                m_part(n)
                if n:
                    y_out(n - 1)
            y_out(len(SSD_UNITS) - 1)
            dve.wait_ge(rs_ready, 2)
            for k in range(KD):
                last = V.scalar_tensor_tensor(mix[:, k, :], mix[:, k, :], col("ssd_norm", k), y_rs, ALU.mult, ALU.mult)
            last.then_inc(ynorm_ready, 1)

            mod_columns(1).then_inc(mod_ready, 1)

            def zero_states():
                V.memset(dn_s[:, 0, :, :], 0.0).then_inc(s_zero, 1)

            dve.wait_ge(mod_ready, 2)
            dve.wait_ge(states_out, 32)
            zero_states()
            for p, (hq, kind) in enumerate(PAIRS):
                if p == 3:
                    mod_columns(2).then_inc(mod_ready, 1)
                    dve.wait_ge(states_out, 64)
                    zero_states()
                for a in range(2):
                    t = TILE[kind][a]
                    dve.wait_ge(dseg_mm[a], p + 1)
                    if p:
                        dve.wait_ge(o_mm[a], p)
                    for h in range(4):
                        c = 32 + 8 * a + 4 * hq + h
                        last = V.tensor_scalar(dn_m[a][:, h, :], ps[:, a, h * P:(h + 1) * P], cums[:, t, c:c + 1], 0.0, ALU.subtract, ALU.min)
                    last.then_inc(dseg_ready[a], 1)
                for a in range(2):
                    t = TILE[kind][a]
                    dve.wait_ge(dec_exp[a], p + 1)
                    link(V.tensor_tensor(dn_m[a], dn_m[a], mask(("upper64", "lower64")[a]).unsqueeze(1).to_broadcast([P, 4, P]), ALU.mult))
                    dve.wait_ge(kq_mm[a], p + 1)
                    link(V.tensor_tensor(dn_qk[a], dn_m[a], ps[:, 3 + 2 * a, :].rearrange("p (h i) -> p h i", h=4), ALU.mult))
                    for h in range(4):
                        b = 8 * a + 4 * hq + h
                        last = V.scalar_tensor_tensor(dn_m[a][:, h, :], ps[:, 2 + 2 * a, h * P:(h + 1) * P], g_beta[:, t, b:b + 1], dn_m[a][:, h, :],
                                                      ALU.mult, ALU.mult)
                    link(last)
                    dve.wait_ge(e_ready[a], p + 1)
                    V.tensor_tensor(dn_e[a], dn_e[a], q_t[:, 4 * hq:4 * hq + 4, t * P:(t + 1) * P], ALU.mult)
                    V.tensor_tensor(dn_o[a], dn_m[a], mask(f"lev{a}_1").unsqueeze(1).to_broadcast([P, 4, P]), ALU.mult).then_inc(lev_in[a], 1)
                ident4 = mask("ident").unsqueeze(1).to_broadcast([P, 4, P])
                for lev in range(6):
                    for a in range(2):
                        if lev == 0:
                            dve.wait_ge(lev_mm1[a], 6 * p + 1)
                            V.tensor_tensor(dn_d[a][:, 1, :, :], ident4, dn_o[a], ALU.subtract)
                            link(V.tensor_tensor(dn_d[a][:, 0, :, :], ident4, ps[:, a, :].rearrange("p (h i) -> p h i", h=4), ALU.subtract))
                        elif lev < 5:
                            dve.wait_ge(lev_mm2[a], 5 * p + lev)
                            V.tensor_tensor(dn_d[a].rearrange("p x h i -> p (x h i)"), dn_d[a].rearrange("p x h i -> p (x h i)"),
                                            ps[:, 2 + 2 * a:4 + 2 * a, :].rearrange("p x i -> p (x i)"), ALU.subtract)
                        else:
                            dve.wait_ge(lev_mm2[a], 5 * p + lev)
                            V.tensor_tensor(dn_d[a][:, 1, :, :], dn_d[a][:, 1, :, :], ps[:, 3 + 2 * a, :].rearrange("p (h i) -> p h i", h=4),
                                            ALU.subtract).then_inc(lev_in[a], 1)
                        if lev < 5:
                            V.tensor_tensor(dn_o[a], dn_m[a], mask(f"lev{a}_{LEVELS[lev + 1]}").unsqueeze(1).to_broadcast([P, 4, P]),
                                            ALU.mult).then_inc(lev_in[a], 1)
                for step in range(2):
                    for a in range(2):
                        t, c = TILE[kind][a], (step if a == 0 else 1 - step)
                        rows = slice(64 * c, 64 * c + 64)
                        dve.wait_ge(ks_mm[a], 2 * p + step + 1)
                        for h in range(4):
                            b = 8 * a + 4 * hq + h
                            last = V.scalar_tensor_tensor(dn_m[a][rows, h, :], ps[rows, a, h * P:(h + 1) * P], g_nec[rows, t, b:b + 1],
                                                          v_tok[rows, t, (4 * hq + h) * P:(4 * hq + h + 1) * P], ALU.mult, ALU.add)
                        last.then_inc(r_ready[a], 1)
                    for a in range(2):
                        t, c = TILE[kind][a], (step if a == 0 else 1 - step)
                        rows = slice(64 * c, 64 * c + 64)
                        b = 8 * a + 4 * hq
                        dve.wait_ge(vn_mm[a], 2 * p + step + 1)
                        v = ps[rows, 2 + 2 * a, :].rearrange("p (h i) -> p h i", h=4)
                        V.tensor_tensor(dn_d[a][rows, 0, :, :], v, g_be[rows, t, b:b + 4].unsqueeze(2).to_broadcast([64, 4, P]), ALU.mult)
                        V.tensor_tensor(dn_o[a][rows, :, :], v, g_beta[rows, t, b:b + 4].unsqueeze(2).to_broadcast([64, 4, P]), ALU.mult).then_inc(vn_ready[a], 1)
                    for a in range(2):
                        t, c = TILE[kind][a], (step if a == 0 else 1 - step)
                        dve.wait_ge(ds_mm[a], 2 * p + step + 1)
                        st = dn_s[:, min(kind, 1), a, :]
                        for h in range(4):
                            cd = 48 + 16 * c + 8 * a + 4 * hq + h
                            last = V.scalar_tensor_tensor(st[:, h * P:(h + 1) * P], st[:, h * P:(h + 1) * P], g_tot[:, t, cd:cd + 1],
                                                          ps[:, 3 + 2 * a, h * P:(h + 1) * P], ALU.mult, ALU.add)
                        last.then_inc(s_ready[a], 1)
                for a in range(2):
                    if LAST_DIR_ADDS[kind][a]:
                        t = TILE[kind][a]
                        dve.wait_ge(o_mm[a], p + 1)
                        dve.wait_ge(o_out[0], p + 1 if kind == 0 else p)
                        dve.wait_ge(o_out[1], p)
                        o = o_t[:, 4 * hq:4 * hq + 4, t * P:(t + 1) * P]
                        V.tensor_tensor(o, o, ps[:, 6 + a, :].rearrange("p (h i) -> p h i", h=4), ALU.add).then_inc(o_out[a], 1)
            for i in range(KD):
                dve.wait_ge(o_rs, i + 1)
                link(V.scalar_tensor_tensor(o_t[:, i, :], o_t[:, i, :], col("dn_norm"), o_rs_t[:, i % 2, :], ALU.mult, ALU.mult))
                V.tensor_tensor(mix[:, KD + i, :], mix[:, KD + i, :], o_t[:, i, :], ALU.mult).then_inc(o_ready, 1)
            dve.wait_ge(x_in, 96)
            V.tensor_tensor(x0_t[:, :, SEQ:TOK], x0_t[:, :, SEQ:TOK], k_t[:, :, 0:DEC_SEQ], ALU.add).then_inc(x_ready, 1)
            dve.wait_ge(x_ready, 2)
            for b in range(KD):
                dve.wait_ge(out_mm, b + 1)
                for c, (lo, hi) in enumerate(SEGS):
                    last = V.scalar_tensor_tensor(x1_t[:, b, lo:hi], ps[:, b % 2, lo:hi], mod[:, 2 * KD + b, c:c + 1], x0_t[:, b, lo:hi], ALU.mult, ALU.add)
                last.then_inc(x1_ready, 1)
            V.scalar_tensor_tensor(amp2[:, :, :], mod[:, 4 * KD:5 * KD, :], 1.0, cols("norm2").unsqueeze(2).to_broadcast([P, KD, 2]), ALU.add, ALU.mult)
            dve.wait_ge(x1_ready, KD)
            dve.wait_ge(rs_ready, 3)
            link(V.tensor_tensor(h2_t, x1_t[:, :, :], rs2.unsqueeze(1).to_broadcast([P, KD, TOK]), ALU.mult))
            for c, (lo, hi) in enumerate(SEGS):
                for k in range(KD):
                    last = V.tensor_scalar(h2_t[:, k, lo:hi], h2_t[:, k, lo:hi], amp2[:, k, c:c + 1], mod[:, 3 * KD + k, c:c + 1], ALU.mult, ALU.add)
            last.then_inc(h2_ready, 1)
            AX = mybir.AxisListType.X
            desc8 = cols("desc8")
            wide = lambda v, n: v.to_broadcast([P, TT, n])

            def pick_first(out, values, top, n):
                d = desc8[:, 0:n].unsqueeze(1).to_broadcast([P, TT, n])
                link(V.tensor_tensor(e_eq[:, :, 0:n], values, wide(top, n), ALU.is_equal))
                link(V.tensor_tensor(e_eq[:, :, 0:n], e_eq[:, :, 0:n], d, ALU.mult))
                link(V.tensor_reduce(e_pick, e_eq[:, :, 0:n], AX, ALU.max))
                link(V.tensor_tensor(out, d, wide(e_pick, n), ALU.is_equal))

            dve.wait_ge(lg_mm, 1)
            link(V.tensor_tensor(lg, ps[:, 7, 0:TT * N_ROUTE].rearrange("p (t n) -> p t n", t=TT),
                                 cols("route_bias").unsqueeze(1).to_broadcast([P, TT, N_ROUTE]), ALU.add))
            link(V.tensor_reduce(gmax, lg[:, :, 0:4], AX, ALU.max))
            V.tensor_tensor(g_exp, lg[:, :, 0:4], wide(gmax, 4), ALU.subtract).then_inc(gd_ready, 1)
            pick_first(gpick, lg[:, :, 0:4], gmax, 4)
            ge = lambda v: v.rearrange("p t (g e) -> p t g e", g=N_GROUPS)
            of_g = lambda v: v.unsqueeze(3).to_broadcast([P, TT, N_GROUPS, PER_GROUP])
            of_e = lambda v: v.unsqueeze(2).to_broadcast([P, TT, N_GROUPS, PER_GROUP])
            link(V.tensor_tensor(ge(spread), ge(lg[:, :, 4:N_ROUTE]), of_g(gpick), ALU.mult))
            link(V.tensor_reduce(es, spread.rearrange("p t (g e) -> p t e g", g=N_GROUPS), AX, ALU.add))
            link(V.tensor_reduce(e_top[:, :, 0:1], es, AX, ALU.max))
            pick_first(pick1, es, e_top[:, :, 0:1], 8)
            link(V.scalar_tensor_tensor(es_rest, pick1, -1e30, es, ALU.mult, ALU.add))
            link(V.tensor_reduce(e_top[:, :, 1:2], es_rest, AX, ALU.max))
            V.tensor_tensor(e_p2, e_top[:, :, 1:2], e_top[:, :, 0:1], ALU.subtract).then_inc(ed_ready, 1)
            pick_first(pick2, es_rest, e_top[:, :, 1:2], 8)
            V.tensor_tensor(ge(a1), of_g(gpick), of_e(pick1), ALU.mult)
            link(V.tensor_tensor(ge(a2), of_g(gpick), of_e(pick2), ALU.mult))
            V.tensor_tensor(any_e, a1, a2, ALU.add).then_inc(any_ready, 1)
            dve.wait_ge(gexp_ready, 1)
            link(V.tensor_reduce(g_w, g_exp, AX, ALU.add))
            dve.wait_ge(eexp_ready, 1)
            link(V.scalar_tensor_tensor(g_w, e_p2, 1.0, g_w, ALU.add, ALU.mult))
            link(V.reciprocal(e_w1, g_w))
            link(V.tensor_tensor(e_w2, e_w1, e_p2, ALU.mult))
            V.tensor_tensor(wsum, pick1, wide(e_w1, 8), ALU.mult)
            link(V.tensor_tensor(es, pick2, wide(e_w2, 8), ALU.mult))
            link(V.tensor_tensor(wsum, wsum, es, ALU.add))
            link(V.tensor_tensor(ge(comb), of_g(gpick), of_e(wsum), ALU.mult))
            V.tensor_copy(tg.rearrange("p t (j x) -> p t j x", x=3)[:, :, :, 1:3], comb.rearrange("p t (j x) -> p t j x", x=2))
            V.tensor_copy(tg.rearrange("p t (j x) -> p t j x", x=3)[:, :, :, 0:1],
                          cols("tok_id").unsqueeze(2).unsqueeze(3).to_broadcast([P, TT, NPAIR, 1]))
            dve.wait_ge(rank_mm, 1)
            rp = ps[:, 7, 0:TT * N_EXPERTS].rearrange("p (t e) -> p t e", t=TT)
            V.tensor_copy(counts, ps[:, 7, TT * N_EXPERTS:(TT + 1) * N_EXPERTS])
            link(V.tensor_copy(rank, rp))
            link(V.scalar_tensor_tensor(rank_only, any_e, -1000.0, rank, ALU.mult, ALU.add))
            link(V.tensor_scalar(rank_only, rank_only, 1000.0, None, ALU.add))
            iota = masks_sb[:, MI["iota"], 0:CAP].unsqueeze(1).to_broadcast([P, N_EXPERTS, CAP])
            for t in range(TT):
                last = V.tensor_tensor(sel[:, t, :, :], iota, rank_only[:, t, :].unsqueeze(2).to_broadcast([P, N_EXPERTS, CAP]), ALU.is_equal)
            last.then_inc(sel_ready, 1)
            V.scalar_tensor_tensor(over, rank, float(CAP), comb, ALU.is_ge, ALU.mult)
            dve.wait_ge(info_mm, 1)
            link(V.tensor_copy(slot_info[:, :, :], ps[:, 0, 0:3 * NPAIR].rearrange("p (j x) -> p j x", x=3)))
            V.tensor_copy(slot_gate[0:64, :], slot_info[0:64, :, 1])
            V.tensor_copy(slot_gate[64:128, :], slot_info[64:128, :, 2])
            V.tensor_copy(slot_tok[:, :], slot_info[:, :, 0]).then_inc(slots_ready, 1)
            dve.wait_ge(slots_ready, 1)
            link(V.tensor_reduce(most_f, counts, AX, ALU.max))
            V.tensor_copy(most[:, 0:1], most_f).then_inc(most_ready, 1)

            dve.wait_ge(h2_stored, 16 * TT)
            V.memset(y_acc, 0.0).then_inc(acc_added, 1)
            for t in range(TT):
                last = V.tensor_scalar(iota_w[:, t * P:(t + 1) * P], masks_sb[:, MI["iota"], :], float(t * P), None, ALU.add)
            last.then_inc(acc_added, 1)
            dve.wait_ge(acc_added, 2)

            def turned_half(i):
                dve.wait_ge(xgt_mm, i + 1)
                V.tensor_copy(xg_t[:, 0:4, :], ps[:, 0, :].rearrange("p (k i) -> p k i", k=4)).then_inc(xgt_ready, 1)

            def expert_pair(i, more):
                tok = slot_info[:, bass.ds(i, 1), 0] if more else slot_info[:, i, 0:1]
                gate = slot_gate[:, bass.ds(i, 1)] if more else slot_gate[:, i:i + 1]
                dve.wait_ge(gate_mm, i + 1)
                V.tensor_scalar(sel_t, iota_w, tok, None, ALU.is_equal)
                dve.wait_ge(up_mm, i + 1)
                dve.wait_ge(silu_done, i + 1)
                V.scalar_tensor_tensor(e_act, e_silu, gate, ps[:, 3, :], ALU.mult, ALU.mult).then_inc(hact_ready, 1)
                if more:
                    turned_half(i + 1)
                dve.wait_ge(down_mm, i + 1)
                V.tensor_copy(e_y[:, 0:512], ps[:, 5, :]).then_inc(y_half, 1)
                for m in range(2 * TT):
                    t, n = m // 2, m % 2
                    dve.wait_ge(spread_mm, i * 6 + m + 1)
                    a = y_acc[:, t, n * 512:(n + 1) * 512]
                    V.tensor_tensor(a, a, ps[:, (7, 4)[n], :], ALU.add).then_inc(acc_added, 1)

            turned_half(0)
            with dve.Fori(0, NPAIR - 1) as i:
                expert_pair(i, True)
            expert_pair(NPAIR - 1, False)

            def finish(t):
                dve.wait_ge(x2_rs, t + 1)
                V.scalar_tensor_tensor(y_acc[:, t, :], y_acc[:, t, :], ss[:, 4 + t:5 + t], final_row, ALU.mult, ALU.mult).then_inc(out_ready, 1)

            with dve.If(more_than_cap(dve)):
                dve.sem_inc(rest_added, 1)
                with dve.Fori(0, N_EXPERTS) as e:
                    for t in range(TT):
                        dve.wait_ge(rest_silu, e * TT + t + 1)
                        V.scalar_tensor_tensor(e_act, e_silu, over[:, t, bass.ds(e, 1)], ps[:, 1, :], ALU.mult, ALU.mult).then_inc(rest_act, 1)
                        dve.wait_ge(rest_down_mm, e * TT + t + 1)
                        V.tensor_tensor(o_scaled, ps[:, 3:5, :].rearrange("p n d -> p (n d)"), gt2_row[:, min(t, 1), :], ALU.mult).then_inc(rest_scaled, 1)
                        dve.wait_ge(rest_scaled, e * TT + t + 1)
                        V.tensor_tensor(x1_tok[:, t, :], x1_tok[:, t, :], o_scaled, ALU.add).then_inc(rest_added, 1)

            for t in range(TT):
                link(V.tensor_tensor(y_acc[:, t, :], y_acc[:, t, :], gt2_row[:, min(t, 1), :], ALU.mult))
                V.tensor_tensor(y_acc[:, t, :], y_acc[:, t, :], x1_tok[:, t, :], ALU.add).then_inc(x2_ready, 1)
                if t:
                    finish(t - 1)
            finish(TT - 1)


def _masks():
    import numpy as np
    p, f = np.arange(P)[:, None], np.arange(P)[None, :]
    same = (p // 64) == (f // 64)
    out = {"ident": p == f, "ones": p >= 0 * f, "upper": p <= f, "lower": p >= f, "upper64": (p <= f) & same, "lower64": (p >= f) & same,
           "ones64": same, "first64": (p < 64) & (f >= 0), "last64": (p >= 64) & (f >= 0), "strict_up": p < f, "iota": f + 0 * p,
           "eps": EPS + 0.0 * (p + f)}
    for m in LEVELS:
        pair = (p // (2 * m)) == (f // (2 * m))
        p_odd, f_odd = (p // m) % 2 == 1, (f // m) % 2 == 1
        out[f"lev0_{m}"] = pair & ~p_odd & f_odd
        out[f"lev1_{m}"] = pair & p_odd & ~f_odd
    return np.ascontiguousarray(np.stack([out[n] for n in MASKS], 1), dtype=np.float32)


def _positions():
    import numpy as np
    quarter = D_MODEL // 4
    omega = (1.0 / (np.float32(10000.0) ** (np.arange(quarter, dtype=np.float32) / np.float32(quarter)))).astype(np.float32)
    n = np.arange(DEC_SEQ)
    ar = (n // 64).astype(np.float32)[:, None] * omega
    ac = (n % 64).astype(np.float32)[:, None] * omega
    return np.ascontiguousarray(np.concatenate([np.sin(ar), np.cos(ar), np.sin(ac), np.cos(ac)], -1).T, dtype=np.float32)


def _layout(inputs):
    import numpy as np
    g = {k: np.asarray(v) for k, v in inputs.items()}

    def on_partitions(v):
        return np.reshape(v, (-1, P)).T

    def on_all(v):
        return np.broadcast_to(np.reshape(v, (1, -1)), (P, np.size(v)))

    conv_w = np.concatenate([g["conv_ssd_w"][0], g["conv_dn_w"][0]], 1)
    parts = {
        "c": np.stack([on_partitions(g["c_ctx"]), on_partitions(g["c"][0])], 2).reshape(P, -1),
        "b_ada": on_partitions(g["b_ada"][0]),
        "norm1": on_partitions(g["norm1_w"][0]), "norm2": on_partitions(g["norm2_w"][0]), "final": on_partitions(g["final_norm_w"]),
        "ssd_norm": on_partitions(g["ssd_norm_w"][0]), "dn_norm": on_partitions(g["dn_norm_w"][0]),
        "ssd_d": on_partitions(np.repeat(g["ssd_d"][0], SSD_HEAD_DIM)),
        "conv_w": conv_w.reshape(CONV_W, -1, P).transpose(2, 1, 0).reshape(P, -1),
        "conv_b": on_partitions(np.concatenate([g["conv_ssd_b"][0], g["conv_dn_b"][0]])),
        "gate_bias": on_all(np.concatenate([g["ssd_dt_bias"].ravel(), g["dn_dt_bias"].ravel()])),
        "a_log": on_all(np.concatenate([g["ssd_a_log"].ravel(), g["dn_a_log"].ravel()])),
        "route_bias": on_all(np.concatenate([g["b_router_group"].ravel(), g["b_router_expert"].ravel()])),
    }
    parts["desc8"] = on_all(np.arange(8, 0, -1, dtype=np.float32))
    parts["tok_id"] = on_partitions(np.arange(TOK, dtype=np.float32))
    params = np.concatenate([parts[n] for n in PC], 1)
    h0 = np.stack([g["state_ssd_fwd"][0, 0], g["state_ssd_bwd"][0, 0]])
    h0 = h0.reshape(2, SSD_GROUPS, 8, SSD_HEAD_DIM, SSD_STATE).transpose(0, 1, 4, 2, 3).reshape(2, P, 512)
    s0 = np.stack([g["state_dn_fwd"][0, 0], g["state_dn_bwd"][0, 0]]).transpose(0, 2, 1, 3)
    router = np.concatenate([g["w_router_group"][0], g["w_router_expert"][0]], 1).reshape(KD, P, N_ROUTE).transpose(1, 0, 2)
    c = np.ascontiguousarray
    return {"x_t": c(g["x_prompt"][0].T), "xs_t": c(g["x_sample"][0].T), "pos_t": _positions(), "params": c(params), "masks": _masks(),
            "w_ada": g["w_ada"][0], "w_in": g["w_in"][0], "w_out": g["w_out"][0], "h0_ssd": c(h0), "s0_dn": c(s0), "router": c(router),
            "w_gate": g["w_gate"][0], "w_up": g["w_up"][0], "w_down": g["w_down"][0]}


_INS = ["x_t", "xs_t", "pos_t", "params", "masks", "w_ada", "w_in", "w_out", "h0_ssd", "s0_dn", "router", "w_gate", "w_up", "w_down"]
_OUTS = [(SEQ, D_MODEL), (DEC_SEQ, D_MODEL), (SSD_WIDTH, SSD_STATE), (SSD_WIDTH, SSD_STATE), (P, DN_HEADS, P), (P, DN_HEADS, P)]


def kernel(**inputs):
    import numpy as np
    import concourse.bacc as _bacc
    from concourse import mybir as _mybir
    from concourse.bass_utils import run_bass_kernel_spmd as _run

    nc = _bacc.Bacc("TRN2", target_bir_lowering=False, num_devices=1)
    given = _layout(inputs)
    f32 = _mybir.dt.float32
    arrays = {f"in_{n}": given[n] for n in _INS}
    args = [nc.dram_tensor(f"in_{n}", given[n].shape, f32, kind="ExternalInput").ap() for n in _INS]
    h2_dram = nc.dram_tensor("h2_rows", (TOK, D_MODEL), f32, kind="Internal").ap()
    outs = [nc.dram_tensor(f"out_{i}", s, f32, kind="ExternalOutput").ap() for i, s in enumerate(_OUTS)]
    hybrid_step(nc, *args, h2_dram, outs)
    r = _run(nc, [arrays], core_ids=[0])
    y_p, y_s, s_f, s_b, d_f, d_b = (r.results[0][f"out_{i}"] for i in range(len(_OUTS)))
    ssd = (1, 1, SSD_HEADS, SSD_HEAD_DIM, SSD_STATE)
    return (y_p.reshape(1, SEQ, D_MODEL), y_s.reshape(1, DEC_SEQ, D_MODEL), s_f.reshape(ssd), s_b.reshape(ssd),
            np.ascontiguousarray(d_f.transpose(1, 0, 2))[None, None], np.ascontiguousarray(d_b.transpose(1, 0, 2))[None, None])
```

```python
import concourse.bass as bass
from concourse import mybir
from contextlib import ExitStack

P = 128
D_MODEL = 1024
KD = D_MODEL // P
SEQ, DEC_SEQ = 128, 256
TOK = SEQ + DEC_SEQ
TT = TOK // P
SEGS = ((0, SEQ), (SEQ, TOK))
EPS = 1e-6
CONV_W = 5
N_MOD = 6
NBM = N_MOD * KD
SSD_HEADS, SSD_HEAD_DIM, SSD_STATE, SSD_GROUPS = 16, 64, 64, 2
SSD_WIDTH = SSD_HEADS * SSD_HEAD_DIM
SSD_XBC = SSD_WIDTH + 2 * SSD_GROUPS * SSD_STATE
DN_HEADS, DN_HEAD_DIM, DN_CHUNK = 8, 128, 64
DN_WIDTH = DN_HEADS * DN_HEAD_DIM
N_GROUPS, PER_GROUP = 4, 8
N_EXPERTS = N_GROUPS * PER_GROUP
N_ROUTE = N_GROUPS + N_EXPERTS
F_EXP = 512
FK = F_EXP // P
CHUNK_COLS = 512

XBC0 = SSD_WIDTH
DT0 = XBC0 + SSD_XBC
QKV0 = DT0 + 2 * SSD_HEADS
ZD0 = QKV0 + 3 * DN_WIDTH
AB0 = ZD0 + DN_WIDTH
N_DT = 2 * SSD_HEADS
N_AB = 4 * DN_HEADS
CONV_BLOCKS = (SSD_XBC + 3 * DN_WIDTH) // P

_cols, PC = 0, {}
for _name, _n in (("c", 2 * KD), ("b_ada", NBM), ("norm1", KD), ("norm2", KD), ("final", KD),
                  ("ssd_norm", KD), ("dn_norm", 1), ("ssd_d", KD), ("conv_w", CONV_BLOCKS * CONV_W),
                  ("conv_b", CONV_BLOCKS), ("gate_bias", 48), ("a_log", 48), ("route_bias", N_ROUTE), ("desc8", 8), ("tok_id", TT)):
    PC[_name] = (_cols, _cols + _n)
    _cols += _n
N_PC = _cols

LEVELS = (1, 2, 4, 8, 16, 32)
MASKS = ["ident", "ones", "upper", "lower", "upper64", "lower64", "ones64", "first64", "last64", "strict_up"] + \
        [f"lev{d}_{m}" for d in (0, 1) for m in LEVELS] + ["iota", "eps"]
MI = {n: i for i, n in enumerate(MASKS)}


def hybrid_step(nc, x_t, xs_t, pos_t, params, masks, w_ada, w_in, w_out, h0_ssd, s0_dn, router, w_gate, w_up, w_down,
                h2_dram, outs):
    fp32, fp32r = mybir.dt.float32, mybir.dt.float32r
    ALU = mybir.AluOpType
    ACT = mybir.ActivationFunctionType
    ctx = ExitStack()
    with ctx:
        def sb(name, shape, dt=fp32):
            return ctx.enter_context(nc.sbuf_tensor(name, shape, dt))

        def sem(name):
            return ctx.enter_context(nc.semaphore(name))

        RING = 4
        ring_a = sb("ring_a", [P, 2, KD, CHUNK_COLS])
        with nc.sbuf_tensor("w_split", [P, 4, 2, KD, P], fp32r) as w_split:
            pass
        ring_b = sb("ring_b", [P, 2, KD, CHUNK_COLS])
        with nc.sbuf_tensor("h1_hi", [P, KD, TOK], fp32r) as h1_hi:
            pass
        buf_h = sb("buf_h", [P, KD * TOK])
        mix = sb("mix", [P, 2 * KD, TOK])
        x_ssd = sb("x_ssd", [P, KD, TOK])
        bc = sb("bc", [P, 2, TOK])
        q_t = sb("q_t", [P, KD, TOK])
        kv = sb("kv", [P, 2 * KD, TOK])
        k_t, v_t = kv[:, 0:KD, :], kv[:, KD:2 * KD, :]
        masks_sb = sb("masks_sb", [P, len(MASKS), P])
        pc = sb("pc", [P, N_PC])
        mod = sb("mod", [P, NBM, 2])
        amp1 = sb("amp1", [P, KD, 2])
        silu_c = sb("silu_c", [P, 2 * KD])
        w_ab = sb("w_ab", [P, KD, N_DT + N_AB])
        gates = sb("gates", [P, TT, 256])
        cums = sb("cums", [P, TT, P])
        b_tok = sb("b_tok", [P, TT, P])
        with nc.sbuf_tensor("below_h1_lo", [P, 4096], fp32), nc.sbuf_tensor("h1_lo", [P, KD, TOK], fp32r) as h1_lo:
            pass
        temp = sb("temp", [P, 8704])

        def carve(start, *dims):
            n = 1
            for d in dims:
                n *= d
            v = temp[:, start:start + n]
            if len(dims) == 1:
                return v
            names = "abcd"[:len(dims)]
            return v.rearrange(f"p ({' '.join(names)}) -> p {' '.join(names)}", **{c: d for c, d in zip(names[1:], dims[1:])})

        ps = ctx.enter_context(nc.psum_tensor("ps", [P, 8, 512], fp32))

        def mask(name):
            return masks_sb[:, MI[name], :]

        def col(name, i=0):
            a = PC[name][0] + i
            return pc[:, a:a + 1]

        def cols(name):
            a, b = PC[name]
            return pc[:, a:b]

        x0_t = q_t
        h1_t = v_t
        h2_t = buf_h[:, :].rearrange("p (k t) -> p k t", k=KD)
        x_tok = buf_h[:, :].rearrange("p (t c) -> p t c", t=TT)
        k_tok = x_tok
        v_tok = x_ssd[:, :, :].rearrange("p k t -> p (k t)").rearrange("p (t c) -> p t c", t=TT)
        o_t = v_t
        g_log, g_dt, g_beta = gates[:, :, 0:48], gates[:, :, 48:80], gates[:, :, 80:96]
        g_dte, g_be, g_nec, g_tot = gates[:, :, 96:128], gates[:, :, 128:144], gates[:, :, 144:160], gates[:, :, 160:240]

        wi = w_in.rearrange("(k p) n -> p k n", p=P)
        wa = w_ada.rearrange("(k p) n -> p k n", p=P)
        wo = w_out.rearrange("(k p) n -> p k n", p=P)
        proj_cols = [(XBC0, 512), (XBC0 + 512, 512), (XBC0 + 1024, 256)] + \
                    [(QKV0 + 512 * c, 512) for c in range(6)] + [(0, 512), (512, 512), (ZD0, 512), (ZD0 + 512, 512)]
        LOAD_PROJ, LOAD_ADA1, LOAD_ADA2, LOAD_OUT = 4, 17, 21, 25
        blocks = []
        for n, (a, w) in enumerate(proj_cols):
            for b in range(w // P):
                i = len(blocks)
                blocks.append((LOAD_PROJ + n, b * P, "conv" if i < CONV_BLOCKS else "z", i if i < CONV_BLOCKS else i - CONV_BLOCKS))
        NB = len(blocks)
        last_block = lambda load: max(n for n, blk in enumerate(blocks) if blk[0] == load)

        def conv_dest(i):
            if i < 8:
                return x_ssd[:, i, :]
            if i < 10:
                return bc[:, i - 8, :]
            return (q_t, k_t, v_t)[(i - 10) // KD][:, (i - 10) % KD, :]

        pc_in = sem("pc_in")
        x_in = sem("x_in")
        masks_in = sem("masks_in")
        wab_in = sem("wab_in")
        h0_in = sem("h0_in")
        s0_in = sem("s0_in")
        w_in_sem = [sem(f"w_ready{i}") for i in range(RING)]
        dve_step = sem("dve_step")
        act_step = sem("act_step")
        silu_ready = sem("silu_ready")
        x_ready = sem("x_ready")
        sq_ready = sem("sq_ready")
        stat_ready = sem("stat_ready")
        rs_ready = sem("rs_ready")
        ada_mm = sem("ada_mm")
        row_ready = sem("row_ready")
        modp_ready = sem("modp_ready")
        mod_ready = sem("mod_ready")
        h1_full = sem("h1_full")
        h1_hi_ready = sem("h1_hi_ready")
        h1_ready = sem("h1_ready")
        hi_ready = sem("hi_ready")
        split_ready = sem("split_ready")
        block_mm = sem("block_mm")
        block_out = sem("block_out")
        conv_done = sem("conv_done")
        conv_out = sem("conv_out")
        tok_mm = sem("tok_mm")
        na_ready = sem("na_ready")
        ln_ready = sem("ln_ready")
        log_ready = sem("log_ready")
        cum_mm = sem("cum_mm")
        cum_ready = sem("cum_ready")
        exps_ready = sem("exps_ready")
        qk_sq = sem("qk_sq")
        qk_sum = sem("qk_sum")
        qk_rs = sem("qk_rs")
        qk_ready = sem("qk_ready")
        xt_mm = sem("xt_mm")
        xt_ready = sem("xt_ready")
        xe_ready = sem("xe_ready")
        st_mm = sem("st_mm")
        st_out = sem("st_out")
        h_ready = sem("h_ready")
        cb_mm = sem("cb_mm")
        cb_ready = sem("cb_ready")
        seg_mm = sem("seg_mm")
        seg_ready = sem("seg_ready")
        dec_ready = sem("dec_ready")
        ssd_m_ready = sem("ssd_m_ready")
        y_mm = sem("y_mm")
        y_ready = sem("y_ready")
        ynorm_ready = sem("ynorm_ready")
        states_out = sem("states_out")
        out_mm = sem("out_mm")
        kvt_mm = sem("kvt_mm")
        kvt_ready = sem("kvt_ready")
        s_zero = sem("s_zero")
        two = lambda name: [sem(f"{name}_fwd"), sem(f"{name}_bwd")]
        dseg_mm = two("dseg_mm")
        kq_mm = two("kq_mm")
        dseg_ready = two("dseg_ready")
        dec_exp = two("dec_exp")
        m_ready = two("dn_m_ready")
        off_ready = two("off_ready")
        d_ready = two("d_ready")
        lev_mm1 = two("lev_mm1")
        lev_p = two("lev_p")
        lev_mm2 = two("lev_mm2")
        ks_mm = two("ks_mm")
        r_ready = two("r_ready")
        vn_mm = two("vn_mm")
        vn_ready = two("vn_ready")
        ds_mm = two("ds_mm")
        s_ready = two("s_ready")
        o_mm = two("o_mm")
        o_out = two("o_out")
        o_sq = sem("o_sq")
        o_sum = sem("o_sum")
        o_rs = sem("o_rs")
        o_ready = sem("o_ready")

        PAIRS = [(hq, kind) for hq in range(2) for kind in range(3)]
        def ada(g, order, before):
            return [(wa[:, :, c * 512:(c + 1) * 512], 512, slot, before) for c, slot in zip(range(4 * g, 4 * g + 4), order)]

        def proj_before(n):
            return None if n == 0 else (ada_mm, 1) if n <= 2 else (split_ready, 1 + last_block(LOAD_PROJ + n - 2))

        proj_slot = lambda n: RING if n == 0 else n % 2
        n_proj = len(proj_cols)
        ada1 = ada(1, ((n_proj - 2) % 2, (n_proj - 1) % 2, 2, 3), (split_ready, 1 + last_block(LOAD_PROJ + n_proj - 2)))
        ada1[1] = ada1[1][:3] + ((split_ready, NB),)
        ada1[2:] = [load[:3] + ((block_mm, NB),) for load in ada1[2:]]
        loads = ada(0, range(4), None) + \
            [(wi[:, :, a:a + w], w, proj_slot(n), proj_before(n)) for n, (a, w) in enumerate(proj_cols)] + \
            ada1 + ada(2, range(4), (ada_mm, 2)) + \
            [(wo[:, kh * KD:(kh + 1) * KD, dh * 512:(dh + 1) * 512], 512, 2 * dh + kh, ((ada_mm, 3), (o_mm[1], len(PAIRS)))[dh]) for dh in range(2) for kh in range(2)]
        slot_of = [load[2] for load in loads]
        arrivals = lambda load: slot_of[:load + 1].count(slot_of[load])

        pad = carve(0, 2, 392)
        conv_acc = carve(784, 2, 388)
        mod_row = carve(1600, 4, 512)
        rs1 = carve(3700, TOK)
        sg = carve(0, 6, TT, 48)
        sq = carve(1024, 2, TOK)
        rs = carve(1792, 2, TOK)
        x_end = carve(0, 4, SSD_WIDTH)
        seg = [carve(1024 * i, 2, 4, P) for i in range(3)]
        c_dec = carve(3072, 2, 2, 4 * P).rearrange("p n d (h i) -> p n d h i", h=4)
        st_stage = carve(5120, 2, KD, SSD_STATE)
        h_st = carve(6144, 4, 512)
        cbm = carve(8192, 2, 2, P)
        y_tmp = w_ab[:, :, :].rearrange("p k n -> p (k n)").rearrange("p (n b i) -> p n b i", n=2, b=2)
        y_sq = carve(0, KD, TOK)
        y_rs = carve(8192, TOK)

        CAP = 64
        NPAIR = N_EXPERTS // 2
        x1_t = q_t
        x1_tok = x_ssd[:, :, :].rearrange("p k t -> p (k t)").rearrange("p (t c) -> p t c", t=TT)
        h2_tok = carve(0, TT, D_MODEL)
        rs2 = carve(8192, TOK)
        amp2 = amp1
        kv_flat = kv[:, :, :].rearrange("p k t -> p (k t)")
        mix_flat = mix[:, :, :].rearrange("p k t -> p (k t)")
        slots = [r[:, i, :, :] for r in (ring_a, ring_b) for i in range(2)] + [m[:, 0:KD * 512].rearrange("p (k n) -> p k n", k=KD) for m in (mix_flat, kv_flat)]
        down = [m.rearrange("p k n -> p (k n)").rearrange("p (f n) -> p f n", f=FK) for m in slots]
        slot_in = w_in_sem + [sem("w_ready4"), sem("w_ready5")]
        n_loads = [slot_of.count(s) for s in range(6)]
        router_sb = bc[:, :, :].rearrange("p k t -> p (k t)")[:, 0:KD * N_ROUTE].rearrange("p (k n) -> p k n", k=KD)
        rt = kv_flat[:, 4096:4096 + TT * 600].rearrange("p (t n) -> p t n", t=TT)
        take = [0]

        def field(n):
            take[0] += n
            return rt[:, :, take[0] - n:take[0]]

        lg, gmax, geq, gpick, g_exp, g_w = field(N_ROUTE), field(1), field(4), field(4), field(4), field(1)
        es, es_rest, e_top, e_eq, e_pick, pick1, pick2 = field(8), field(8), field(2), field(8), field(1), field(8), field(8)
        e_p2, e_w1, e_w2, wsum = field(1), field(1), field(1), field(8)
        spread, a1, a2, any_e, comb, rank, rank_only, over = [field(N_EXPERTS) for _ in range(8)]
        tg = field(3 * NPAIR)
        sel = mix[:, :, :].rearrange("p k t -> p (k t)").rearrange("p (t e c) -> p t e c", t=TT, e=N_EXPERTS)
        slot_info = sb("slot_info", [P, NPAIR, 3])
        slot_gate = sb("slot_gate", [P, NPAIR])
        slot_tok = sb("slot_tok", [P, NPAIR], mybir.dt.uint32)
        cur_tok = sb("cur_tok", [P, 1], mybir.dt.uint32)
        xg = carve(3072, D_MODEL)
        xg_t = carve(4096, KD, P)
        e_silu = carve(5120, F_EXP)
        e_act = carve(5632, F_EXP)
        e_act_t = carve(6144, FK, P)
        e_y = carve(6656, D_MODEL)
        sel_t = carve(7680, TOK)
        iota_w = carve(8192, TOK)
        y_acc = carve(0, TT, D_MODEL)
        x2_sq = carve(4096, D_MODEL)
        ss, most_f, counts = cums[:, 0, 0:8], cums[:, 0, 8:9], cums[:, 0, 16:48]
        gt2_row = q_t[:, :, :].rearrange("p k t -> p (k t)")[:, 0:2048].rearrange("p (c d) -> p c d", c=2)
        final_row = q_t[:, :, :].rearrange("p k t -> p (k t)")[:, 2048:3072]
        most = sb("most", [P, 2], mybir.dt.int32)
        o_scaled = carve(4096, D_MODEL)
        most_ready = sem("most_ready")
        rest_in = [sem(f"rest_{n}_in") for n in ("gate", "up", "down")]
        rest_up_mm = sem("rest_up_mm")
        rest_silu = sem("rest_silu")
        rest_act = sem("rest_act")
        rest_at_mm = sem("rest_at_mm")
        rest_at = sem("rest_at")
        rest_down_mm = sem("rest_down_mm")
        rest_scaled = sem("rest_scaled")
        rest_added = sem("rest_added")
        router_in = sem("router_in")
        h2_stored = sem("h2_stored")
        x1_ready = sem("x1_ready")
        h2_ready = sem("h2_ready")
        lg_mm = sem("lg_mm")
        h2t_mm = sem("h2t_mm")
        h2t_ready = sem("h2t_ready")
        x1t_mm = sem("x1t_mm")
        x1t_ready = sem("x1t_ready")
        gd_ready = sem("gd_ready")
        gexp_ready = sem("gexp_ready")
        ed_ready = sem("ed_ready")
        eexp_ready = sem("eexp_ready")
        any_ready = sem("any_ready")
        rank_mm = sem("rank_mm")
        sel_ready = sem("sel_ready")
        info_mm = sem("info_mm")
        slots_ready = sem("slots_ready")
        rows_mm = sem("rows_mm")
        rows_ready = sem("rows_ready")
        cur_ready = sem("cur_ready")
        gather_go = sem("gather_go")
        xg_in = sem("xg_in")
        xgt_mm = sem("xgt_mm")
        xgt_ready = sem("xgt_ready")
        gate_mm = sem("gate_mm")
        up_mm = sem("up_mm")
        silu_done = sem("silu_done")
        hact_ready = sem("hact_ready")
        at_mm = sem("at_mm")
        at_ready = sem("at_ready")
        down_mm = sem("down_mm")
        y_half = sem("y_half")
        spread_mm = sem("spread_mm")
        acc_added = sem("acc_added")
        x2_ready = sem("x2_ready")
        x2_rs = sem("x2_rs")
        out_ready = sem("out_ready")
        out_stored = sem("out_stored")
        TILE = ((0, 0), (1, 2), (2, 1))
        LAST_DIR_ADDS = ((False, True), (False, False), (True, True))
        tiles = [[temp[:, 512 * i:512 * i + 512] for i in range(13)] + [slots[3][:, 6, :]],
                 [slots[2 + i // 8][:, i % 8, :] for i in range(14)]]
        tiles = [[v.rearrange("p (h i) -> p h i", h=4) for v in tiles[a]] for a in range(2)]
        dn_m, dn_p, dn_d, dn_r, dn_vb, dn_vo = [[tiles[a][i] for a in range(2)] for i in (0, 1, 2, 3, 4, 5)]
        dn_off, dn_e, dn_qk, dn_dt = [[[tiles[a][i], tiles[a][i + 1]] for a in range(2)] for i in (12, 6, 8, 10)]
        dn_s = carve(6656, 2, 2, 4 * P)
        bank_a, bank_b, bank_x, bank_o = (0, 2), (1, 3), (4, 5), (6, 7)
        DN_ROUND = ((1, 0), (0, 0), (1, 1), (1, 2), (0, 1), (1, 3), (0, 2), (1, 4), (1, 5), (0, 3), (1, 6), (1, 7), (0, 4), (1, 8),
                    (1, 9), (0, 5), (1, 10), (1, 11), (0, 6), (1, 12))

        def dn_rounds(chunk_step, inverse_step):
            for r in range(-1, len(PAIRS)):
                for inverse, n in DN_ROUND:
                    if inverse and r + 1 < len(PAIRS):
                        inverse_step(r + 1, n)
                    elif not inverse and r >= 0:
                        chunk_step(r, n)

        def dn_pair(p):
            return (*PAIRS[p], TILE[PAIRS[p][1]])

        def dn_rows(step, a):
            c = step if a == 0 else 1 - step
            return c, slice(64 * c, 64 * c + 64)

        mod_row1 = carve(4096, 4, 512)
        mod_row2 = carve(6144, 4, 512)
        o_sq_t = buf_h[:, 0:2 * TOK].rearrange("p (n t) -> p n t", n=2)
        o_rs_t = buf_h[:, 2 * TOK:4 * TOK].rearrange("p (n t) -> p n t", n=2)

        SSD_UNITS = [(t, u) for t in range(TT) for u in range(4)]
        ENDS = [(0, 0), (0, 1), (1, 0), (2, 1)]

        block = ctx.enter_context(nc.Block())

        def more_than_cap(eng):
            eng.wait_ge(most_ready, 1)
            return eng.value_load(most[0:1, 0:1], min_val=0, max_val=TOK) > CAP

        @block.sync
        def _(sp):
            sp.dma_start(pc[:, :], params).then_inc(pc_in, 16)
            sp.dma_start(x0_t[:, :, 0:SEQ], x_t.rearrange("(k p) t -> p k t", p=P)).then_inc(x_in, 16)
            sp.dma_start(x0_t[:, :, SEQ:TOK], xs_t.rearrange("(k p) t -> p k t", p=P)).then_inc(x_in, 16)
            sp.dma_start(k_t[:, :, 0:DEC_SEQ], pos_t.rearrange("(k p) t -> p k t", p=P)).then_inc(x_in, 16)
            def load(i):
                src, n, slot, before = loads[i]
                if before:
                    sp.wait_ge(*before)
                sp.dma_start(slots[slot][:, :, 0:n], src).then_inc(slot_in[slot], 16)

            for i in range(len(loads) - 2):
                load(i)
                if i == 3:
                    sp.dma_start(masks_sb[:, :, :], masks).then_inc(masks_in, 16)
                    sp.dma_start(w_ab[:, :, 0:N_DT], wi[:, :, DT0:DT0 + N_DT]).then_inc(wab_in, 16)
                    sp.dma_start(w_ab[:, :, N_DT:N_DT + N_AB], wi[:, :, AB0:AB0 + N_AB]).then_inc(wab_in, 16)

            for a in range(2):
                sp.wait_ge(o_mm[a], len(PAIRS))
            sp.dma_start(x0_t[:, :, 0:SEQ], x_t.rearrange("(k p) t -> p k t", p=P)).then_inc(x_in, 16)
            sp.dma_start(x0_t[:, :, SEQ:TOK], xs_t.rearrange("(k p) t -> p k t", p=P)).then_inc(x_in, 16)
            sp.dma_start(k_t[:, :, 0:DEC_SEQ], pos_t.rearrange("(k p) t -> p k t", p=P)).then_inc(x_in, 16)
            load(len(loads) - 2)
            load(len(loads) - 1)

            def expert_load(e, s):
                src = (w_gate, w_gate, w_up, w_up, w_down, w_down)[s]
                e = e + s % 2
                src = src[e, :, :] if isinstance(e, int) else src[bass.ds(e, 1), :, :].rearrange("a d f -> (a d) f")
                dst = slots[s] if s < 4 else down[s]
                sp.dma_start(dst, src.rearrange("(k p) n -> p k n", p=P)).then_inc(slot_in[s], 16)

            for s in range(6):
                if s < RING:
                    sp.wait_ge(out_mm, KD)
                elif s == 4:
                    for t in range(TT):
                        sp.wait_ge(h2t_ready, t + 1)
                        sp.dma_start(h2_dram[t * P:(t + 1) * P, :], h2_tok[:, t, :]).then_inc(h2_stored, 16)
                    sp.wait_ge(info_mm, 1)
                else:
                    sp.wait_ge(stat_ready, 3)
                    sp.wait_ge(x_ready, 2)
                expert_load(0, s)
            with sp.Fori(1, NPAIR) as i:
                for s in range(6):
                    sp.wait_ge((gate_mm, up_mm, down_mm)[s // 2], i)
                    expert_load(2 * i, s)
            with sp.If(more_than_cap(sp)):
                sp.wait_ge(down_mm, NPAIR)
                with sp.Fori(0, N_EXPERTS) as e:
                    sp.wait_ge(rest_added, e * TT + 1)
                    for n, src in enumerate((w_gate, w_up, w_down)):
                        dst = down[2] if n == 2 else slots[n]
                        sp.dma_start(dst, src[bass.ds(e, 1), :, :].rearrange("a (k p) n -> p (a k) n", p=P)).then_inc(rest_in[n], 16)
            for t in range(TT):
                sp.wait_ge(out_ready, t + 1)
                dst = outs[0] if t == 0 else outs[1][(t - 1) * P:t * P, :]
                sp.dma_start(dst, y_acc[:, t, :]).then_inc(out_stored, 16)
            sp.wait_ge(out_stored, 16 * TT)
        @block.gpsimd
        def _(pool):
            for n, (load, c, kind, i) in enumerate(blocks):
                pool.wait_ge(hi_ready, n + 1)
                nc.gpsimd.tensor_tensor(w_split[:, n % 4, 1, :, :], slots[slot_of[load]][:, :, c:c + P],
                                        w_split[:, n % 4, 0, :, :].bitcast(fp32), ALU.subtract).then_inc(split_ready, 1)
            pool.wait_ge(qk_ready, 2 * KD)
            for d in range(2):
                pool.dma_start(h_st[:, 2 * d, :], h0_ssd[d]).then_inc(h0_in, 16)
            for d in range(2):
                pool.wait_ge(st_out, d + 1)
                pool.dma_start(outs[2 + d].rearrange("(b q) n -> q b n", q=P), st_stage[:, d, :, :]).then_inc(states_out, 16)
            pool.wait_ge(ssd_m_ready, len(SSD_UNITS))
            pool.dma_start(router_sb, router).then_inc(router_in, 16)

            def first_states(hq):
                for d in range(2):
                    pool.dma_start(dn_s[:, 1, d, :], s0_dn[d, :, 4 * hq:4 * hq + 4, :].rearrange("k h v -> k (h v)")).then_inc(s0_in, 16)

            def inverse_step(p, n):
                lev = (n - 1) // 2 + 1 if n else 1
                if n == 0 or (n % 2 and 3 <= n <= 9):
                    for a in range(2):
                        pool.wait_ge(m_ready[a], 2 * p + 1)
                        if p or n:
                            pool.wait_ge(lev_mm1[a], 6 * p + lev - 1)
                        if lev == 2:
                            pool.wait_ge(d_ready[a], 7 * p + 2)
                        nc.gpsimd.tensor_tensor(dn_off[a][lev % 2], dn_m[a], mask(f"lev{a}_{LEVELS[lev]}").unsqueeze(1).to_broadcast([P, 4, P]),
                                                ALU.mult).then_inc(off_ready[a], 1)

            def chunk_step(p, n):
                hq, kind = PAIRS[p]
                if kind == 0 and n == 5:
                    for d in range(2):
                        pool.wait_ge(s_ready[d], 2 * p + 2)
                        pool.dma_start(outs[4 + d][:, 4 * hq:4 * hq + 4, :].rearrange("k h v -> k (h v)"), dn_s[:, 0, d, :]).then_inc(states_out, 16)
                if p == 2 and n == 5:
                    for d in range(2):
                        pool.wait_ge(s_ready[d], 2 * p + 2)
                    first_states(1)

            pool.wait_ge(modp_ready, 3)
            pool.wait_ge(ynorm_ready, 1)
            first_states(0)
            dn_rounds(chunk_step, inverse_step)
            pool.wait_ge(states_out, 96)

            def gather():
                pool.indirect_dma_start(out=xg, out_offset=None, in_=h2_dram,
                                        in_offset=bass.IndirectOffsetOnAxis(ap=cur_tok[:, 0:1], axis=0)).then_inc(xg_in, 16)

            pool.wait_ge(slots_ready, 1)
            pool.wait_ge(h2_stored, 16 * TT)
            nc.gpsimd.tensor_copy(cur_tok[:, :], slot_tok[:, 0:1]).then_inc(cur_ready, 1)
            pool.wait_ge(cur_ready, 1)
            gather()
            with pool.Fori(1, NPAIR) as i:
                pool.wait_ge(xg_in, i * 16)
                nc.gpsimd.tensor_copy(cur_tok[:, :], slot_tok[:, bass.ds(i, 1)]).then_inc(cur_ready, 1)
                pool.wait_ge(cur_ready, i + 1)
                pool.wait_ge(xgt_mm, i)
                pool.sem_inc(gather_go, 1)
                gather()

        @block.tensor
        def _(pe):
            def ready(i):
                pe.wait_ge(slot_in[slot_of[i]], 16 * arrivals(i))

            def ada_products(first, bank, ks):
                for k in ks:
                    for j in range(4):
                        if k == 0:
                            ready(first + j)
                        last = nc.tensor.matmul(ps[32 * j:32 * j + 2, bank, :], silu_c[:, 2 * k:2 * k + 2],
                                                slots[slot_of[first + j]][:, k, :], start=(k == 0), stop=(k == KD - 1), tile_position=(0, 32 * j))
                if k == KD - 1:
                    last.then_inc(ada_mm, 1)

            def ada_columns(g, rows):
                pe.wait_ge(row_ready, g + 1)
                if g:
                    pe.wait_ge(mod_ready, g)
                for j in range(4):
                    for b in range(4):
                        m = 16 * g + 4 * j + b
                        last = nc.tensor.matmul(ps[:, 7, 2 * m:2 * m + 2], rows[0:2, j, b * P:(b + 1) * P],
                                                masks_sb[0:2, MI["ident"], 0:2],
                                                start=True, stop=True)
                last.then_inc(modp_ready, 1)

            pe.wait_ge(masks_in, 16)
            pe.wait_ge(sq_ready, 1)
            for k in range(KD):
                last = nc.tensor.matmul(ps[:, 1, 0:TOK], mask("ones"), v_t[:, k, :], start=(k == 0), stop=(k == KD - 1))
            last.then_inc(stat_ready, 1)
            pe.wait_ge(silu_ready, 1)
            ada_products(0, 0, range(KD))
            ada_columns(0, mod_row)

            for n, (load, c, kind, i) in enumerate(blocks):
                pe.wait_ge(split_ready, n + 1)
                if n >= 3:
                    pe.wait_ge(block_out, n - 2)
                w_hi, w_lo = w_split[:, n % 4, 0, :, :], w_split[:, n % 4, 1, :, :]
                for k in range(KD):
                    if n == 0:
                        pe.wait_ge(h1_ready, k + 1)
                    for x, (w, h) in enumerate(((w_hi, h1_hi), (w_lo, h1_hi), (w_hi, h1_lo))):
                        last = nc.tensor.matmul(ps[:, 2 + n % 3, 0:TOK], w[:, k, :], h[:, k, :],
                                                start=(k == 0 and x == 0), stop=(k == KD - 1 and x == 2))
                last.then_inc(block_mm, 1)
                if n == 9:
                    pe.wait_ge(wab_in, 32)
                    for t in range(TT):
                        for k in range(KD):
                            last = nc.tensor.matmul(ps[:, 5, 64 * t:64 * t + 64], h1_t[:, k, t * P:(t + 1) * P],
                                                    w_ab[:, k, :], start=(k == 0), stop=(k == KD - 1))
                    last.then_inc(tok_mm, 1)

            pe.wait_ge(log_ready, 1)
            for t in range(TT):
                for m, a, b, o in (("upper", 0, 16, 0), ("lower", 16, 32, 16), ("upper64", 32, 40, 32), ("lower64", 40, 48, 40),
                                   ("ones", 0, 32, 48), ("ones64", 32, 48, 80), ("first64", 32, 48, 96), ("last64", 32, 48, 112)):
                    last = nc.tensor.matmul(ps[:, 6, t * P + o:t * P + o + b - a], mask(m), g_log[:, t, a:b], start=True, stop=True)
            last.then_inc(cum_mm, 1)

            for i in range(2 * KD):
                pe.wait_ge(qk_sq, i + 1)
                nc.tensor.matmul(ps[:, i % 2, 0:TOK], mask("ones"), sq[:, i % 2, :], start=True, stop=True).then_inc(qk_sum, 1)
                if 4 <= i < 4 + KD:
                    ada_products(LOAD_ADA1, 5, [i - 4])
            ada_columns(1, mod_row1)

            for t in range(TT):
                if t:
                    pe.wait_ge(xt_ready, t)
                for b in range(KD):
                    nc.tensor.transpose(ps[:, 2 + b // 4, (b % 4) * P:(b % 4 + 1) * P], x_ssd[:, b, t * P:(t + 1) * P], mask("ident"))
                nc.tensor.transpose(ps[:, 4, 0:P], bc[:, 0, t * P:(t + 1) * P], mask("ident")).then_inc(xt_mm, 1)

            pe.wait_ge(xe_ready, 4)
            for d in range(2):
                for b in range(KD):
                    g = b // 4
                    last = nc.tensor.matmul(ps[:, 5 + d, b * 64:(b + 1) * 64], x_end[:, d, b * P:(b + 1) * P],
                                            b_tok[:, 0, 64 * g:64 * g + 64], start=True, stop=True)
                last.then_inc(st_mm, 1)
            for d in range(2):
                for g in range(SSD_GROUPS):
                    last = nc.tensor.matmul(ps[64 * g:64 * g + 64, d, :], b_tok[:, 1 + d, 64 * g:64 * g + 64],
                                            x_end[:, 2 + d, g * 512:(g + 1) * 512], start=True, stop=True, tile_position=(0, 64 * g))
                last.then_inc(st_mm, 1)

            def seg_products(n):
                t, u = SSD_UNITS[n]
                if n == 0:
                    pe.wait_ge(h_ready, 1)
                    pe.wait_ge(st_out, 2)
                if n >= 2:
                    pe.wait_ge(dec_ready, n - 1)
                if u == 0:
                    if t:
                        pe.wait_ge(cb_ready, t)
                    for g in range(2):
                        last = nc.tensor.matmul(ps[:, 6 + g, 0:P], bc[64 * g:64 * g + 64, 0, t * P:(t + 1) * P],
                                                bc[64 * g:64 * g + 64, 1, t * P:(t + 1) * P], start=True, stop=True, tile_position=(64 * g, 0))
                    last.then_inc(cb_mm, 1)
                for d in range(2):
                    for h in range(4):
                        hh = 16 * d + 4 * u + h
                        last = nc.tensor.matmul(ps[:, 2 * (n % 2) + d, h * P:(h + 1) * P],
                                                g_log[:, t, hh:hh + 1].to_broadcast([P, P]), mask(("upper", "lower")[d]),
                                                start=True, stop=True)
                last.then_inc(seg_mm, 1)

            def y_products(n):
                t, u = SSD_UNITS[n]
                g = u // 2
                pe.wait_ge(ssd_m_ready, n + 1)
                if n >= 2:
                    pe.wait_ge(y_ready, n - 1)
                for b in range(2):
                    for d in range(2):
                        for e in range(2):
                            h = 2 * b + e
                            out = ps[64 * e:64 * e + 64, 4 + n % 2, b * P:(b + 1) * P]
                            head = 4 * u + h
                            last = nc.tensor.matmul(out, x_tok[:, t, 64 * head:64 * head + 64], seg[n % 3][:, d, h, :],
                                                    start=(d == 0), stop=(d == 1 and t == 0), tile_position=(0, 64 * e))
                        if t:
                            for e in range(2):
                                h = 2 * b + e
                                out = ps[64 * e:64 * e + 64, 4 + n % 2, b * P:(b + 1) * P]
                                st = 2 * d + (t - 1 if d == 0 else 2 - t)
                                lo = (4 * u + h) % 8
                                last = nc.tensor.matmul(out, h_st[64 * g:64 * g + 64, st, 64 * lo:64 * lo + 64],
                                                        c_dec[64 * g:64 * g + 64, n % 2, d, h, :], start=False, stop=(d == 1),
                                                        tile_position=(64 * g, 64 * e))
                last.then_inc(y_mm, 1)

            for n in range(len(SSD_UNITS) + 2):
                if n < len(SSD_UNITS):
                    seg_products(n)
                if n >= 2:
                    y_products(n - 2)
            pe.wait_ge(sq_ready, 2)
            for k in range(KD):
                last = nc.tensor.matmul(ps[:, 6, 0:TOK], mask("ones"), y_sq[:, k, :], start=(k == 0), stop=(k == KD - 1))
            last.then_inc(stat_ready, 1)

            ada_products(LOAD_ADA2, 5, range(KD))

            for t in range(TT):
                if t:
                    pe.wait_ge(kvt_ready, t)
                for i, src in enumerate((k_t, v_t)):
                    for b in range(KD):
                        last = nc.tensor.transpose(ps[:, 2 * i + b // 4, (b % 4) * P:(b % 4 + 1) * P], src[:, b, t * P:(t + 1) * P], mask("ident"))
                last.then_inc(kvt_mm, 1)
            ada_columns(2, mod_row2)

            def inverse_step(p, n):
                hq, kind, tile = dn_pair(p)
                lev = (n - 1) // 2
                for a in range(2):
                    t = tile[a]
                    tok = slice(t * P, (t + 1) * P)
                    A, B = ps[:, bank_a[a], :], ps[:, bank_b[a], :]
                    off, d, dt, prod = dn_off[a][lev % 2], dn_d[a], dn_dt[a][p % 2], dn_p[a]
                    if n == 0:
                        if p:
                            pe.wait_ge(d_ready[a], 7 * p)
                        for h in range(4):
                            c = 32 + 8 * a + 4 * hq + h
                            last = nc.tensor.matmul(A[:, h * P:(h + 1) * P], g_log[:, t, c:c + 1].to_broadcast([P, P]),
                                                    mask(("upper64", "lower64")[a]), start=True, stop=True)
                        last.then_inc(dseg_mm[a], 1)
                        for h in range(4):
                            last = nc.tensor.matmul(B[:, h * P:(h + 1) * P], k_t[:, 4 * hq + h, tok], k_t[:, 4 * hq + h, tok],
                                                    start=True, stop=True)
                        last.then_inc(dseg_mm[a], 1)
                    elif n == 1:
                        pe.wait_ge(dec_exp[a], 2 * p + 2)
                        for h in range(4):
                            last = nc.tensor.matmul(A[:, h * P:(h + 1) * P], k_t[:, 4 * hq + h, tok], q_t[:, 4 * hq + h, tok],
                                                    start=True, stop=True)
                        last.then_inc(kq_mm[a], 1)
                    elif n == 2 or n % 2:
                        if n == 2:
                            lev, off = 0, dn_off[a][0]
                        if lev == 0:
                            pe.wait_ge(m_ready[a], 2 * p + 2)
                        else:
                            pe.wait_ge(off_ready[a], 5 * p + lev)
                        pe.wait_ge(d_ready[a], 7 * p + lev + 1)
                        for h in range(4):
                            last = nc.tensor.matmul(A[:, h * P:(h + 1) * P], off[:, h, :], mask("ident") if lev == 0 else d[:, h, :],
                                                    start=True, stop=True)
                        last.then_inc(lev_mm1[a], 1)
                    else:
                        lev = (n - 2) // 2
                        pe.wait_ge(lev_p[a], 5 * p + lev)
                        if lev < 5:
                            for h in range(4):
                                nc.tensor.matmul(A[:, h * P:(h + 1) * P], dt[:, h, :], prod[:, h, :], start=True, stop=True)
                        for h in range(4):
                            last = nc.tensor.matmul(B[:, h * P:(h + 1) * P], prod[:, h, :], dt[:, h, :], start=True, stop=True)
                        last.then_inc(lev_mm2[a], 1)

            def chunk_step(p, n):
                hq, kind, tile = dn_pair(p)
                step = n // 3
                for a in range(2):
                    t = tile[a]
                    c, rows = dn_rows(step, a)
                    X, O = ps[:, bank_x[a], :], ps[:, bank_o[a], :]
                    st = dn_s[:, min(kind, 1), a, :]
                    if n in (0, 3):
                        if p or step:
                            pe.wait_ge(s_ready[a], 2 * p + step)
                        if step == 0:
                            if kind == 0:
                                pe.wait_ge(s_zero, hq + 1)
                            elif kind == 1:
                                pe.wait_ge(s0_in, 32 * (hq + 1))
                            pe.wait_ge(d_ready[a], 7 * p + 7)
                            if p:
                                pe.wait_ge(o_out[a], p)
                        for h in range(4):
                            last = nc.tensor.matmul(X[rows, h * P:(h + 1) * P], k_t[:, 4 * hq + h, t * P + 64 * c:t * P + 64 * c + 64],
                                                    st[:, h * P:(h + 1) * P], start=True, stop=True)
                        last.then_inc(ks_mm[a], 1)
                        for h in range(4):
                            nc.tensor.matmul(O[:, h * P + 64 * c:h * P + 64 * c + 64], st[:, h * P:(h + 1) * P], dn_e[a][p % 2][:, h, rows],
                                             start=(step == 0 and h == 0), stop=False, skip_group_check=True)
                    elif n in (1, 4):
                        pe.wait_ge(r_ready[a], 2 * p + step + 1)
                        for h in range(4):
                            last = nc.tensor.matmul(X[rows, h * P:(h + 1) * P], dn_dt[a][p % 2][rows, h, rows], dn_r[a][rows, h, :],
                                                    start=True, stop=True)
                        last.then_inc(vn_mm[a], 1)
                    elif n in (2, 5):
                        pe.wait_ge(vn_ready[a], 2 * p + step + 1)
                        for h in range(4):
                            last = nc.tensor.matmul(X[:, h * P:(h + 1) * P], k_tok[rows, t, (4 * hq + h) * P:(4 * hq + h + 1) * P],
                                                    dn_vb[a][rows, h, :], start=True, stop=True)
                        last.then_inc(ds_mm[a], 1)
                    else:
                        for h in range(4):
                            last = nc.tensor.matmul(O[:, h * P:(h + 1) * P], dn_vo[a][:, h, :], dn_qk[a][p % 2][:, h, :],
                                                    start=False, stop=(h == 3), skip_group_check=True)
                        last.then_inc(o_mm[a], 1)

            pe.wait_ge(kvt_ready, TT)
            dn_rounds(chunk_step, inverse_step)
            for i in range(KD):
                pe.wait_ge(o_sq, i + 1)
                nc.tensor.matmul(ps[:, i % 2, 0:TOK], mask("ones"), o_sq_t[:, i % 2, :], start=True, stop=True).then_inc(o_sum, 1)

            pe.wait_ge(o_ready, KD)
            pe.wait_ge(ynorm_ready, 1)
            for b in range(KD):
                dh = b // 4
                if b % 4 == 0:
                    ready(LOAD_OUT + 2 * dh)
                    ready(LOAD_OUT + 2 * dh + 1)
                if b >= 2:
                    pe.wait_ge(x1_ready, b - 1)
                for k in range(2 * KD):
                    w = slots[slot_of[LOAD_OUT + 2 * dh + k // KD]][:, k % KD, (b % 4) * P:(b % 4 + 1) * P]
                    last = nc.tensor.matmul(ps[:, b % 2, 0:TOK], w, mix[:, k, :], start=(k == 0), stop=(k == 2 * KD - 1))
                last.then_inc(out_mm, 1)
            pe.wait_ge(sq_ready, 3)
            for k in range(KD):
                last = nc.tensor.matmul(ps[:, 2, 0:TOK], mask("ones"), v_t[:, k, :], start=(k == 0), stop=(k == KD - 1))
            last.then_inc(stat_ready, 1)
            pe.wait_ge(h2_ready, 1)
            pe.wait_ge(router_in, 16)
            for t in range(TT):
                for k in range(KD):
                    last = nc.tensor.matmul(ps[:, 7, t * N_ROUTE:(t + 1) * N_ROUTE], h2_t[:, k, t * P:(t + 1) * P], router_sb[:, k, :],
                                            start=(k == 0), stop=(k == KD - 1))
            last.then_inc(lg_mm, 1)
            for t in range(TT):
                if t:
                    pe.wait_ge(h2t_ready, t)
                for b in range(KD):
                    last = nc.tensor.transpose(ps[:, 3 + b // 4, (b % 4) * P:(b % 4 + 1) * P], h2_t[:, b, t * P:(t + 1) * P], mask("ident"))
                last.then_inc(h2t_mm, 1)
            pe.wait_ge(any_ready, 1)
            for t in range(TT + 1):
                for u in range(min(t + 1, TT)):
                    last = nc.tensor.matmul(ps[:, 7, t * N_EXPERTS:(t + 1) * N_EXPERTS], mask("strict_up" if u == t else "ones"), any_e[:, u, :],
                                            start=(u == 0), stop=(u == min(t, TT - 1)))
            last.then_inc(rank_mm, 1)
            pe.wait_ge(sel_ready, 1)
            for j in range(NPAIR):
                for t in range(TT):
                    last = nc.tensor.matmul(ps[:, 0, 3 * j:3 * j + 3], sel[:, t, 2 * j:2 * j + 2, :].rearrange("p e c -> p (e c)"),
                                            tg[:, t, 3 * j:3 * j + 3], start=(t == 0), stop=(t == TT - 1))
            last.then_inc(info_mm, 1)

            for t in range(TT):
                if t:
                    pe.wait_ge(x1t_ready, t)
                for b in range(KD):
                    last = nc.tensor.transpose(ps[:, 5 + b // 4, (b % 4) * P:(b % 4 + 1) * P], x1_t[:, b, t * P:(t + 1) * P], mask("ident"))
                last.then_inc(x1t_mm, 1)
            pe.wait_ge(slots_ready, 1)
            pe.wait_ge(x1t_ready, TT)
            for i in range(3):
                for k in range(KD):
                    src = mod[:, 5 * KD + k, i:i + 1] if i < 2 else col("final", k)
                    last = nc.tensor.matmul(ps[:, 2 * i + k // 4, (k % 4) * P:(k % 4 + 1) * P], src.to_broadcast([P, P]), mask("ident"),
                                            start=True, stop=True)
            last.then_inc(rows_mm, 1)
            def turn_rows(i):
                pe.wait_ge(xg_in, i * 16 + 16)
                for b in range(KD):
                    last = nc.tensor.transpose(ps[:, b // 4, (b % 4) * P:(b % 4 + 1) * P], xg[:, b * P:(b + 1) * P], mask("ident"))
                last.then_inc(xgt_mm, 1)

            def expert_pair(i, more):
                pe.wait_ge(xgt_ready, i * 2 + 2)
                for n, done_sem in ((0, gate_mm), (1, up_mm)):
                    for e in range(2):
                        pe.wait_ge(slot_in[2 * n + e], i * 16 + 16 * (n_loads[2 * n + e] + 1))
                    for k in range(KD):
                        for e in range(2):
                            last = nc.tensor.matmul(ps[64 * e:64 * e + 64, 2 + n, :], xg_t[:, k, 64 * e:64 * e + 64], slots[2 * n + e][:, k, :],
                                                    start=(k == 0), stop=(k == KD - 1), tile_position=(0, 64 * e))
                    last.then_inc(done_sem, 1)
                if more:
                    turn_rows(i + 1)
                pe.wait_ge(hact_ready, i + 1)
                for f in range(FK):
                    last = nc.tensor.transpose(ps[:, 4, f * P:(f + 1) * P], e_act[:, f * P:(f + 1) * P], mask("ident"))
                last.then_inc(at_mm, 1)
                pe.wait_ge(at_ready, i + 1)
                for e in range(2):
                    pe.wait_ge(slot_in[4 + e], i * 16 + 16 * (n_loads[4 + e] + 1))
                for n in range(2):
                    for f in range(FK):
                        for e in range(2):
                            last = nc.tensor.matmul(ps[64 * e:64 * e + 64, 5 + n, :], e_act_t[:, f, 64 * e:64 * e + 64],
                                                    down[4 + e][:, f, n * 512:(n + 1) * 512], start=(f == 0), stop=(f == FK - 1),
                                                    tile_position=(0, 64 * e))
                last.then_inc(down_mm, 1)
                pe.wait_ge(y_half, i * 2 + 2)
                for m in range(2 * TT):
                    t, n = m // 2, m % 2
                    pe.wait_ge(acc_added, i * 6 + m + 1)
                    nc.tensor.matmul(ps[:, (7, 4)[n], :], sel_t[:, t * P:(t + 1) * P], e_y[:, n * 512:(n + 1) * 512],
                                     start=True, stop=True).then_inc(spread_mm, 1)

            pe.wait_ge(rows_ready, 1)
            turn_rows(0)
            with pe.Fori(0, NPAIR - 1) as i:
                expert_pair(i, True)
            expert_pair(NPAIR - 1, False)

            with pe.If(more_than_cap(pe)):
                with pe.Fori(0, N_EXPERTS) as e:
                    for t in range(TT):
                        if t == 0:
                            pe.wait_ge(rest_in[0], e * 16 + 16)
                            pe.wait_ge(rest_in[1], e * 16 + 16)
                        for n in range(2):
                            for k in range(KD):
                                last = nc.tensor.matmul(ps[:, n, :], h2_t[:, k, t * P:(t + 1) * P], slots[n][:, k, :], start=(k == 0), stop=(k == KD - 1))
                        last.then_inc(rest_up_mm, 1)
                        pe.wait_ge(rest_act, e * TT + t + 1)
                        for f in range(FK):
                            last = nc.tensor.transpose(ps[:, 2, f * P:(f + 1) * P], e_act[:, f * P:(f + 1) * P], mask("ident"))
                        last.then_inc(rest_at_mm, 1)
                        if t == 0:
                            pe.wait_ge(rest_in[2], e * 16 + 16)
                        pe.wait_ge(rest_at, e * TT + t + 1)
                        pe.wait_ge(rest_added, e * TT + t + 1)
                        for n in range(2):
                            for f in range(FK):
                                last = nc.tensor.matmul(ps[:, 3 + n, :], e_act_t[:, f, :], down[2][:, f, n * 512:(n + 1) * 512],
                                                        start=(f == 0), stop=(f == FK - 1))
                        last.then_inc(rest_down_mm, 1)

        @block.scalar
        def _(act):
            steps = [0]

            def link(ins):
                steps[0] += 1
                ins.then_inc(act_step, 1)
                act.wait_ge(act_step, steps[0])

            def rsqrt(out, in_, scale, tmp):
                link(nc.scalar.activation(tmp, in_, ACT.Ln, bias=eps_col, scale=scale))
                return nc.scalar.activation(out, tmp, ACT.Exp, scale=-0.5)

            def ada_rows(g, bank, rows):
                act.wait_ge(ada_mm, g + 1)
                for j in range(4):
                    last = nc.scalar.copy(rows[0:2, j, :], ps[32 * j:32 * j + 2, bank, :])
                last.then_inc(row_ready, 1)

            act.wait_ge(pc_in, 16)
            nc.scalar.activation(silu_c[:, :], cols("c"), ACT.Silu).then_inc(silu_ready, 1)
            act.wait_ge(x_ready, 1)
            eps_col = masks_sb[:, MI["eps"], 0:1]
            nc.scalar.activation(v_t[:, :, :], x0_t[:, :, :], ACT.Square).then_inc(sq_ready, 1)
            act.wait_ge(stat_ready, 1)
            rsqrt(rs1, ps[:, 1, 0:TOK], 1.0 / D_MODEL, rs1).then_inc(rs_ready, 1)
            ada_rows(0, 0, mod_row)

            def hi_part(n):
                load, c = blocks[n][:2]
                if c == 0:
                    act.wait_ge(slot_in[slot_of[load]], 16 * arrivals(load))
                nc.scalar.copy(w_split[:, n % 4, 0, :, :], slots[slot_of[load]][:, :, c:c + P]).then_inc(hi_ready, 1)

            AHEAD = 3
            for n in range(AHEAD):
                hi_part(n)
            for k in range(KD):
                act.wait_ge(h1_full, k + 1)
                nc.scalar.copy(h1_hi[:, k, :], h1_t[:, k, :]).then_inc(h1_hi_ready, 1)

            def conv_silu(i):
                act.wait_ge(conv_done, i + 1)
                dest = conv_dest(i)
                if i == 10 + 2 * KD:
                    act.wait_ge(tok_mm, 1)
                nc.scalar.activation(dest[:, 0:SEQ], conv_acc[:, i % 2, 0:SEQ], ACT.Silu)
                nc.scalar.activation(dest[:, SEQ:TOK], conv_acc[:, i % 2, SEQ + 4:TOK + 4], ACT.Silu).then_inc(conv_out, 1)

            for n, (load, c, kind, i) in enumerate(blocks):
                act.wait_ge(block_mm, n + 1)
                if n + AHEAD < NB:
                    hi_part(n + AHEAD)
                bank = 2 + n % 3
                if kind == "conv":
                    if i >= 2:
                        act.wait_ge(conv_done, i - 1)
                    nc.scalar.copy(pad[:, i % 2, 2:2 + SEQ], ps[:, bank, 0:SEQ])
                    nc.scalar.copy(pad[:, i % 2, SEQ + 6:TOK + 6], ps[:, bank, SEQ:TOK]).then_inc(block_out, 1)
                    if i:
                        conv_silu(i - 1)
                else:
                    if i == 0:
                        conv_silu(CONV_BLOCKS - 1)
                    nc.scalar.activation(mix[:, i, :], ps[:, bank, 0:TOK], ACT.Silu).then_inc(block_out, 1)

            act.wait_ge(na_ready, 1)
            nc.scalar.preload_act_table_set("natural_log_exp_and_others")
            nc.scalar.activation(sg[:, 2, :, :], sg[:, 1, :, :], ACT.Exp)
            nc.scalar.activation(g_beta, ps[:, 5, 0:192].rearrange("p (t c) -> p t c", t=TT)[:, :, 48:64], ACT.Exp, scale=-1.0)
            link(nc.scalar.activation(sg[:, 4, 0, :], cols("a_log"), ACT.Exp))
            nc.scalar.activation(sg[:, 3, :, :], sg[:, 2, :, :], ACT.Ln, bias=1.0).then_inc(ln_ready, 1)
            act.wait_ge(cum_ready, 1)
            nc.scalar.activation(sg[:, 0, :, :], sg[:, 1, :, :], ACT.Exp)
            nc.scalar.activation(g_nec, cums[:, :, 32:48], ACT.Exp)
            nc.scalar.activation(g_tot, cums[:, :, 48:128], ACT.Exp).then_inc(exps_ready, 1)

            for i in range(2 * KD):
                src = (q_t, k_t)[i // KD][:, i % KD, :]
                if i >= 2:
                    act.wait_ge(qk_sum, i - 1)
                nc.scalar.activation(sq[:, i % 2, :], src, ACT.Square).then_inc(qk_sq, 1)
                if i:
                    def norm(i):
                        act.wait_ge(qk_sum, i + 1)
                        if i >= 2:
                            act.wait_ge(qk_ready, i - 1)
                        rsqrt(rs[:, i % 2, :], ps[:, i % 2, 0:TOK], 1.0, rs[:, i % 2, :]).then_inc(qk_rs, 1)
                    norm(i - 1)
                if i == 6 + KD:
                    ada_rows(1, 5, mod_row1)
            norm(2 * KD - 1)

            for t in range(TT):
                act.wait_ge(xt_mm, t + 1)
                nc.scalar.copy(x_tok[:, t, 0:512], ps[:, 2, :])
                nc.scalar.copy(x_tok[:, t, 512:1024], ps[:, 3, :])
                nc.scalar.copy(b_tok[:, t, :], ps[:, 4, 0:P]).then_inc(xt_ready, 1)
            for d in range(2):
                act.wait_ge(st_mm, d + 1)
                nc.scalar.copy(st_stage[:, d, :, :], ps[:, 5 + d, :].rearrange("p (b n) -> p b n", b=KD)).then_inc(st_out, 1)

            for n, (t, u) in enumerate(SSD_UNITS):
                g = u // 2
                act.wait_ge(seg_ready, n + 1)
                if t:
                    if n >= 2:
                        act.wait_ge(y_mm, n - 1)
                    for d in range(2):
                        nc.scalar.activation(c_dec[64 * g:64 * g + 64, n % 2, d, :, :],
                                             ps[64 * g:64 * g + 64, 2 * (n % 2) + d, :].rearrange("p (h i) -> p h i", h=4), ACT.Exp)
                nc.scalar.activation(seg[n % 3], seg[n % 3], ACT.Exp).then_inc(dec_ready, 1)
            act.wait_ge(y_ready, len(SSD_UNITS))
            nc.scalar.activation(y_sq, mix[:, 0:KD, :], ACT.Square).then_inc(sq_ready, 1)
            act.wait_ge(stat_ready, 2)
            rsqrt(y_rs, ps[:, 6, 0:TOK], 1.0 / SSD_WIDTH, y_rs).then_inc(rs_ready, 1)

            ada_rows(2, 5, mod_row2)
            for t in range(TT):
                act.wait_ge(kvt_mm, t + 1)
                for i, dst in enumerate((k_tok, v_tok)):
                    for b in range(2):
                        last = nc.scalar.copy(dst[:, t, b * 512:(b + 1) * 512], ps[:, 2 * i + b, :])
                last.then_inc(kvt_ready, 1)

            def inverse_step(p, n):
                for a in range(2):
                    A = ps[:, bank_a[a], :].rearrange("p (h i) -> p h i", h=4)
                    if n == 0:
                        act.wait_ge(dseg_ready[a], p + 1)
                        nc.scalar.activation(dn_m[a], dn_m[a], ACT.Exp).then_inc(dec_exp[a], 1)
                        if p >= 2:
                            act.wait_ge(o_mm[a], p - 1)
                        nc.scalar.activation(dn_e[a][p % 2], A, ACT.Exp).then_inc(dec_exp[a], 1)
                    elif n >= 3 and n % 2:
                        act.wait_ge(lev_mm1[a], 6 * p + (n - 1) // 2 + 1)
                        nc.scalar.copy(dn_p[a], A).then_inc(lev_p[a], 1)

            def chunk_step(p, n):
                hq, kind, tile = dn_pair(p)
                for a in range(2):
                    if n == 6 and not LAST_DIR_ADDS[kind][a]:
                        act.wait_ge(o_mm[a], p + 1)
                        nc.scalar.copy(o_t[:, 4 * hq:4 * hq + 4, tile[a] * P:(tile[a] + 1) * P],
                                       ps[:, bank_o[a], :].rearrange("p (h i) -> p h i", h=4)).then_inc(o_out[a], 1)

            dn_rounds(chunk_step, inverse_step)
            for i in range(KD):
                if i == 0:
                    for a in range(2):
                        act.wait_ge(o_out[a], len(PAIRS))
                if i >= 2:
                    act.wait_ge(o_sum, i - 1)
                nc.scalar.activation(o_sq_t[:, i % 2, :], o_t[:, i, :], ACT.Square).then_inc(o_sq, 1)
                if i:
                    def o_norm(i):
                        act.wait_ge(o_sum, i + 1)
                        if i >= 2:
                            act.wait_ge(o_ready, i - 1)
                        rsqrt(o_rs_t[:, i % 2, :], ps[:, i % 2, 0:TOK], 1.0 / DN_HEAD_DIM, o_rs_t[:, i % 2, :]).then_inc(o_rs, 1)
                    o_norm(i - 1)
            o_norm(KD - 1)

            act.wait_ge(x1_ready, KD)
            act.wait_ge(o_ready, KD)
            nc.scalar.activation(v_t[:, :, :], x1_t[:, :, :], ACT.Square).then_inc(sq_ready, 1)
            act.wait_ge(stat_ready, 3)
            rsqrt(rs2, ps[:, 2, 0:TOK], 1.0 / D_MODEL, rs2).then_inc(rs_ready, 1)
            for t in range(TT):
                act.wait_ge(h2t_mm, t + 1)
                nc.scalar.copy(h2_tok[:, t, 0:512], ps[:, 3, :])
                nc.scalar.copy(h2_tok[:, t, 512:1024], ps[:, 4, :]).then_inc(h2t_ready, 1)
            act.wait_ge(gd_ready, 1)
            nc.scalar.activation(g_exp, g_exp, ACT.Exp).then_inc(gexp_ready, 1)
            act.wait_ge(ed_ready, 1)
            nc.scalar.activation(e_p2, e_p2, ACT.Exp).then_inc(eexp_ready, 1)
            for t in range(TT):
                act.wait_ge(x1t_mm, t + 1)
                nc.scalar.copy(x1_tok[:, t, 0:512], ps[:, 5, :])
                nc.scalar.copy(x1_tok[:, t, 512:1024], ps[:, 6, :]).then_inc(x1t_ready, 1)
            act.wait_ge(rows_mm, 1)
            for i in range(3):
                for n in range(2):
                    dst = gt2_row[:, i, n * 512:(n + 1) * 512] if i < 2 else final_row[:, n * 512:(n + 1) * 512]
                    last = nc.scalar.copy(dst, ps[:, 2 * i + n, :])
            last.then_inc(rows_ready, 1)
            def turned_half(i):
                act.wait_ge(xgt_mm, i + 1)
                nc.scalar.copy(xg_t[:, 4:8, :], ps[:, 1, :].rearrange("p (k i) -> p k i", k=4)).then_inc(xgt_ready, 1)

            def expert_pair(i, more):
                act.wait_ge(gate_mm, i + 1)
                nc.scalar.activation(e_silu, ps[:, 2, :], ACT.Silu).then_inc(silu_done, 1)
                if more:
                    turned_half(i + 1)
                act.wait_ge(at_mm, i + 1)
                nc.scalar.copy(e_act_t, ps[:, 4, :].rearrange("p (f i) -> p f i", f=FK)).then_inc(at_ready, 1)
                act.wait_ge(down_mm, i + 1)
                nc.scalar.copy(e_y[:, 512:1024], ps[:, 6, :]).then_inc(y_half, 1)

            turned_half(0)
            with act.Fori(0, NPAIR - 1) as i:
                expert_pair(i, True)
            expert_pair(NPAIR - 1, False)
            with act.If(more_than_cap(act)):
                with act.Fori(0, N_EXPERTS) as e:
                    for t in range(TT):
                        act.wait_ge(rest_up_mm, e * TT + t + 1)
                        nc.scalar.activation(e_silu, ps[:, 0, :], ACT.Silu).then_inc(rest_silu, 1)
                        act.wait_ge(rest_at_mm, e * TT + t + 1)
                        nc.scalar.copy(e_act_t, ps[:, 2, :].rearrange("p (f i) -> p f i", f=FK)).then_inc(rest_at, 1)
            for t in range(TT):
                act.wait_ge(x2_ready, t + 1)
                link(nc.scalar.activation(x2_sq, y_acc[:, t, :], ACT.Square, accum_out=ss[:, t:t + 1]))
                rsqrt(ss[:, 4 + t:5 + t], ss[:, t:t + 1], 1.0 / D_MODEL, ss[:, t:t + 1]).then_inc(x2_rs, 1)

        @block.vector
        def _(dve):
            steps = [0]

            def link(ins):
                steps[0] += 1
                ins.then_inc(dve_step, 1)
                dve.wait_ge(dve_step, steps[0])

            V = nc.vector
            link(V.memset(pad, 0.0))
            dve.wait_ge(x_in, 48)
            V.tensor_tensor(x0_t[:, :, SEQ:TOK], x0_t[:, :, SEQ:TOK], k_t[:, :, 0:DEC_SEQ], ALU.add).then_inc(x_ready, 1)
            dve.wait_ge(pc_in, 16)
            dve.wait_ge(rs_ready, 1)
            link(V.tensor_tensor(h1_t, x0_t[:, :, :], rs1.unsqueeze(1).to_broadcast([P, KD, TOK]), ALU.mult))

            def mod_columns(g):
                dve.wait_ge(modp_ready, g + 1)
                b_ada = cols("b_ada")[:, 16 * g:16 * g + 16].unsqueeze(2).to_broadcast([P, 16, 2])
                return V.tensor_tensor(mod[:, 16 * g:16 * g + 16, :], ps[:, 7, 32 * g:32 * g + 32].rearrange("p (m c) -> p m c", c=2), b_ada, ALU.add)

            mod_columns(0).then_inc(mod_ready, 1)
            dve.wait_ge(mod_ready, 1)
            link(V.scalar_tensor_tensor(amp1[:, :, :], mod[:, KD:2 * KD, :], 1.0, cols("norm1").unsqueeze(2).to_broadcast([P, KD, 2]), ALU.add, ALU.mult))
            for k in range(KD):
                for c, (a, b) in enumerate(SEGS):
                    last = V.tensor_scalar(h1_t[:, k, a:b], h1_t[:, k, a:b], amp1[:, k, c:c + 1], mod[:, k, c:c + 1], ALU.mult, ALU.add)
                last.then_inc(h1_full, 1)
            for k in range(KD):
                dve.wait_ge(h1_hi_ready, k + 1)
                V.tensor_tensor(h1_lo[:, k, :], h1_t[:, k, :], h1_hi[:, k, :].bitcast(fp32), ALU.subtract).then_inc(h1_ready, 1)

            W5 = TOK + 4
            for i in range(CONV_BLOCKS):
                dve.wait_ge(block_out, i + 1)
                if i >= 2:
                    dve.wait_ge(conv_out, i - 1)
                c_acc, row = conv_acc[:, i % 2, :], pad[:, i % 2, :]
                link(V.tensor_scalar(c_acc, row[:, 0:W5], col("conv_w", CONV_W * i), col("conv_b", i), ALU.mult, ALU.add))
                for j in range(1, CONV_W):
                    ins = V.scalar_tensor_tensor(c_acc, row[:, j:j + W5], col("conv_w", CONV_W * i + j), c_acc, ALU.mult, ALU.add)
                    if j < CONV_W - 1:
                        link(ins)
                ins.then_inc(conv_done, 1)

            dve.wait_ge(tok_mm, 1)
            dve.wait_ge(conv_out, CONV_BLOCKS)
            gp = ps[:, 5, 0:192].rearrange("p (t c) -> p t c", t=TT)
            link(V.tensor_tensor(sg[:, 0, :, :], gp[:, :, 0:48], cols("gate_bias").unsqueeze(1).to_broadcast([P, TT, 48]), ALU.add))
            V.scalar_tensor_tensor(sg[:, 1, :, :], sg[:, 0, :, :], -1.0, sg[:, 0, :, :], ALU.mult, ALU.min).then_inc(na_ready, 1)
            dve.wait_ge(ln_ready, 1)
            link(V.scalar_tensor_tensor(sg[:, 5, :, :], sg[:, 0, :, :], 0.0, sg[:, 3, :, :], ALU.max, ALU.add))
            V.tensor_copy(g_dt, sg[:, 5, :, 0:32])
            link(V.tensor_scalar(g_beta, g_beta, 1.0, None, ALU.add))
            link(V.reciprocal(g_beta, g_beta))
            V.scalar_tensor_tensor(g_log, sg[:, 5, :, :], -1.0, sg[:, 4, 0:1, :].to_broadcast([P, TT, 48]), ALU.mult, ALU.mult).then_inc(log_ready, 1)
            dve.wait_ge(cum_mm, 1)
            link(V.tensor_copy(cums[:, :, :], ps[:, 6, 0:TT * P].rearrange("p (t c) -> p t c", t=TT)))
            V.tensor_tensor(sg[:, 1, :, :], cums[:, :, 48:96], cums[:, :, 0:48], ALU.subtract).then_inc(cum_ready, 1)
            dve.wait_ge(exps_ready, 1)
            V.tensor_tensor(g_dte, g_dt, sg[:, 0, :, 0:32], ALU.mult)
            V.tensor_tensor(g_be, g_beta, sg[:, 0, :, 32:48], ALU.mult)
            link(V.tensor_scalar(g_nec, g_nec, -1.0, None, ALU.mult))

            for i in range(2 * KD):
                dve.wait_ge(qk_rs, i + 1)
                x = (q_t, k_t)[i // KD][:, i % KD, :]
                V.scalar_tensor_tensor(x, x, (DN_HEAD_DIM ** -0.5, 1.0)[i // KD], rs[:, i % 2, :], ALU.mult, ALU.mult).then_inc(qk_ready, 1)
            mod_columns(1).then_inc(mod_ready, 1)

            for n, (t, d) in enumerate(ENDS):
                dve.wait_ge(xt_ready, t + 1)
                if n == 0:
                    dve.wait_ge(qk_ready, 2 * KD)
                V.tensor_tensor(x_end[:, n, :].rearrange("p (h c) -> p h c", c=64), x_tok[:, t, :].rearrange("p (h c) -> p h c", c=64),
                                g_dte[:, t, 16 * d:16 * d + 16].unsqueeze(2).to_broadcast([P, 16, 64]), ALU.mult).then_inc(xe_ready, 1)
            dve.wait_ge(h0_in, 32)
            for d in range(2):
                for g in range(2):
                    sl = slice(64 * g, 64 * g + 64)
                    last = V.tensor_tensor(h_st[sl, 2 * d + 1, :].rearrange("p (h c) -> p h c", c=64), h_st[sl, 2 * d, :].rearrange("p (h c) -> p h c", c=64),
                                           g_tot[sl, 1 + d, 16 * d + 8 * g:16 * d + 8 * g + 8].unsqueeze(2).to_broadcast([64, 8, 64]), ALU.mult)
                link(last)
                dve.wait_ge(st_mm, 3 + d)
                last = V.tensor_tensor(h_st[:, 2 * d + 1, :], h_st[:, 2 * d + 1, :], ps[:, d, :], ALU.add)
            last.then_inc(h_ready, 1)

            def seg_part(n):
                t, u = SSD_UNITS[n]
                dve.wait_ge(seg_mm, n + 1)
                if n >= 3:
                    dve.wait_ge(y_mm, n - 2)
                for d in range(2):
                    for h in range(4):
                        hh = 16 * d + 4 * u + h
                        last = V.tensor_scalar(seg[n % 3][:, d, h, :], ps[:, 2 * (n % 2) + d, h * P:(h + 1) * P], cums[:, t, hh:hh + 1], 0.0,
                                               ALU.subtract, ALU.min)
                last.then_inc(seg_ready, 1)

            def m_part(n):
                t, u = SSD_UNITS[n]
                g = u // 2
                if u == 0:
                    dve.wait_ge(cb_mm, t + 1)
                    for d in range(2):
                        last = V.tensor_tensor(cbm[:, d, :, :], ps[:, 6:8, 0:P],
                                               mask(("upper", "lower")[d]).unsqueeze(1).to_broadcast([P, 2, P]), ALU.mult)
                    last.then_inc(cb_ready, 1)
                    dve.wait_ge(cb_ready, t + 1)
                dve.wait_ge(dec_ready, n + 1)
                for d in range(2):
                    for h in range(4):
                        hh = 16 * d + 4 * u + h
                        last = V.scalar_tensor_tensor(seg[n % 3][:, d, h, :], seg[n % 3][:, d, h, :], g_dt[:, t, hh:hh + 1], cbm[:, d, g, :],
                                                      ALU.mult, ALU.mult)
                    if t:
                        sl = slice(64 * g, 64 * g + 64)
                        last = V.tensor_tensor(c_dec[sl, n % 2, d, :, :], c_dec[sl, n % 2, d, :, :],
                                               bc[sl, 1, t * P:(t + 1) * P].unsqueeze(1).to_broadcast([64, 4, P]), ALU.mult)
                last.then_inc(ssd_m_ready, 1)

            def y_out(n):
                t, u = SSD_UNITS[n]
                dve.wait_ge(y_mm, n + 1)
                if n >= 2:
                    dve.wait_ge(y_ready, n - 1)
                for b in range(2):
                    last = V.scalar_tensor_tensor(y_tmp[:, n % 2, b, :], x_ssd[:, 2 * u + b, t * P:(t + 1) * P], col("ssd_d", 2 * u + b),
                                                  ps[:, 4 + n % 2, b * P:(b + 1) * P], ALU.mult, ALU.add)
                link(last)
                V.tensor_tensor(mix[:, 2 * u:2 * u + 2, t * P:(t + 1) * P], mix[:, 2 * u:2 * u + 2, t * P:(t + 1) * P], y_tmp[:, n % 2, :, :],
                                ALU.mult).then_inc(y_ready, 1)

            seg_part(0)
            for n in range(len(SSD_UNITS)):
                if n + 1 < len(SSD_UNITS):
                    seg_part(n + 1)
                m_part(n)
                if n:
                    y_out(n - 1)
            y_out(len(SSD_UNITS) - 1)
            dve.wait_ge(rs_ready, 2)
            for k in range(KD):
                last = V.scalar_tensor_tensor(mix[:, k, :], mix[:, k, :], col("ssd_norm", k), y_rs, ALU.mult, ALU.mult)
            last.then_inc(ynorm_ready, 1)

            def zero_states():
                V.memset(dn_s[:, 0, :, :], 0.0).then_inc(s_zero, 1)

            mod_columns(2).then_inc(mod_ready, 1)
            dve.wait_ge(states_out, 32)
            zero_states()
            ident4 = mask("ident").unsqueeze(1).to_broadcast([P, 4, P])
            heads = lambda bank: ps[:, bank, :].rearrange("p (h i) -> p h i", h=4)

            def inverse_step(p, n):
                hq, kind, tile = dn_pair(p)
                if n == 0:
                    for a in range(2):
                        dve.wait_ge(dseg_mm[a], 2 * p + 1)
                        if p:
                            dve.wait_ge(off_ready[a], 5 * p)
                        for h in range(4):
                            c = 32 + 8 * a + 4 * hq + h
                            last = V.tensor_scalar(dn_m[a][:, h, :], ps[:, bank_a[a], h * P:(h + 1) * P], cums[:, tile[a], c:c + 1], 0.0,
                                                   ALU.subtract, ALU.min)
                        last.then_inc(dseg_ready[a], 1)
                    for a in range(2):
                        dve.wait_ge(dec_exp[a], 2 * p + 1)
                        if p >= 2:
                            dve.wait_ge(o_mm[a], p - 1)
                        link(V.tensor_tensor(dn_qk[a][p % 2], dn_m[a], mask(("upper64", "lower64")[a]).unsqueeze(1).to_broadcast([P, 4, P]), ALU.mult))
                        dve.wait_ge(dseg_mm[a], 2 * p + 2)
                        for h in range(4):
                            b = 8 * a + 4 * hq + h
                            last = V.scalar_tensor_tensor(dn_m[a][:, h, :], ps[:, bank_b[a], h * P:(h + 1) * P], g_beta[:, tile[a], b:b + 1],
                                                          dn_qk[a][p % 2][:, h, :], ALU.mult, ALU.mult)
                        last.then_inc(m_ready[a], 1)
                        dve.wait_ge(m_ready[a], 2 * p + 1)
                        V.tensor_tensor(dn_off[a][0], dn_m[a], mask(f"lev{a}_1").unsqueeze(1).to_broadcast([P, 4, P]), ALU.mult).then_inc(m_ready[a], 1)
                elif n == 1:
                    for a in range(2):
                        dve.wait_ge(kq_mm[a], p + 1)
                        V.tensor_tensor(dn_qk[a][p % 2], dn_qk[a][p % 2], heads(bank_a[a]), ALU.mult).then_inc(d_ready[a], 1)
                elif n == 2:
                    for a in range(2):
                        dve.wait_ge(m_ready[a], 2 * p + 2)
                        V.tensor_tensor(dn_dt[a][p % 2], ident4, dn_off[a][0], ALU.subtract)
                        dve.wait_ge(lev_mm1[a], 6 * p + 1)
                        V.tensor_tensor(dn_d[a], ident4, heads(bank_a[a]), ALU.subtract).then_inc(d_ready[a], 1)
                    for a in range(2):
                        dve.wait_ge(dec_exp[a], 2 * p + 2)
                        V.tensor_tensor(dn_e[a][p % 2], dn_e[a][p % 2], q_t[:, 4 * hq:4 * hq + 4, tile[a] * P:(tile[a] + 1) * P], ALU.mult)
                elif n % 2 == 0:
                    lev = (n - 2) // 2
                    for a in range(2):
                        dve.wait_ge(lev_mm2[a], 5 * p + lev)
                        if lev < 5:
                            V.tensor_tensor(dn_d[a], dn_d[a], heads(bank_a[a]), ALU.subtract)
                        V.tensor_tensor(dn_dt[a][p % 2], dn_dt[a][p % 2], heads(bank_b[a]), ALU.subtract).then_inc(d_ready[a], 1)

            def chunk_step(p, n):
                hq, kind, tile = dn_pair(p)
                step = n // 3
                if p == 3 and n == 0:
                    dve.wait_ge(states_out, 64)
                    zero_states()
                for a in range(2):
                    t = tile[a]
                    c, rows = dn_rows(step, a)
                    b = 8 * a + 4 * hq
                    X = ps[:, bank_x[a], :]
                    if n in (0, 3):
                        dve.wait_ge(ks_mm[a], 2 * p + step + 1)
                        for h in range(4):
                            last = V.scalar_tensor_tensor(dn_r[a][rows, h, :], X[rows, h * P:(h + 1) * P], g_nec[rows, t, b + h:b + h + 1],
                                                          v_tok[rows, t, (4 * hq + h) * P:(4 * hq + h + 1) * P], ALU.mult, ALU.add)
                        last.then_inc(r_ready[a], 1)
                    elif n in (1, 4):
                        dve.wait_ge(vn_mm[a], 2 * p + step + 1)
                        if p:
                            dve.wait_ge(o_mm[a], p)
                        v = heads(bank_x[a])[rows, :, :]
                        V.tensor_tensor(dn_vb[a][rows, :, :], v, g_be[rows, t, b:b + 4].unsqueeze(2).to_broadcast([64, 4, P]), ALU.mult)
                        V.tensor_tensor(dn_vo[a][rows, :, :], v, g_beta[rows, t, b:b + 4].unsqueeze(2).to_broadcast([64, 4, P]), ALU.mult).then_inc(vn_ready[a], 1)
                    elif n in (2, 5):
                        dve.wait_ge(ds_mm[a], 2 * p + step + 1)
                        st = dn_s[:, min(kind, 1), a, :]
                        for h in range(4):
                            cd = 48 + 16 * c + b + h
                            last = V.scalar_tensor_tensor(st[:, h * P:(h + 1) * P], st[:, h * P:(h + 1) * P], g_tot[:, t, cd:cd + 1],
                                                          X[:, h * P:(h + 1) * P], ALU.mult, ALU.add)
                        last.then_inc(s_ready[a], 1)
                    elif n == 6 and LAST_DIR_ADDS[kind][a]:
                        dve.wait_ge(o_mm[a], p + 1)
                        dve.wait_ge(o_out[0], p + 1 if kind == 0 else p)
                        dve.wait_ge(o_out[1], p)
                        o = o_t[:, 4 * hq:4 * hq + 4, t * P:(t + 1) * P]
                        V.tensor_tensor(o, o, heads(bank_o[a]), ALU.add).then_inc(o_out[a], 1)

            dn_rounds(chunk_step, inverse_step)
            for i in range(KD):
                dve.wait_ge(o_rs, i + 1)
                link(V.scalar_tensor_tensor(o_t[:, i, :], o_t[:, i, :], col("dn_norm"), o_rs_t[:, i % 2, :], ALU.mult, ALU.mult))
                V.tensor_tensor(mix[:, KD + i, :], mix[:, KD + i, :], o_t[:, i, :], ALU.mult).then_inc(o_ready, 1)
            dve.wait_ge(x_in, 96)
            V.tensor_tensor(x0_t[:, :, SEQ:TOK], x0_t[:, :, SEQ:TOK], k_t[:, :, 0:DEC_SEQ], ALU.add).then_inc(x_ready, 1)
            dve.wait_ge(x_ready, 2)
            for b in range(KD):
                dve.wait_ge(out_mm, b + 1)
                for c, (lo, hi) in enumerate(SEGS):
                    last = V.scalar_tensor_tensor(x1_t[:, b, lo:hi], ps[:, b % 2, lo:hi], mod[:, 2 * KD + b, c:c + 1], x0_t[:, b, lo:hi], ALU.mult, ALU.add)
                last.then_inc(x1_ready, 1)
            V.scalar_tensor_tensor(amp2[:, :, :], mod[:, 4 * KD:5 * KD, :], 1.0, cols("norm2").unsqueeze(2).to_broadcast([P, KD, 2]), ALU.add, ALU.mult)
            dve.wait_ge(x1_ready, KD)
            dve.wait_ge(rs_ready, 3)
            link(V.tensor_tensor(h2_t, x1_t[:, :, :], rs2.unsqueeze(1).to_broadcast([P, KD, TOK]), ALU.mult))
            for c, (lo, hi) in enumerate(SEGS):
                for k in range(KD):
                    last = V.tensor_scalar(h2_t[:, k, lo:hi], h2_t[:, k, lo:hi], amp2[:, k, c:c + 1], mod[:, 3 * KD + k, c:c + 1], ALU.mult, ALU.add)
            last.then_inc(h2_ready, 1)
            AX = mybir.AxisListType.X
            desc8 = cols("desc8")
            wide = lambda v, n: v.to_broadcast([P, TT, n])

            def pick_first(out, values, top, n):
                d = desc8[:, 0:n].unsqueeze(1).to_broadcast([P, TT, n])
                link(V.tensor_tensor(e_eq[:, :, 0:n], values, wide(top, n), ALU.is_equal))
                link(V.tensor_tensor(e_eq[:, :, 0:n], e_eq[:, :, 0:n], d, ALU.mult))
                link(V.tensor_reduce(e_pick, e_eq[:, :, 0:n], AX, ALU.max))
                link(V.tensor_tensor(out, d, wide(e_pick, n), ALU.is_equal))

            dve.wait_ge(lg_mm, 1)
            link(V.tensor_tensor(lg, ps[:, 7, 0:TT * N_ROUTE].rearrange("p (t n) -> p t n", t=TT),
                                 cols("route_bias").unsqueeze(1).to_broadcast([P, TT, N_ROUTE]), ALU.add))
            link(V.tensor_reduce(gmax, lg[:, :, 0:4], AX, ALU.max))
            V.tensor_tensor(g_exp, lg[:, :, 0:4], wide(gmax, 4), ALU.subtract).then_inc(gd_ready, 1)
            pick_first(gpick, lg[:, :, 0:4], gmax, 4)
            ge = lambda v: v.rearrange("p t (g e) -> p t g e", g=N_GROUPS)
            of_g = lambda v: v.unsqueeze(3).to_broadcast([P, TT, N_GROUPS, PER_GROUP])
            of_e = lambda v: v.unsqueeze(2).to_broadcast([P, TT, N_GROUPS, PER_GROUP])
            link(V.tensor_tensor(ge(spread), ge(lg[:, :, 4:N_ROUTE]), of_g(gpick), ALU.mult))
            link(V.tensor_reduce(es, spread.rearrange("p t (g e) -> p t e g", g=N_GROUPS), AX, ALU.add))
            link(V.tensor_reduce(e_top[:, :, 0:1], es, AX, ALU.max))
            pick_first(pick1, es, e_top[:, :, 0:1], 8)
            link(V.scalar_tensor_tensor(es_rest, pick1, -1e30, es, ALU.mult, ALU.add))
            link(V.tensor_reduce(e_top[:, :, 1:2], es_rest, AX, ALU.max))
            V.tensor_tensor(e_p2, e_top[:, :, 1:2], e_top[:, :, 0:1], ALU.subtract).then_inc(ed_ready, 1)
            pick_first(pick2, es_rest, e_top[:, :, 1:2], 8)
            V.tensor_tensor(ge(a1), of_g(gpick), of_e(pick1), ALU.mult)
            link(V.tensor_tensor(ge(a2), of_g(gpick), of_e(pick2), ALU.mult))
            V.tensor_tensor(any_e, a1, a2, ALU.add).then_inc(any_ready, 1)
            dve.wait_ge(gexp_ready, 1)
            link(V.tensor_reduce(g_w, g_exp, AX, ALU.add))
            dve.wait_ge(eexp_ready, 1)
            link(V.scalar_tensor_tensor(g_w, e_p2, 1.0, g_w, ALU.add, ALU.mult))
            link(V.reciprocal(e_w1, g_w))
            link(V.tensor_tensor(e_w2, e_w1, e_p2, ALU.mult))
            V.tensor_tensor(wsum, pick1, wide(e_w1, 8), ALU.mult)
            link(V.tensor_tensor(es, pick2, wide(e_w2, 8), ALU.mult))
            link(V.tensor_tensor(wsum, wsum, es, ALU.add))
            link(V.tensor_tensor(ge(comb), of_g(gpick), of_e(wsum), ALU.mult))
            V.tensor_copy(tg.rearrange("p t (j x) -> p t j x", x=3)[:, :, :, 1:3], comb.rearrange("p t (j x) -> p t j x", x=2))
            V.tensor_copy(tg.rearrange("p t (j x) -> p t j x", x=3)[:, :, :, 0:1],
                          cols("tok_id").unsqueeze(2).unsqueeze(3).to_broadcast([P, TT, NPAIR, 1]))
            dve.wait_ge(rank_mm, 1)
            rp = ps[:, 7, 0:TT * N_EXPERTS].rearrange("p (t e) -> p t e", t=TT)
            V.tensor_copy(counts, ps[:, 7, TT * N_EXPERTS:(TT + 1) * N_EXPERTS])
            link(V.tensor_copy(rank, rp))
            link(V.scalar_tensor_tensor(rank_only, any_e, -1000.0, rank, ALU.mult, ALU.add))
            link(V.tensor_scalar(rank_only, rank_only, 1000.0, None, ALU.add))
            iota = masks_sb[:, MI["iota"], 0:CAP].unsqueeze(1).to_broadcast([P, N_EXPERTS, CAP])
            for t in range(TT):
                last = V.tensor_tensor(sel[:, t, :, :], iota, rank_only[:, t, :].unsqueeze(2).to_broadcast([P, N_EXPERTS, CAP]), ALU.is_equal)
            last.then_inc(sel_ready, 1)
            V.scalar_tensor_tensor(over, rank, float(CAP), comb, ALU.is_ge, ALU.mult)
            dve.wait_ge(info_mm, 1)
            link(V.tensor_copy(slot_info[:, :, :], ps[:, 0, 0:3 * NPAIR].rearrange("p (j x) -> p j x", x=3)))
            V.tensor_copy(slot_gate[0:64, :], slot_info[0:64, :, 1])
            V.tensor_copy(slot_gate[64:128, :], slot_info[64:128, :, 2])
            V.tensor_copy(slot_tok[:, :], slot_info[:, :, 0]).then_inc(slots_ready, 1)
            dve.wait_ge(slots_ready, 1)
            link(V.tensor_reduce(most_f, counts, AX, ALU.max))
            V.tensor_copy(most[:, 0:1], most_f).then_inc(most_ready, 1)

            dve.wait_ge(h2_stored, 16 * TT)
            V.memset(y_acc, 0.0).then_inc(acc_added, 1)
            for t in range(TT):
                last = V.tensor_scalar(iota_w[:, t * P:(t + 1) * P], masks_sb[:, MI["iota"], :], float(t * P), None, ALU.add)
            last.then_inc(acc_added, 1)
            dve.wait_ge(acc_added, 2)

            def turned_half(i):
                dve.wait_ge(xgt_mm, i + 1)
                V.tensor_copy(xg_t[:, 0:4, :], ps[:, 0, :].rearrange("p (k i) -> p k i", k=4)).then_inc(xgt_ready, 1)

            def expert_pair(i, more):
                tok = slot_info[:, bass.ds(i, 1), 0] if more else slot_info[:, i, 0:1]
                gate = slot_gate[:, bass.ds(i, 1)] if more else slot_gate[:, i:i + 1]
                dve.wait_ge(gate_mm, i + 1)
                V.tensor_scalar(sel_t, iota_w, tok, None, ALU.is_equal)
                dve.wait_ge(up_mm, i + 1)
                dve.wait_ge(silu_done, i + 1)
                V.scalar_tensor_tensor(e_act, e_silu, gate, ps[:, 3, :], ALU.mult, ALU.mult).then_inc(hact_ready, 1)
                if more:
                    turned_half(i + 1)
                dve.wait_ge(down_mm, i + 1)
                V.tensor_copy(e_y[:, 0:512], ps[:, 5, :]).then_inc(y_half, 1)
                for m in range(2 * TT):
                    t, n = m // 2, m % 2
                    dve.wait_ge(spread_mm, i * 6 + m + 1)
                    a = y_acc[:, t, n * 512:(n + 1) * 512]
                    V.tensor_tensor(a, a, ps[:, (7, 4)[n], :], ALU.add).then_inc(acc_added, 1)

            turned_half(0)
            with dve.Fori(0, NPAIR - 1) as i:
                expert_pair(i, True)
            expert_pair(NPAIR - 1, False)

            def finish(t):
                dve.wait_ge(x2_rs, t + 1)
                V.scalar_tensor_tensor(y_acc[:, t, :], y_acc[:, t, :], ss[:, 4 + t:5 + t], final_row, ALU.mult, ALU.mult).then_inc(out_ready, 1)

            with dve.If(more_than_cap(dve)):
                dve.sem_inc(rest_added, 1)
                with dve.Fori(0, N_EXPERTS) as e:
                    for t in range(TT):
                        dve.wait_ge(rest_silu, e * TT + t + 1)
                        V.scalar_tensor_tensor(e_act, e_silu, over[:, t, bass.ds(e, 1)], ps[:, 1, :], ALU.mult, ALU.mult).then_inc(rest_act, 1)
                        dve.wait_ge(rest_down_mm, e * TT + t + 1)
                        V.tensor_tensor(o_scaled, ps[:, 3:5, :].rearrange("p n d -> p (n d)"), gt2_row[:, min(t, 1), :], ALU.mult).then_inc(rest_scaled, 1)
                        dve.wait_ge(rest_scaled, e * TT + t + 1)
                        V.tensor_tensor(x1_tok[:, t, :], x1_tok[:, t, :], o_scaled, ALU.add).then_inc(rest_added, 1)

            for t in range(TT):
                link(V.tensor_tensor(y_acc[:, t, :], y_acc[:, t, :], gt2_row[:, min(t, 1), :], ALU.mult))
                V.tensor_tensor(y_acc[:, t, :], y_acc[:, t, :], x1_tok[:, t, :], ALU.add).then_inc(x2_ready, 1)
                if t:
                    finish(t - 1)
            finish(TT - 1)


def _masks():
    import numpy as np
    p, f = np.arange(P)[:, None], np.arange(P)[None, :]
    same = (p // 64) == (f // 64)
    out = {"ident": p == f, "ones": p >= 0 * f, "upper": p <= f, "lower": p >= f, "upper64": (p <= f) & same, "lower64": (p >= f) & same,
           "ones64": same, "first64": (p < 64) & (f >= 0), "last64": (p >= 64) & (f >= 0), "strict_up": p < f, "iota": f + 0 * p,
           "eps": EPS + 0.0 * (p + f)}
    for m in LEVELS:
        pair = (p // (2 * m)) == (f // (2 * m))
        p_odd, f_odd = (p // m) % 2 == 1, (f // m) % 2 == 1
        out[f"lev0_{m}"] = pair & ~p_odd & f_odd
        out[f"lev1_{m}"] = pair & p_odd & ~f_odd
    return np.ascontiguousarray(np.stack([out[n] for n in MASKS], 1), dtype=np.float32)


def _positions():
    import numpy as np
    quarter = D_MODEL // 4
    omega = (1.0 / (np.float32(10000.0) ** (np.arange(quarter, dtype=np.float32) / np.float32(quarter)))).astype(np.float32)
    n = np.arange(DEC_SEQ)
    ar = (n // 64).astype(np.float32)[:, None] * omega
    ac = (n % 64).astype(np.float32)[:, None] * omega
    return np.ascontiguousarray(np.concatenate([np.sin(ar), np.cos(ar), np.sin(ac), np.cos(ac)], -1).T, dtype=np.float32)


def _layout(inputs):
    import numpy as np
    g = {k: np.asarray(v) for k, v in inputs.items()}

    def on_partitions(v):
        return np.reshape(v, (-1, P)).T

    def on_all(v):
        return np.broadcast_to(np.reshape(v, (1, -1)), (P, np.size(v)))

    conv_w = np.concatenate([g["conv_ssd_w"][0], g["conv_dn_w"][0]], 1)
    parts = {
        "c": np.stack([on_partitions(g["c_ctx"]), on_partitions(g["c"][0])], 2).reshape(P, -1),
        "b_ada": on_partitions(g["b_ada"][0]),
        "norm1": on_partitions(g["norm1_w"][0]), "norm2": on_partitions(g["norm2_w"][0]), "final": on_partitions(g["final_norm_w"]),
        "ssd_norm": on_partitions(g["ssd_norm_w"][0]), "dn_norm": on_partitions(g["dn_norm_w"][0]),
        "ssd_d": on_partitions(np.repeat(g["ssd_d"][0], SSD_HEAD_DIM)),
        "conv_w": conv_w.reshape(CONV_W, -1, P).transpose(2, 1, 0).reshape(P, -1),
        "conv_b": on_partitions(np.concatenate([g["conv_ssd_b"][0], g["conv_dn_b"][0]])),
        "gate_bias": on_all(np.concatenate([g["ssd_dt_bias"].ravel(), g["dn_dt_bias"].ravel()])),
        "a_log": on_all(np.concatenate([g["ssd_a_log"].ravel(), g["dn_a_log"].ravel()])),
        "route_bias": on_all(np.concatenate([g["b_router_group"].ravel(), g["b_router_expert"].ravel()])),
    }
    parts["desc8"] = on_all(np.arange(8, 0, -1, dtype=np.float32))
    parts["tok_id"] = on_partitions(np.arange(TOK, dtype=np.float32))
    params = np.concatenate([parts[n] for n in PC], 1)
    h0 = np.stack([g["state_ssd_fwd"][0, 0], g["state_ssd_bwd"][0, 0]])
    h0 = h0.reshape(2, SSD_GROUPS, 8, SSD_HEAD_DIM, SSD_STATE).transpose(0, 1, 4, 2, 3).reshape(2, P, 512)
    s0 = np.stack([g["state_dn_fwd"][0, 0], g["state_dn_bwd"][0, 0]]).transpose(0, 2, 1, 3)
    router = np.concatenate([g["w_router_group"][0], g["w_router_expert"][0]], 1).reshape(KD, P, N_ROUTE).transpose(1, 0, 2)
    c = np.ascontiguousarray
    return {"x_t": c(g["x_prompt"][0].T), "xs_t": c(g["x_sample"][0].T), "pos_t": _positions(), "params": c(params), "masks": _masks(),
            "w_ada": g["w_ada"][0], "w_in": g["w_in"][0], "w_out": g["w_out"][0], "h0_ssd": c(h0), "s0_dn": c(s0), "router": c(router),
            "w_gate": g["w_gate"][0], "w_up": g["w_up"][0], "w_down": g["w_down"][0]}


_INS = ["x_t", "xs_t", "pos_t", "params", "masks", "w_ada", "w_in", "w_out", "h0_ssd", "s0_dn", "router", "w_gate", "w_up", "w_down"]
_OUTS = [(SEQ, D_MODEL), (DEC_SEQ, D_MODEL), (SSD_WIDTH, SSD_STATE), (SSD_WIDTH, SSD_STATE), (P, DN_HEADS, P), (P, DN_HEADS, P)]


def kernel(**inputs):
    import numpy as np
    import concourse.bacc as _bacc
    from concourse import mybir as _mybir
    from concourse.bass_utils import run_bass_kernel_spmd as _run

    nc = _bacc.Bacc("TRN2", target_bir_lowering=False, num_devices=1)
    given = _layout(inputs)
    f32 = _mybir.dt.float32
    arrays = {f"in_{n}": given[n] for n in _INS}
    args = [nc.dram_tensor(f"in_{n}", given[n].shape, f32, kind="ExternalInput").ap() for n in _INS]
    h2_dram = nc.dram_tensor("h2_rows", (TOK, D_MODEL), f32, kind="Internal").ap()
    outs = [nc.dram_tensor(f"out_{i}", s, f32, kind="ExternalOutput").ap() for i, s in enumerate(_OUTS)]
    hybrid_step(nc, *args, h2_dram, outs)
    r = _run(nc, [arrays], core_ids=[0])
    y_p, y_s, s_f, s_b, d_f, d_b = (r.results[0][f"out_{i}"] for i in range(len(_OUTS)))
    ssd = (1, 1, SSD_HEADS, SSD_HEAD_DIM, SSD_STATE)
    return (y_p.reshape(1, SEQ, D_MODEL), y_s.reshape(1, DEC_SEQ, D_MODEL), s_f.reshape(ssd), s_b.reshape(ssd),
            np.ascontiguousarray(d_f.transpose(1, 0, 2))[None, None], np.ascontiguousarray(d_b.transpose(1, 0, 2))[None, None])
```

```python
import concourse.bass as bass
from concourse import mybir
from contextlib import ExitStack

P = 128
D_MODEL = 1024
KD = D_MODEL // P
SEQ, DEC_SEQ = 128, 256
TOK = SEQ + DEC_SEQ
TT = TOK // P
SEGS = ((0, SEQ), (SEQ, TOK))
EPS = 1e-6
CONV_W = 5
N_MOD = 6
NBM = N_MOD * KD
SSD_HEADS, SSD_HEAD_DIM, SSD_STATE, SSD_GROUPS = 16, 64, 64, 2
SSD_WIDTH = SSD_HEADS * SSD_HEAD_DIM
SSD_XBC = SSD_WIDTH + 2 * SSD_GROUPS * SSD_STATE
DN_HEADS, DN_HEAD_DIM, DN_CHUNK = 8, 128, 64
DN_WIDTH = DN_HEADS * DN_HEAD_DIM
N_GROUPS, PER_GROUP = 4, 8
N_EXPERTS = N_GROUPS * PER_GROUP
N_ROUTE = N_GROUPS + N_EXPERTS
F_EXP = 512
FK = F_EXP // P
CHUNK_COLS = 512

XBC0 = SSD_WIDTH
DT0 = XBC0 + SSD_XBC
QKV0 = DT0 + 2 * SSD_HEADS
ZD0 = QKV0 + 3 * DN_WIDTH
AB0 = ZD0 + DN_WIDTH
N_DT = 2 * SSD_HEADS
N_AB = 4 * DN_HEADS
CONV_BLOCKS = (SSD_XBC + 3 * DN_WIDTH) // P

_cols, PC = 0, {}
for _name, _n in (("c", 2 * KD), ("b_ada", NBM), ("norm1", KD), ("norm2", KD), ("final", KD),
                  ("ssd_norm", KD), ("dn_norm", 1), ("ssd_d", KD), ("conv_w", CONV_BLOCKS * CONV_W),
                  ("conv_b", CONV_BLOCKS), ("gate_bias", 48), ("a_log", 48), ("route_bias", N_ROUTE), ("desc8", 8), ("tok_id", TT), ("eps", 1)):
    PC[_name] = (_cols, _cols + _n)
    _cols += _n
N_PC = _cols

LEVELS = (1, 2, 4, 8, 16, 32)
MASKS = ["ident", "ones", "upper", "lower", "upper64", "lower64", "ones64", "first64", "last64", "strict_up"] + \
        [f"lev{d}_{m}" for d in (0, 1) for m in LEVELS] + ["iota"]
MI = {n: i for i, n in enumerate(MASKS)}


def hybrid_step(nc, x_t, xs_t, pos_t, params, masks, w_ada, w_in, w_out, h0_ssd, s0_dn, router, final_rows, w_gate, w_up, w_down,
                h2_dram, outs):
    fp32, fp32r = mybir.dt.float32, mybir.dt.float32r
    ALU = mybir.AluOpType
    ACT = mybir.ActivationFunctionType
    ctx = ExitStack()
    with ctx:
        def sb(name, shape, dt=fp32):
            return ctx.enter_context(nc.sbuf_tensor(name, shape, dt))

        def sem(name):
            return ctx.enter_context(nc.semaphore(name))

        RING = 4
        CAP = 64
        NPAIR = N_EXPERTS // 2
        ring_a = sb("ring_a", [P, 2, KD, CHUNK_COLS])
        with nc.sbuf_tensor("w_split", [P, 4, 2, KD, P], fp32r) as w_split:
            pass
        ring_b = sb("ring_b", [P, 2, KD, CHUNK_COLS])
        with nc.sbuf_tensor("h1_hi", [P, KD, TOK], fp32r) as h1_hi:
            pass
        buf_h = sb("buf_h", [P, KD * TOK])
        with nc.sbuf_tensor("sel", [P, TT, N_EXPERTS, CAP], fp32r) as sel:
            pass
        mix = sb("mix", [P, 2 * KD, TOK])
        x_ssd = sb("x_ssd", [P, KD, TOK])
        bc = sb("bc", [P, 2, TOK])
        q_t = sb("q_t", [P, KD, TOK])
        kv = sb("kv", [P, 2 * KD, TOK])
        k_t, v_t = kv[:, 0:KD, :], kv[:, KD:2 * KD, :]
        masks_sb = sb("masks_sb", [P, len(MASKS), P])
        pc = sb("pc", [P, N_PC])
        mod = sb("mod", [P, NBM, 2])
        amp1 = sb("amp1", [P, KD, 2])
        silu_c = sb("silu_c", [P, KD, 32])
        w_ab = sb("w_ab", [P, KD, N_DT + N_AB])
        with nc.sbuf_tensor("slot_parts", [P, TT, NPAIR, 6], fp32r) as tg:
            pass
        gates = sb("gates", [P, TT, 240])
        cums = sb("cums", [P, TT, P])
        b_tok = sb("b_tok", [P, TT, P])
        with nc.sbuf_tensor("below_h1_lo", [P, 4096], fp32), nc.sbuf_tensor("h1_lo", [P, KD, TOK], fp32r) as h1_lo:
            pass
        temp = sb("temp", [P, 8704])

        def carve(start, *dims):
            n = 1
            for d in dims:
                n *= d
            v = temp[:, start:start + n]
            if len(dims) == 1:
                return v
            names = "abcd"[:len(dims)]
            return v.rearrange(f"p ({' '.join(names)}) -> p {' '.join(names)}", **{c: d for c, d in zip(names[1:], dims[1:])})

        ps = ctx.enter_context(nc.psum_tensor("ps", [P, 8, 512], fp32))

        def mask(name):
            return masks_sb[:, MI[name], :]

        def col(name, i=0):
            a = PC[name][0] + i
            return pc[:, a:a + 1]

        def cols(name):
            a, b = PC[name]
            return pc[:, a:b]

        x0_t = q_t
        h1_t = v_t
        h2_t = buf_h[:, :].rearrange("p (k t) -> p k t", k=KD)
        x_tok = buf_h[:, :].rearrange("p (t c) -> p t c", t=TT)
        k_tok = x_tok
        v_tok = x_ssd[:, :, :].rearrange("p k t -> p (k t)").rearrange("p (t c) -> p t c", t=TT)
        o_t = v_t
        g_log, g_dt, g_beta = gates[:, :, 0:48], gates[:, :, 48:80], gates[:, :, 80:96]
        g_dte, g_be, g_nec, g_tot = gates[:, :, 96:128], gates[:, :, 128:144], gates[:, :, 144:160], gates[:, :, 160:240]

        wi = w_in.rearrange("(k p) n -> p k n", p=P)
        wa = w_ada.rearrange("(k p) n -> p k n", p=P)
        wo = w_out.rearrange("(k p) n -> p k n", p=P)
        proj_cols = [(XBC0, 512), (XBC0 + 512, 512), (XBC0 + 1024, 256)] + \
                    [(QKV0 + 512 * c, 512) for c in range(6)] + [(0, 512), (512, 512), (ZD0, 512), (ZD0 + 512, 512)]
        LOAD_PROJ, LOAD_ADA1, LOAD_ADA2, LOAD_OUT = 4, 17, 21, 25
        blocks = []
        for n, (a, w) in enumerate(proj_cols):
            for b in range(w // P):
                i = len(blocks)
                blocks.append((LOAD_PROJ + n, b * P, "conv" if i < CONV_BLOCKS else "z", i if i < CONV_BLOCKS else i - CONV_BLOCKS))
        NB = len(blocks)
        last_block = lambda load: max(n for n, blk in enumerate(blocks) if blk[0] == load)

        def conv_dest(i):
            if i < 8:
                return x_ssd[:, i, :]
            if i < 10:
                return bc[:, i - 8, :]
            return (q_t, k_t, v_t)[(i - 10) // KD][:, (i - 10) % KD, :]

        pc_in = sem("pc_in")
        x_in = sem("x_in")
        masks_in = sem("masks_in")
        wab_in = sem("wab_in")
        h0_in = sem("h0_in")
        s0_in = sem("s0_in")
        w_in_sem = [sem(f"w_ready{i}") for i in range(RING)]
        dve_step = sem("dve_step")
        act_step = sem("act_step")
        silu_zero = sem("silu_zero")
        silu_ready = sem("silu_ready")
        x_ready = sem("x_ready")
        sq_ready = sem("sq_ready")
        stat_ready = sem("stat_ready")
        rs_ready = sem("rs_ready")
        ada_mm = sem("ada_mm")
        row_ready = sem("row_ready")
        modp_ready = sem("modp_ready")
        mod_ready = sem("mod_ready")
        h1_full = sem("h1_full")
        h1_hi_ready = sem("h1_hi_ready")
        h1_ready = sem("h1_ready")
        hi_ready = sem("hi_ready")
        split_ready = sem("split_ready")
        block_mm = sem("block_mm")
        block_out = sem("block_out")
        conv_done = sem("conv_done")
        conv_out = sem("conv_out")
        tok_mm = sem("tok_mm")
        z_ready = sem("z_ready")
        na_ready = sem("na_ready")
        ln_ready = sem("ln_ready")
        log_ready = sem("log_ready")
        cum_mm = sem("cum_mm")
        cum_ready = sem("cum_ready")
        exps_ready = sem("exps_ready")
        qk_sq = sem("qk_sq")
        qk_sum = sem("qk_sum")
        qk_rs = sem("qk_rs")
        qk_ready = sem("qk_ready")
        xt_mm = sem("xt_mm")
        xt_ready = sem("xt_ready")
        xe_ready = sem("xe_ready")
        st_mm = sem("st_mm")
        st_out = sem("st_out")
        h_ready = sem("h_ready")
        c_ready = sem("c_ready")
        cb_mm = sem("cb_mm")
        cb_ready = sem("cb_ready")
        seg_mm = sem("seg_mm")
        seg_ready = sem("seg_ready")
        dec_ready = sem("dec_ready")
        ssd_m_ready = sem("ssd_m_ready")
        y_mm = sem("y_mm")
        y_ready = sem("y_ready")
        ynorm_ready = sem("ynorm_ready")
        states_out = sem("states_out")
        out_mm = sem("out_mm")
        kvt_mm = sem("kvt_mm")
        kvt_ready = sem("kvt_ready")
        s_zero = sem("s_zero")
        two = lambda name: [sem(f"{name}_fwd"), sem(f"{name}_bwd")]
        dseg_mm = two("dseg_mm")
        kq_mm = two("kq_mm")
        dseg_ready = two("dseg_ready")
        dec_exp = two("dec_exp")
        m_ready = two("dn_m_ready")
        off_ready = two("off_ready")
        d_ready = two("d_ready")
        lev_mm1 = two("lev_mm1")
        lev_p = two("lev_p")
        lev_mm2 = two("lev_mm2")
        ks_mm = two("ks_mm")
        r_ready = two("r_ready")
        vn_mm = two("vn_mm")
        vn_ready = two("vn_ready")
        ds_mm = two("ds_mm")
        s_ready = two("s_ready")
        o_mm = two("o_mm")
        o_out = two("o_out")
        o_sq = sem("o_sq")
        o_sum = sem("o_sum")
        o_rs = sem("o_rs")
        o_ready = sem("o_ready")

        PAIRS = [(hq, kind) for hq in range(2) for kind in range(3)]
        def ada(g, order, before):
            return [(wa[:, 2 * i:2 * i + 2, 2048 * g:2048 * (g + 1)], None, slot, before) for i, slot in enumerate(order)]

        def proj_before(n):
            return None if n == 0 else (ada_mm, 1) if n <= 2 else (split_ready, 1 + last_block(LOAD_PROJ + n - 2))

        proj_slot = lambda n: RING if n == 0 else n % 2
        n_proj = len(proj_cols)
        ada1 = ada(1, ((n_proj - 2) % 2, (n_proj - 1) % 2, 2, 3), (split_ready, 1 + last_block(LOAD_PROJ + n_proj - 2)))
        ada1[1] = ada1[1][:3] + ((split_ready, NB),)
        ada1[2:] = [load[:3] + ((block_mm, NB),) for load in ada1[2:]]
        loads = ada(0, range(4), None) + \
            [(wi[:, :, a:a + w], w, proj_slot(n), proj_before(n)) for n, (a, w) in enumerate(proj_cols)] + \
            ada1 + ada(2, range(4), (ada_mm, 2)) + \
            [(wo[:, kh * KD:(kh + 1) * KD, dh * 512:(dh + 1) * 512], 512, 2 * dh + kh, ((ada_mm, 3), (o_mm[1], len(PAIRS)))[dh]) for dh in range(2) for kh in range(2)]
        slot_of = [load[2] for load in loads]
        arrivals = lambda load: slot_of[:load + 1].count(slot_of[load])
        ada_rows_of = lambda slot: slots[slot].rearrange("p k n -> p (k n)").rearrange("p (k n) -> p k n", k=2)

        pad = carve(0, 2, 392)
        conv_acc = carve(784, 2, 388)
        mod_row = carve(1600, 512)
        rs1 = carve(3700, TOK)
        sg = carve(7168, 6, TT, 48)
        sq = carve(2560, 2, TOK)
        rs = carve(1792, 2, TOK)
        x_end = carve(3072, 2, SSD_WIDTH)
        seg = [carve(1024 * i, 2, 4, P) for i in range(3)]
        c_dec = carve(3072, 2, 2, 4 * P).rearrange("p n d (h i) -> p n d h i", h=4)
        st_stage = carve(5120, 2, KD, SSD_STATE)
        h_st = carve(6144, 4, 512)
        cbm = carve(8192, 2, 2, P)
        y_tmp = w_ab[:, :, :].rearrange("p k n -> p (k n)").rearrange("p (n b i) -> p n b i", n=2, b=2)
        y_sq = carve(3072, KD, TOK)
        y_rs = b_tok[:, :, :].rearrange("p t c -> p (t c)")

        x1_t = q_t
        x1_tok = x_ssd[:, :, :].rearrange("p k t -> p (k t)").rearrange("p (t c) -> p t c", t=TT)
        h2_tok = carve(0, TT, D_MODEL)
        rs2 = carve(8192, TOK)
        amp2 = amp1
        kv_flat = kv[:, :, :].rearrange("p k t -> p (k t)")
        mix_flat = mix[:, :, :].rearrange("p k t -> p (k t)")
        slots = [r[:, i, :, :] for r in (ring_a, ring_b) for i in range(2)] + [m[:, 0:KD * 512].rearrange("p (k n) -> p k n", k=KD) for m in (mix_flat, kv_flat)]
        down = [m.rearrange("p k n -> p (k n)").rearrange("p (f n) -> p f n", f=FK) for m in slots]
        slot_in = w_in_sem + [sem("w_ready4"), sem("w_ready5")]
        n_loads = [slot_of.count(s) for s in range(6)]
        router_sb = bc[:, :, :].rearrange("p k t -> p (k t)")[:, 0:KD * N_ROUTE].rearrange("p (k n) -> p k n", k=KD)
        rt = kv_flat[:, 4096:4096 + TT * 600].rearrange("p (t n) -> p t n", t=TT)
        take = [0]

        def field(n):
            take[0] += n
            return rt[:, :, take[0] - n:take[0]]

        lg, gmax, geq, gpick, g_exp, g_w = field(N_ROUTE), field(1), field(4), field(4), field(4), field(1)
        es, es_rest, e_top, e_eq, e_pick, pick1, pick2 = field(8), field(8), field(2), field(8), field(1), field(8), field(8)
        e_p2, e_w1, e_w2, wsum = field(1), field(1), field(1), field(8)
        spread, a1, a2, any_e, comb, rank, rank_only, over = [field(N_EXPERTS) for _ in range(8)]
        info = silu_c[:, :, :].rearrange("p k c -> p (k c)")
        slot_info, slot_gate = info[:, 0:5 * NPAIR].rearrange("p (j x) -> p j x", x=5), info[:, 5 * NPAIR:6 * NPAIR]
        slot_tok = sb("slot_tok", [P, NPAIR], mybir.dt.uint32)
        cur_tok = sb("cur_tok", [P, 1], mybir.dt.uint32)
        xg = carve(3072, D_MODEL)
        xg_t = carve(4096, KD, P)
        e_silu = carve(5120, F_EXP)
        e_act = carve(5632, F_EXP)
        e_act_t = carve(6144, FK, P)
        e_y = carve(6656, D_MODEL)
        sel_t = carve(7680, TOK)
        iota_w = carve(8192, TOK)
        y_acc = carve(0, TT, D_MODEL)
        x2_sq = carve(4096, D_MODEL)
        ss, most_f, counts = cums[:, 0, 0:8], cums[:, 0, 8:9], cums[:, 0, 16:48]
        gt2_row = q_t[:, :, :].rearrange("p k t -> p (k t)")[:, 0:2048].rearrange("p (c d) -> p c d", c=2)
        final_row = q_t[:, :, :].rearrange("p k t -> p (k t)")[:, 2048:3072]
        most = sb("most", [P, 2], mybir.dt.int32)
        o_scaled = carve(4096, D_MODEL)
        most_ready = sem("most_ready")
        rest_in = [sem(f"rest_{n}_in") for n in ("gate", "up", "down")]
        rest_up_mm = sem("rest_up_mm")
        rest_silu = sem("rest_silu")
        rest_act = sem("rest_act")
        rest_at_mm = sem("rest_at_mm")
        rest_at = sem("rest_at")
        rest_down_mm = sem("rest_down_mm")
        rest_scaled = sem("rest_scaled")
        rest_added = sem("rest_added")
        router_in = sem("router_in")
        h2_stored = sem("h2_stored")
        x1_ready = sem("x1_ready")
        h2_ready = [sem("h2_ready_a"), sem("h2_ready_b")]
        h2_scaled = sem("h2_scaled")
        lg_mm = sem("lg_mm")
        h2t_mm = sem("h2t_mm")
        h2t_ready = sem("h2t_ready")
        x1t_mm = sem("x1t_mm")
        x1t_ready = sem("x1t_ready")
        gd_ready = sem("gd_ready")
        gexp_ready = sem("gexp_ready")
        any_ready = sem("any_ready")
        rank_mm = sem("rank_mm")
        sel_ready = sem("sel_ready")
        info_mm = sem("info_mm")
        slots_ready = sem("slots_ready")
        rows_mm = sem("rows_mm")
        rows_ready = sem("rows_ready")
        cur_ready = sem("cur_ready")
        gather_go = sem("gather_go")
        xg_in = sem("xg_in")
        xgt_mm = sem("xgt_mm")
        xgt_ready = sem("xgt_ready")
        gate_mm = sem("gate_mm")
        up_mm = sem("up_mm")
        silu_done = sem("silu_done")
        hact_ready = sem("hact_ready")
        at_mm = sem("at_mm")
        at_ready = sem("at_ready")
        down_mm = sem("down_mm")
        y_half = sem("y_half")
        spread_mm = sem("spread_mm")
        acc_added = sem("acc_added")
        x2_ready = sem("x2_ready")
        x2_rs = sem("x2_rs")
        out_ready = sem("out_ready")
        out_stored = sem("out_stored")
        TILE = ((0, 0), (1, 2), (2, 1))
        LAST_DIR_ADDS = ((False, True), (False, False), (True, True))
        tiles = [[temp[:, 512 * i:512 * i + 512] for i in range(13)] + [slots[3][:, 6, :]],
                 [slots[2 + i // 8][:, i % 8, :] for i in range(14)]]
        tiles = [[v.rearrange("p (h i) -> p h i", h=4) for v in tiles[a]] for a in range(2)]
        dn_m, dn_p, dn_d, dn_r, dn_vb, dn_vo = [[tiles[a][i] for a in range(2)] for i in (0, 1, 2, 6, 7, 8)]
        dn_e, dn_qk, dn_dt, dn_off = [[[tiles[a][i], tiles[a][j]] for a in range(2)] for i, j in ((3, 9), (4, 10), (5, 11), (12, 13))]
        dn_s = carve(6656, 2, 2, 4 * P)
        bank_a, bank_b, bank_x, bank_o = (0, 2), (1, 3), (4, 5), (6, 7)
        DN_ROUND = ((1, 0), (0, 0), (1, 1), (0, 1), (1, 2), (0, 2), (1, 3), (1, 4), (0, 3), (1, 5), (1, 6), (0, 4), (1, 7), (1, 8),
                    (0, 5), (1, 9), (1, 10), (0, 6), (1, 11), (1, 12))

        def dn_rounds(chunk_step, inverse_step):
            for r in range(-1, len(PAIRS)):
                for inverse, n in DN_ROUND:
                    if inverse and r + 1 < len(PAIRS):
                        inverse_step(r + 1, n)
                    elif not inverse and r >= 0:
                        chunk_step(r, n)

        def dn_pair(p):
            return (*PAIRS[p], TILE[PAIRS[p][1]])

        def dn_rows(step, a):
            c = step if a == 0 else 1 - step
            return c, slice(64 * c, 64 * c + 64)

        mod_row1 = w_ab[:, :, :].rearrange("p k n -> p (k n)")
        mod_row2 = slots[3][:, 7, :]
        o_sq_t = buf_h[:, 0:2 * TOK].rearrange("p (n t) -> p n t", n=2)
        o_rs_t = buf_h[:, 2 * TOK:4 * TOK].rearrange("p (n t) -> p n t", n=2)

        SSD_UNITS = [(t, u) for t in range(TT) for u in range(4)]
        ENDS = [(0, 0), (0, 1), (1, 0), (2, 1)]

        block = ctx.enter_context(nc.Block())

        def more_than_cap(eng):
            eng.wait_ge(most_ready, 1)
            return eng.value_load(most[0:1, 0:1], min_val=0, max_val=TOK) > CAP

        @block.sync
        def _(sp):
            sp.dma_start(pc[:, :], params).then_inc(pc_in, 16)
            sp.dma_start(masks_sb[:, 0:2, :], masks[:, 0:2, :]).then_inc(masks_in, 16)
            sp.dma_start(x0_t[:, :, 0:SEQ], x_t.rearrange("(k p) t -> p k t", p=P)).then_inc(x_in, 16)
            sp.dma_start(x0_t[:, :, SEQ:TOK], xs_t.rearrange("(k p) t -> p k t", p=P)).then_inc(x_in, 16)
            sp.dma_start(k_t[:, :, 0:DEC_SEQ], pos_t.rearrange("(k p) t -> p k t", p=P)).then_inc(x_in, 16)
            def load(i):
                src, n, slot, before = loads[i]
                if before:
                    sp.wait_ge(*before)
                dst = slots[slot][:, :, 0:n] if n else ada_rows_of(slot)
                sp.dma_start(dst, src).then_inc(slot_in[slot], 16)

            for i in range(len(loads) - 2):
                load(i)
                if i == 4:
                    sp.dma_start(masks_sb[:, 2:, :], masks[:, 2:, :]).then_inc(masks_in, 16)
                    sp.dma_start(w_ab[:, :, 0:N_DT], wi[:, :, DT0:DT0 + N_DT]).then_inc(wab_in, 16)
                    sp.dma_start(w_ab[:, :, N_DT:N_DT + N_AB], wi[:, :, AB0:AB0 + N_AB]).then_inc(wab_in, 16)

            for a in range(2):
                sp.wait_ge(o_mm[a], len(PAIRS))
            sp.dma_start(x0_t[:, :, 0:SEQ], x_t.rearrange("(k p) t -> p k t", p=P)).then_inc(x_in, 16)
            sp.dma_start(x0_t[:, :, SEQ:TOK], xs_t.rearrange("(k p) t -> p k t", p=P)).then_inc(x_in, 16)
            sp.dma_start(k_t[:, :, 0:DEC_SEQ], pos_t.rearrange("(k p) t -> p k t", p=P)).then_inc(x_in, 16)
            load(len(loads) - 2)
            load(len(loads) - 1)

            def expert_load(e, s):
                src = (w_gate, w_gate, w_up, w_up, w_down, w_down)[s]
                e = e + s % 2
                src = src[e, :, :] if isinstance(e, int) else src[bass.ds(e, 1), :, :].rearrange("a d f -> (a d) f")
                dst = slots[s] if s < 4 else down[s]
                sp.dma_start(dst, src.rearrange("(k p) n -> p k n", p=P)).then_inc(slot_in[s], 16)

            sp.wait_ge(out_mm, KD)
            for s in range(RING):
                expert_load(0, s)
            sp.wait_ge(stat_ready, 2 + KD)
            sp.wait_ge(x_ready, 2)
            expert_load(0, 5)
            for t in range(TT):
                sp.wait_ge(h2t_ready, t + 1)
                sp.dma_start(h2_dram[t * P:(t + 1) * P, :], h2_tok[:, t, :]).then_inc(h2_stored, 16)
            sp.wait_ge(info_mm, 1)
            sp.wait_ge(xg_in, 16)
            expert_load(0, 4)
            sp.wait_ge(x1t_mm, TT)
            sp.dma_start(final_row, final_rows).then_inc(pc_in, 16)
            with sp.Fori(1, NPAIR) as i:
                for s in range(6):
                    sp.wait_ge((gate_mm, up_mm, down_mm)[s // 2], i)
                    expert_load(2 * i, s)
            with sp.If(more_than_cap(sp)):
                sp.wait_ge(down_mm, NPAIR)
                with sp.Fori(0, N_EXPERTS) as e:
                    sp.wait_ge(rest_added, e * TT + 1)
                    for n, src in enumerate((w_gate, w_up, w_down)):
                        dst = down[2] if n == 2 else slots[n]
                        sp.dma_start(dst, src[bass.ds(e, 1), :, :].rearrange("a (k p) n -> p (a k) n", p=P)).then_inc(rest_in[n], 16)
            for t in range(TT):
                sp.wait_ge(out_ready, t + 1)
                dst = outs[0] if t == 0 else outs[1][(t - 1) * P:t * P, :]
                sp.dma_start(dst, y_acc[:, t, :]).then_inc(out_stored, 16)
            sp.wait_ge(out_stored, 16 * TT)
        @block.gpsimd
        def _(pool):
            for n, (load, c, kind, i) in enumerate(blocks):
                pool.wait_ge(hi_ready, n + 1)
                nc.gpsimd.tensor_tensor(w_split[:, n % 4, 1, :, :], slots[slot_of[load]][:, :, c:c + P],
                                        w_split[:, n % 4, 0, :, :].bitcast(fp32), ALU.subtract).then_inc(split_ready, 1)
            pool.wait_ge(qk_ready, 2 * KD)
            for d in range(2):
                pool.dma_start(h_st[:, 2 * d, :], h0_ssd[d]).then_inc(h0_in, 16)
            for d in range(2):
                pool.wait_ge(st_out, d + 1)
                pool.dma_start(outs[2 + d].rearrange("(b q) n -> q b n", q=P), st_stage[:, d, :, :]).then_inc(states_out, 16)
            for n, (t, u) in enumerate(SSD_UNITS):
                sl = slice(64 * (u // 2), 64 * (u // 2) + 64)
                if t:
                    pool.wait_ge(dec_ready, n + 1)
                    nc.gpsimd.tensor_tensor(c_dec[sl, n % 2, :, :, :].rearrange("p d h i -> p (d h) i"),
                                            c_dec[sl, n % 2, :, :, :].rearrange("p d h i -> p (d h) i"),
                                            bc[sl, 1, t * P:(t + 1) * P].unsqueeze(1).to_broadcast([64, 8, P]), ALU.mult).then_inc(c_ready, 1)
            pool.wait_ge(ssd_m_ready, len(SSD_UNITS))
            pool.dma_start(router_sb, router).then_inc(router_in, 16)

            def first_states(hq):
                for d in range(2):
                    pool.dma_start(dn_s[:, 1, d, :], s0_dn[d, :, 4 * hq:4 * hq + 4, :].rearrange("k h v -> k (h v)")).then_inc(s0_in, 16)

            def inverse_step(p, n):
                lev = (n - 1) // 2 + 1 if n else 1
                if n == 0 or (n % 2 and 3 <= n <= 9):
                    for a in range(2):
                        pool.wait_ge(m_ready[a], 2 * p + 1)
                        if p or n:
                            pool.wait_ge(lev_mm1[a], 6 * p + lev - 1)
                        if lev == 2:
                            pool.wait_ge(d_ready[a], 7 * p + 2)
                        nc.gpsimd.tensor_tensor(dn_off[a][lev % 2], dn_m[a], mask(f"lev{a}_{LEVELS[lev]}").unsqueeze(1).to_broadcast([P, 4, P]),
                                                ALU.mult).then_inc(off_ready[a], 1)

            def chunk_step(p, n):
                hq, kind = PAIRS[p]
                if kind == 0 and n == 5:
                    for d in range(2):
                        pool.wait_ge(s_ready[d], 2 * p + 2)
                        pool.dma_start(outs[4 + d][:, 4 * hq:4 * hq + 4, :].rearrange("k h v -> k (h v)"), dn_s[:, 0, d, :]).then_inc(states_out, 16)
                if p == 2 and n == 5:
                    for d in range(2):
                        pool.wait_ge(s_ready[d], 2 * p + 2)
                    first_states(1)

            pool.wait_ge(kvt_ready, 2)
            first_states(0)
            dn_rounds(chunk_step, inverse_step)
            pool.wait_ge(states_out, 96)

            pool.wait_ge(rs_ready, 3)
            pool.wait_ge(x1_ready, KD)
            for k in range(4, KD):
                nc.gpsimd.tensor_tensor(h2_t[:, k, :], x1_t[:, k, :], rs2, ALU.mult).then_inc(h2_scaled, 1)

            def gather():
                pool.indirect_dma_start(out=xg, out_offset=None, in_=h2_dram,
                                        in_offset=bass.IndirectOffsetOnAxis(ap=cur_tok[:, 0:1], axis=0)).then_inc(xg_in, 16)

            pool.wait_ge(slots_ready, 1)
            pool.wait_ge(h2_stored, 16 * TT)
            nc.gpsimd.tensor_copy(cur_tok[:, :], slot_tok[:, 0:1]).then_inc(cur_ready, 1)
            pool.wait_ge(cur_ready, 1)
            gather()
            with pool.Fori(1, NPAIR) as i:
                pool.wait_ge(xg_in, i * 16)
                nc.gpsimd.tensor_copy(cur_tok[:, :], slot_tok[:, bass.ds(i, 1)]).then_inc(cur_ready, 1)
                pool.wait_ge(cur_ready, i + 1)
                pool.wait_ge(xgt_mm, i)
                pool.sem_inc(gather_go, 1)
                gather()

        @block.tensor
        def _(pe):
            def ready(i):
                pe.wait_ge(slot_in[slot_of[i]], 16 * arrivals(i))

            def ada_products(first, bank, ks):
                for k in ks:
                    if k % 2 == 0:
                        ready(first + k // 2)
                    for j in range(4):
                        last = nc.tensor.matmul(ps[32 * j:32 * j + 32, bank, :], silu_c[:, k, :],
                                                ada_rows_of(slot_of[first + k // 2])[:, k % 2, j * 512:(j + 1) * 512], start=(k == 0), stop=(k == KD - 1), tile_position=(0, 32 * j))
                if k == KD - 1:
                    last.then_inc(ada_mm, 1)

            def ada_columns(g, rows):
                pe.wait_ge(row_ready, g + 1)
                if g:
                    pe.wait_ge(mod_ready, g)
                for b in range(4):
                    last = nc.tensor.transpose(ps[:, 7, b * P:(b + 1) * P], rows[:, b * P:(b + 1) * P], mask("ident"))
                last.then_inc(modp_ready, 1)

            pe.wait_ge(masks_in, 16)
            pe.wait_ge(sq_ready, 1)
            for k in range(KD):
                last = nc.tensor.matmul(ps[:, 1, 0:TOK], mask("ones"), v_t[:, k, :], start=(k == 0), stop=(k == KD - 1))
            last.then_inc(stat_ready, 1)
            pe.wait_ge(silu_ready, 1)
            ada_products(0, 0, range(KD))
            ada_columns(0, mod_row)

            def norm_sum(i):
                pe.wait_ge(qk_sq, i + 1)
                if i >= 2:
                    pe.wait_ge(qk_rs, i - 1)
                nc.tensor.matmul(ps[:, i % 2, 0:TOK], mask("ones"), sq[:, i % 2, :], start=True, stop=True).then_inc(qk_sum, 1)

            for n, (load, c, kind, i) in enumerate(blocks):
                pe.wait_ge(split_ready, n + 1)
                if n >= 3:
                    pe.wait_ge(block_out, n - 2)
                w_hi, w_lo = w_split[:, n % 4, 0, :, :], w_split[:, n % 4, 1, :, :]
                for k in range(KD):
                    if n == 0:
                        pe.wait_ge(h1_ready, k + 1)
                    for x, (w, h) in enumerate(((w_hi, h1_hi), (w_lo, h1_hi), (w_hi, h1_lo))):
                        last = nc.tensor.matmul(ps[:, 2 + n % 3, 0:TOK], w[:, k, :], h[:, k, :],
                                                start=(k == 0 and x == 0), stop=(k == KD - 1 and x == 2))
                last.then_inc(block_mm, 1)
                if n == 9:
                    pe.wait_ge(masks_in, 32)
                    pe.wait_ge(wab_in, 32)
                    for t in range(TT):
                        for k in range(KD):
                            last = nc.tensor.matmul(ps[:, 5, 64 * t:64 * t + 64], h1_t[:, k, t * P:(t + 1) * P],
                                                    w_ab[:, k, :], start=(k == 0), stop=(k == KD - 1))
                    last.then_inc(tok_mm, 1)
                if kind == "z" and i == 3:
                    pe.wait_ge(log_ready, 1)
                    for t in range(TT):
                        for m, a, b, o in (("upper", 0, 16, 0), ("lower", 16, 32, 16), ("upper64", 32, 40, 32), ("lower64", 40, 48, 40),
                                           ("ones", 0, 32, 48), ("ones64", 32, 48, 80), ("first64", 32, 48, 96), ("last64", 32, 48, 112)):
                            last = nc.tensor.matmul(ps[:, 6, t * P + o:t * P + o + b - a], mask(m), g_log[:, t, a:b], start=True, stop=True)
                    last.then_inc(cum_mm, 1)
                if kind == "z" and i:
                    norm_sum(i - 1)
            norm_sum(2 * KD - 1)

            for t in range(TT):
                if t:
                    pe.wait_ge(xt_ready, t)
                else:
                    pe.wait_ge(block_out, NB)
                for b in range(KD):
                    nc.tensor.transpose(ps[:, 2 + b // 4, (b % 4) * P:(b % 4 + 1) * P], x_ssd[:, b, t * P:(t + 1) * P], mask("ident"))
                nc.tensor.transpose(ps[:, 4, 0:P], bc[:, 0, t * P:(t + 1) * P], mask("ident")).then_inc(xt_mm, 1)

            def state_products(i):
                pe.wait_ge(xe_ready, i + 1)
                if i in (1, 2):
                    pe.wait_ge(st_out, i)
                elif i == 3:
                    pe.wait_ge(h_ready, 1)
                for b in range(KD if i < 2 else 0):
                    g = b // 4
                    last = nc.tensor.matmul(ps[:, 5, b * 64:(b + 1) * 64], x_end[:, i % 2, b * P:(b + 1) * P],
                                            b_tok[:, 0, 64 * g:64 * g + 64], start=True, stop=True)
                for g in range(SSD_GROUPS if i >= 2 else 0):
                    last = nc.tensor.matmul(ps[64 * g:64 * g + 64, 5, :], b_tok[:, i - 1, 64 * g:64 * g + 64],
                                            x_end[:, i % 2, g * 512:(g + 1) * 512], start=True, stop=True, tile_position=(0, 64 * g))
                last.then_inc(st_mm, 1)

            def seg_products(n):
                t, u = SSD_UNITS[n]
                if n == 0:
                    pe.wait_ge(qk_rs, 2 * KD)
                elif n == 1:
                    pe.wait_ge(xt_ready, TT)
                if n >= 2:
                    pe.wait_ge(dec_ready, n - 1)
                if u == 0:
                    if t:
                        pe.wait_ge(cb_ready, t)
                    for g in range(2):
                        last = nc.tensor.matmul(ps[:, 6 + g, 0:P], bc[64 * g:64 * g + 64, 0, t * P:(t + 1) * P],
                                                bc[64 * g:64 * g + 64, 1, t * P:(t + 1) * P], start=True, stop=True, tile_position=(64 * g, 0))
                    last.then_inc(cb_mm, 1)
                for d in range(2):
                    for h in range(4):
                        hh = 16 * d + 4 * u + h
                        last = nc.tensor.matmul(ps[:, 2 * (n % 2) + d, h * P:(h + 1) * P],
                                                g_log[:, t, hh:hh + 1].to_broadcast([P, P]), mask(("upper", "lower")[d]),
                                                start=True, stop=True)
                last.then_inc(seg_mm, 1)

            def y_products(n):
                t, u = SSD_UNITS[n]
                g = u // 2
                pe.wait_ge(ssd_m_ready, n + 1)
                if t:
                    pe.wait_ge(c_ready, n - 3)
                    pe.wait_ge(h_ready, 2)
                if n:
                    pe.wait_ge(y_ready, n)
                for b in range(2):
                    for d in range(2):
                        for e in range(2):
                            h = 2 * b + e
                            out = ps[64 * e:64 * e + 64, 4, b * P:(b + 1) * P]
                            head = 4 * u + h
                            last = nc.tensor.matmul(out, x_tok[:, t, 64 * head:64 * head + 64], seg[n % 3][:, d, h, :],
                                                    start=(d == 0), stop=(d == 1 and t == 0), tile_position=(0, 64 * e))
                        if t:
                            for e in range(2):
                                h = 2 * b + e
                                out = ps[64 * e:64 * e + 64, 4, b * P:(b + 1) * P]
                                st = 2 * d + (t - 1 if d == 0 else 2 - t)
                                lo = (4 * u + h) % 8
                                last = nc.tensor.matmul(out, h_st[64 * g:64 * g + 64, st, 64 * lo:64 * lo + 64],
                                                        c_dec[64 * g:64 * g + 64, n % 2, d, h, :], start=False, stop=(d == 1),
                                                        tile_position=(64 * g, 64 * e))
                last.then_inc(y_mm, 1)

            for n in range(len(SSD_UNITS) + 2):
                if n < len(SSD_UNITS):
                    seg_products(n)
                if 1 <= n <= 4:
                    state_products(n - 1)
                if n >= 2:
                    y_products(n - 2)
                if 5 <= n <= 8:
                    pe.wait_ge(h_ready, 2)
                    ada_products(LOAD_ADA1, 5, [2 * (n - 5), 2 * (n - 5) + 1])

            for t in range(TT):
                if t == 0:
                    pe.wait_ge(y_ready, len(SSD_UNITS))
                else:
                    pe.wait_ge(kvt_ready, 2 * t)
                for i, src in enumerate((k_t, v_t)):
                    for b in range(KD):
                        last = nc.tensor.transpose(ps[:, 2 * i + b // 4, (b % 4) * P:(b % 4 + 1) * P], src[:, b, t * P:(t + 1) * P], mask("ident"))
                last.then_inc(kvt_mm, 1)
                ada_products(LOAD_ADA2, 4, range(3 * t, min(3 * t + 3, KD)))
            def inverse_step(p, n):
                inverse_products(p, n)
                if p == 0:
                    beside_first_inverse(n)

            def inverse_products(p, n):
                hq, kind, tile = dn_pair(p)
                lev = (n - 1) // 2
                for a in range(2):
                    t = tile[a]
                    tok = slice(t * P, (t + 1) * P)
                    A, B = ps[:, bank_a[a], :], ps[:, bank_b[a], :]
                    off, d, dt, prod = dn_off[a][lev % 2], dn_d[a], dn_dt[a][p % 2], dn_p[a]
                    if n == 0:
                        if p:
                            pe.wait_ge(d_ready[a], 7 * p)
                        for h in range(4):
                            c = 32 + 8 * a + 4 * hq + h
                            last = nc.tensor.matmul(A[:, h * P:(h + 1) * P], g_log[:, t, c:c + 1].to_broadcast([P, P]),
                                                    mask(("upper64", "lower64")[a]), start=True, stop=True)
                        last.then_inc(dseg_mm[a], 1)
                        for h in range(4):
                            last = nc.tensor.matmul(B[:, h * P:(h + 1) * P], k_t[:, 4 * hq + h, tok], k_t[:, 4 * hq + h, tok],
                                                    start=True, stop=True)
                        last.then_inc(dseg_mm[a], 1)
                    elif n == 1:
                        pe.wait_ge(dec_exp[a], 2 * p + 2)
                        for h in range(4):
                            last = nc.tensor.matmul(A[:, h * P:(h + 1) * P], k_t[:, 4 * hq + h, tok], q_t[:, 4 * hq + h, tok],
                                                    start=True, stop=True)
                        last.then_inc(kq_mm[a], 1)
                    elif n == 2 or n % 2:
                        if n == 2:
                            lev, off = 0, dn_off[a][0]
                        if lev == 0:
                            pe.wait_ge(m_ready[a], 2 * p + 2)
                        else:
                            pe.wait_ge(off_ready[a], 5 * p + lev)
                        pe.wait_ge(d_ready[a], 7 * p + lev + 1)
                        for h in range(4):
                            last = nc.tensor.matmul(A[:, h * P:(h + 1) * P], off[:, h, :], mask("ident") if lev == 0 else d[:, h, :],
                                                    start=True, stop=True)
                        last.then_inc(lev_mm1[a], 1)
                    else:
                        lev = (n - 2) // 2
                        pe.wait_ge(lev_p[a], 5 * p + lev)
                        if lev < 5:
                            for h in range(4):
                                nc.tensor.matmul(A[:, h * P:(h + 1) * P], dt[:, h, :], prod[:, h, :], start=True, stop=True)
                        for h in range(4):
                            last = nc.tensor.matmul(B[:, h * P:(h + 1) * P], prod[:, h, :], dt[:, h, :], start=True, stop=True)
                        last.then_inc(lev_mm2[a], 1)

            def chunk_step(p, n):
                hq, kind, tile = dn_pair(p)
                step = n // 3
                for a in range(2):
                    t = tile[a]
                    c, rows = dn_rows(step, a)
                    X, O = ps[:, bank_x[a], :], ps[:, bank_o[a], :]
                    st = dn_s[:, min(kind, 1), a, :]
                    if n in (0, 3):
                        if p or step:
                            pe.wait_ge(s_ready[a], 2 * p + step)
                        if step == 0:
                            if kind == 0:
                                pe.wait_ge(s_zero, hq + 1)
                            elif kind == 1:
                                pe.wait_ge(s0_in, 32 * (hq + 1))
                            pe.wait_ge(d_ready[a], 7 * p + 7)
                            if p:
                                pe.wait_ge(o_out[a], p)
                        for h in range(4):
                            last = nc.tensor.matmul(X[rows, h * P:(h + 1) * P], k_t[:, 4 * hq + h, t * P + 64 * c:t * P + 64 * c + 64],
                                                    st[:, h * P:(h + 1) * P], start=True, stop=True)
                        last.then_inc(ks_mm[a], 1)
                        for h in range(4):
                            nc.tensor.matmul(O[:, h * P + 64 * c:h * P + 64 * c + 64], st[:, h * P:(h + 1) * P], dn_e[a][p % 2][:, h, rows],
                                             start=(step == 0 and h == 0), stop=False, skip_group_check=True)
                    elif n in (1, 4):
                        pe.wait_ge(r_ready[a], 2 * p + step + 1)
                        for h in range(4):
                            last = nc.tensor.matmul(X[rows, h * P:(h + 1) * P], dn_dt[a][p % 2][rows, h, rows], dn_r[a][rows, h, :],
                                                    start=True, stop=True)
                        last.then_inc(vn_mm[a], 1)
                    elif n in (2, 5):
                        pe.wait_ge(vn_ready[a], 2 * p + step + 1)
                        for h in range(4):
                            last = nc.tensor.matmul(X[:, h * P:(h + 1) * P], k_tok[rows, t, (4 * hq + h) * P:(4 * hq + h + 1) * P],
                                                    dn_vb[a][rows, h, :], start=True, stop=True)
                        last.then_inc(ds_mm[a], 1)
                    else:
                        for h in range(4):
                            last = nc.tensor.matmul(O[:, h * P:(h + 1) * P], dn_vo[a][:, h, :], dn_qk[a][p % 2][:, h, :],
                                                    start=False, stop=(h == 3), skip_group_check=True)
                        last.then_inc(o_mm[a], 1)

            def beside_first_inverse(n):
                if n == 0:
                    pe.wait_ge(sq_ready, 2)
                    for k in range(KD):
                        last = nc.tensor.matmul(ps[:, 6, 0:TOK], mask("ones"), y_sq[:, k, :], start=(k == 0), stop=(k == KD - 1))
                    last.then_inc(stat_ready, 1)
                elif n == 2:
                    ada_columns(1, mod_row1)
                elif n == 4:
                    ada_columns(2, mod_row2)

            pe.wait_ge(kvt_ready, 2 * TT)
            dn_rounds(chunk_step, inverse_step)
            def out_products(b, ks):
                for k in ks:
                    if k >= KD:
                        pe.wait_ge(o_ready, k - KD + 1)
                    load = LOAD_OUT + 2 * (b // 4) + k // KD
                    last = nc.tensor.matmul(ps[:, 4 + b % 2, 0:TOK], slots[slot_of[load]][:, k % KD, (b % 4) * P:(b % 4 + 1) * P], mix[:, k, :],
                                            start=(k == 0), stop=(k == 2 * KD - 1))
                return last

            ready(LOAD_OUT)
            pe.wait_ge(ynorm_ready, KD)
            for i in range(KD):
                pe.wait_ge(o_sq, i + 1)
                nc.tensor.matmul(ps[:, i % 2, 0:TOK], mask("ones"), o_sq_t[:, i % 2, :], start=True, stop=True).then_inc(o_sum, 1)
                out_products(i // 4, (2 * (i % 4), 2 * (i % 4) + 1))

            def square_sum(b):
                pe.wait_ge(sq_ready, 3 + b)
                nc.tensor.matmul(ps[:, 2, 0:TOK], mask("ones"), v_t[:, b, :], start=(b == 0), stop=(b == KD - 1)).then_inc(stat_ready, 1)

            for b in range(KD):
                if b % 4 == 0:
                    ready(LOAD_OUT + b // 2)
                    ready(LOAD_OUT + b // 2 + 1)
                if b >= 2:
                    pe.wait_ge(x1_ready, b - 1)
                out_products(b, range(KD if b < 2 else 0, 2 * KD)).then_inc(out_mm, 1)
                if b:
                    square_sum(b - 1)
            square_sum(KD - 1)
            pe.wait_ge(router_in, 16)
            for n, k in enumerate((0, 4, 1, 5, 2, 6, 3, 7)):
                pe.wait_ge(h2_ready[k // 4], k % 4 + 1)
                for t in range(TT):
                    last = nc.tensor.matmul(ps[:, 5 + t, 0:N_ROUTE], h2_t[:, k, t * P:(t + 1) * P], router_sb[:, k, :],
                                            start=(n == 0), stop=(n == KD - 1))
            last.then_inc(lg_mm, 1)
            for t in range(TT):
                if t:
                    pe.wait_ge(h2t_ready, t)
                for b in range(KD):
                    last = nc.tensor.transpose(ps[:, 3 + b // 4, (b % 4) * P:(b % 4 + 1) * P], h2_t[:, b, t * P:(t + 1) * P], mask("ident"))
                last.then_inc(h2t_mm, 1)
            pe.wait_ge(any_ready, 1)
            for t in range(TT + 1):
                for u in range(min(t + 1, TT)):
                    last = nc.tensor.matmul(ps[:, 7, t * N_EXPERTS:(t + 1) * N_EXPERTS], mask("strict_up" if u == t else "ones"), any_e[:, u, :],
                                            start=(u == 0), stop=(u == min(t, TT - 1)))
            last.then_inc(rank_mm, 1)
            for t in range(TT):
                if t:
                    pe.wait_ge(x1t_ready, t)
                for b in range(KD):
                    last = nc.tensor.transpose(ps[:, 5 + b // 4, (b % 4) * P:(b % 4 + 1) * P], x1_t[:, b, t * P:(t + 1) * P], mask("ident"))
                last.then_inc(x1t_mm, 1)
            pe.wait_ge(sel_ready, 1)
            for j in range(NPAIR):
                for t in range(TT):
                    last = nc.tensor.matmul(ps[:, 0, 8 * j:8 * j + 6], sel[:, t, 2 * j:2 * j + 2, :].rearrange("p e c -> p (e c)"),
                                            tg[:, t, j, :], start=(t == 0), stop=(t == TT - 1))
            last.then_inc(info_mm, 1)
            pe.wait_ge(x1t_ready, TT)
            for i in range(2):
                for k in range(KD):
                    last = nc.tensor.matmul(ps[:, 2 + 2 * i + k // 4, (k % 4) * P:(k % 4 + 1) * P],
                                            mod[:, 5 * KD + k, i:i + 1].to_broadcast([P, P]), mask("ident"), start=True, stop=True)
            last.then_inc(rows_mm, 1)
            def turn_rows(i):
                pe.wait_ge(xg_in, i * 16 + 16)
                for b in range(KD):
                    last = nc.tensor.transpose(ps[:, b // 4, (b % 4) * P:(b % 4 + 1) * P], xg[:, b * P:(b + 1) * P], mask("ident"))
                last.then_inc(xgt_mm, 1)

            def expert_pair(i, more):
                pe.wait_ge(xgt_ready, i * 2 + 2)
                for n, done_sem in ((0, gate_mm), (1, up_mm)):
                    for e in range(2):
                        pe.wait_ge(slot_in[2 * n + e], i * 16 + 16 * (n_loads[2 * n + e] + 1))
                    for k in range(KD):
                        for e in range(2):
                            last = nc.tensor.matmul(ps[64 * e:64 * e + 64, 2 + n, :], xg_t[:, k, 64 * e:64 * e + 64], slots[2 * n + e][:, k, :],
                                                    start=(k == 0), stop=(k == KD - 1), tile_position=(0, 64 * e))
                    last.then_inc(done_sem, 1)
                if more:
                    turn_rows(i + 1)
                pe.wait_ge(hact_ready, i + 1)
                for f in range(FK):
                    last = nc.tensor.transpose(ps[:, 4, f * P:(f + 1) * P], e_act[:, f * P:(f + 1) * P], mask("ident"))
                last.then_inc(at_mm, 1)
                pe.wait_ge(at_ready, i + 1)
                for e in range(2):
                    pe.wait_ge(slot_in[4 + e], i * 16 + 16 * (n_loads[4 + e] + 1))
                for n in range(2):
                    for f in range(FK):
                        for e in range(2):
                            last = nc.tensor.matmul(ps[64 * e:64 * e + 64, 5 + n, :], e_act_t[:, f, 64 * e:64 * e + 64],
                                                    down[4 + e][:, f, n * 512:(n + 1) * 512], start=(f == 0), stop=(f == FK - 1),
                                                    tile_position=(0, 64 * e))
                last.then_inc(down_mm, 1)
                pe.wait_ge(y_half, i * 2 + 2)
                for m in range(2 * TT):
                    t, n = m // 2, m % 2
                    pe.wait_ge(acc_added, i * 6 + m + 1)
                    nc.tensor.matmul(ps[:, (7, 4)[n], :], sel_t[:, t * P:(t + 1) * P], e_y[:, n * 512:(n + 1) * 512],
                                     start=True, stop=True).then_inc(spread_mm, 1)

            pe.wait_ge(slots_ready, 1)
            turn_rows(0)
            pe.wait_ge(rows_ready, 1)
            with pe.Fori(0, NPAIR - 1) as i:
                expert_pair(i, True)
            expert_pair(NPAIR - 1, False)

            with pe.If(more_than_cap(pe)):
                with pe.Fori(0, N_EXPERTS) as e:
                    for t in range(TT):
                        if t == 0:
                            pe.wait_ge(rest_in[0], e * 16 + 16)
                            pe.wait_ge(rest_in[1], e * 16 + 16)
                        for n in range(2):
                            for k in range(KD):
                                last = nc.tensor.matmul(ps[:, n, :], h2_t[:, k, t * P:(t + 1) * P], slots[n][:, k, :], start=(k == 0), stop=(k == KD - 1))
                        last.then_inc(rest_up_mm, 1)
                        pe.wait_ge(rest_act, e * TT + t + 1)
                        for f in range(FK):
                            last = nc.tensor.transpose(ps[:, 2, f * P:(f + 1) * P], e_act[:, f * P:(f + 1) * P], mask("ident"))
                        last.then_inc(rest_at_mm, 1)
                        if t == 0:
                            pe.wait_ge(rest_in[2], e * 16 + 16)
                        pe.wait_ge(rest_at, e * TT + t + 1)
                        pe.wait_ge(rest_added, e * TT + t + 1)
                        for n in range(2):
                            for f in range(FK):
                                last = nc.tensor.matmul(ps[:, 3 + n, :], e_act_t[:, f, :], down[2][:, f, n * 512:(n + 1) * 512],
                                                        start=(f == 0), stop=(f == FK - 1))
                        last.then_inc(rest_down_mm, 1)

        @block.scalar
        def _(act):
            steps = [0]

            def link(ins):
                steps[0] += 1
                ins.then_inc(act_step, 1)
                act.wait_ge(act_step, steps[0])

            def rsqrt(out, in_, scale, tmp):
                link(nc.scalar.activation(tmp, in_, ACT.Ln, bias=eps_col, scale=scale))
                return nc.scalar.activation(out, tmp, ACT.Exp, scale=-0.5)

            def ada_rows(g, bank, rows):
                act.wait_ge(ada_mm, g + 1)
                nc.scalar.copy(rows, ps[:, bank, :]).then_inc(row_ready, 1)

            act.wait_ge(pc_in, 16)
            act.wait_ge(silu_zero, 1)
            nc.scalar.activation(silu_c[:, :, 0:2], cols("c").rearrange("p (k c) -> p k c", c=2), ACT.Silu).then_inc(silu_ready, 1)
            act.wait_ge(x_ready, 1)
            eps_col = col("eps")
            nc.scalar.preload_act_table_set("natural_log_exp_and_others")
            nc.scalar.activation(v_t[:, :, :], x0_t[:, :, :], ACT.Square).then_inc(sq_ready, 1)
            act.wait_ge(stat_ready, 1)
            rsqrt(rs1, ps[:, 1, 0:TOK], 1.0 / D_MODEL, rs1).then_inc(rs_ready, 1)
            ada_rows(0, 0, mod_row)

            def hi_part(n):
                load, c = blocks[n][:2]
                if c == 0:
                    act.wait_ge(slot_in[slot_of[load]], 16 * arrivals(load))
                nc.scalar.copy(w_split[:, n % 4, 0, :, :], slots[slot_of[load]][:, :, c:c + P]).then_inc(hi_ready, 1)

            AHEAD = 3
            for n in range(AHEAD):
                hi_part(n)
            for k in range(KD):
                act.wait_ge(h1_full, k + 1)
                nc.scalar.copy(h1_hi[:, k, :], h1_t[:, k, :]).then_inc(h1_hi_ready, 1)

            def norm(i):
                act.wait_ge(qk_sum, i + 1)
                if i >= 2:
                    act.wait_ge(qk_ready, i - 1)
                rsqrt(rs[:, i % 2, :], ps[:, i % 2, 0:TOK], 1.0, rs[:, i % 2, :]).then_inc(qk_rs, 1)

            def conv_silu(i):
                act.wait_ge(conv_done, i + 1)
                dest = conv_dest(i)
                if i == 10 + 2 * KD:
                    act.wait_ge(tok_mm, 1)
                nc.scalar.activation(dest[:, 0:SEQ], conv_acc[:, i % 2, 0:SEQ], ACT.Silu)
                nc.scalar.activation(dest[:, SEQ:TOK], conv_acc[:, i % 2, SEQ + 4:TOK + 4], ACT.Silu).then_inc(conv_out, 1)

            for n, (load, c, kind, i) in enumerate(blocks):
                act.wait_ge(block_mm, n + 1)
                if n + AHEAD < NB:
                    hi_part(n + AHEAD)
                bank = 2 + n % 3
                if kind == "conv":
                    if i >= 2:
                        act.wait_ge(conv_done, i - 1)
                    nc.scalar.copy(pad[:, i % 2, 2:2 + SEQ], ps[:, bank, 0:SEQ])
                    nc.scalar.copy(pad[:, i % 2, SEQ + 6:TOK + 6], ps[:, bank, SEQ:TOK]).then_inc(block_out, 1)
                    if i:
                        conv_silu(i - 1)
                else:
                    nc.scalar.copy(mix[:, i, :], ps[:, bank, 0:TOK]).then_inc(block_out, 1)
                    if i == 0:
                        conv_silu(CONV_BLOCKS - 1)
                    elif i == 1:
                        act.wait_ge(na_ready, 1)
                        nc.scalar.preload_act_table_set("natural_log_exp_and_others")
                        nc.scalar.activation(sg[:, 2, :, :], sg[:, 1, :, :], ACT.Exp)
                        nc.scalar.activation(g_beta, ps[:, 5, 0:192].rearrange("p (t c) -> p t c", t=TT)[:, :, 48:64], ACT.Exp, scale=-1.0)
                        link(nc.scalar.activation(sg[:, 4, 0, :], cols("a_log"), ACT.Exp))
                        nc.scalar.activation(sg[:, 3, :, :], sg[:, 2, :, :], ACT.Ln, bias=1.0).then_inc(ln_ready, 1)
                    else:
                        norm(i - 2)
                        if i == 4:
                            act.wait_ge(cum_ready, 1)
                            nc.scalar.activation(sg[:, 0, :, :], sg[:, 1, :, :], ACT.Exp)
                            nc.scalar.activation(g_nec, cums[:, :, 32:48], ACT.Exp)
                            nc.scalar.activation(g_tot, cums[:, :, 48:128], ACT.Exp).then_inc(exps_ready, 1)

            norm(2 * KD - 2)
            norm(2 * KD - 1)

            for t in range(TT):
                act.wait_ge(xt_mm, t + 1)
                nc.scalar.copy(x_tok[:, t, 0:512], ps[:, 2, :])
                nc.scalar.copy(x_tok[:, t, 512:1024], ps[:, 3, :])
                nc.scalar.copy(b_tok[:, t, :], ps[:, 4, 0:P]).then_inc(xt_ready, 1)
            act.wait_ge(block_out, NB)
            nc.scalar.activation(mix[:, :, :], mix[:, :, :], ACT.Silu).then_inc(z_ready, 1)
            nc.scalar.preload_act_table_set("natural_log_exp_and_others")
            for n, (t, u) in enumerate(SSD_UNITS):
                g = u // 2
                if 1 <= n <= 2:
                    act.wait_ge(st_mm, n)
                    nc.scalar.copy(st_stage[:, n - 1, :, :], ps[:, 5, :].rearrange("p (b n) -> p b n", b=KD)).then_inc(st_out, 1)
                if n == 4:
                    act.wait_ge(st_mm, 4)
                act.wait_ge(seg_ready, n + 1)
                if t:
                    if n >= 2:
                        act.wait_ge(y_mm, n - 1)
                    for d in range(2):
                        nc.scalar.activation(c_dec[64 * g:64 * g + 64, n % 2, d, :, :],
                                             ps[64 * g:64 * g + 64, 2 * (n % 2) + d, :].rearrange("p (h i) -> p h i", h=4), ACT.Exp)
                nc.scalar.activation(seg[n % 3], seg[n % 3], ACT.Exp).then_inc(dec_ready, 1)
            for t in range(TT):
                act.wait_ge(kvt_mm, t + 1)
                for b in range(2):
                    last = nc.scalar.copy(k_tok[:, t, b * 512:(b + 1) * 512], ps[:, b, :])
                last.then_inc(kvt_ready, 1)
                if t == 0:
                    ada_rows(1, 5, mod_row1)
            act.wait_ge(states_out, 32)
            nc.scalar.activation(y_sq, mix[:, 0:KD, :], ACT.Square).then_inc(sq_ready, 1)
            ada_rows(2, 4, mod_row2)

            def inverse_step(p, n):
                for a in range(2):
                    A = ps[:, bank_a[a], :].rearrange("p (h i) -> p h i", h=4)
                    if n == 0:
                        act.wait_ge(dseg_ready[a], p + 1)
                        nc.scalar.activation(dn_m[a], dn_m[a], ACT.Exp).then_inc(dec_exp[a], 1)
                        if p >= 2:
                            act.wait_ge(o_mm[a], p - 1)
                        nc.scalar.activation(dn_e[a][p % 2], A, ACT.Exp).then_inc(dec_exp[a], 1)
                    elif n >= 3 and n % 2:
                        act.wait_ge(lev_mm1[a], 6 * p + (n - 1) // 2 + 1)
                        nc.scalar.copy(dn_p[a], A).then_inc(lev_p[a], 1)
                if p == 0 and n == 3:
                    act.wait_ge(stat_ready, 2)
                    rsqrt(y_rs, ps[:, 6, 0:TOK], 1.0 / SSD_WIDTH, y_rs).then_inc(rs_ready, 1)

            def chunk_step(p, n):
                hq, kind, tile = dn_pair(p)
                for a in range(2):
                    if n == 6 and not LAST_DIR_ADDS[kind][a]:
                        act.wait_ge(o_mm[a], p + 1)
                        nc.scalar.copy(o_t[:, 4 * hq:4 * hq + 4, tile[a] * P:(tile[a] + 1) * P],
                                       ps[:, bank_o[a], :].rearrange("p (h i) -> p h i", h=4)).then_inc(o_out[a], 1)

            dn_rounds(chunk_step, inverse_step)
            for i in range(KD):
                if i == 0:
                    for a in range(2):
                        act.wait_ge(o_out[a], len(PAIRS))
                if i >= 2:
                    act.wait_ge(o_sum, i - 1)
                nc.scalar.activation(o_sq_t[:, i % 2, :], o_t[:, i, :], ACT.Square).then_inc(o_sq, 1)
                if i:
                    def o_norm(i):
                        act.wait_ge(o_sum, i + 1)
                        if i >= 2:
                            act.wait_ge(o_ready, i - 1)
                        rsqrt(o_rs_t[:, i % 2, :], ps[:, i % 2, 0:TOK], 1.0 / DN_HEAD_DIM, o_rs_t[:, i % 2, :]).then_inc(o_rs, 1)
                    o_norm(i - 1)
            o_norm(KD - 1)

            act.wait_ge(o_ready, KD)
            for b in range(KD):
                act.wait_ge(x1_ready, b + 1)
                nc.scalar.activation(v_t[:, b, :], x1_t[:, b, :], ACT.Square).then_inc(sq_ready, 1)
            act.wait_ge(stat_ready, 2 + KD)
            rsqrt(rs2, ps[:, 2, 0:TOK], 1.0 / D_MODEL, rs2).then_inc(rs_ready, 1)
            for k in range(4, KD):
                act.wait_ge(h2_scaled, k - 3)
                for c, (lo, hi) in enumerate(SEGS):
                    last = nc.scalar.activation(h2_t[:, k, lo:hi], h2_t[:, k, lo:hi], ACT.Identity, bias=mod[:, 3 * KD + k, c:c + 1],
                                                scale=amp2[:, k, c:c + 1])
                last.then_inc(h2_ready[1], 1)
            for t in range(TT):
                act.wait_ge(h2t_mm, t + 1)
                nc.scalar.copy(h2_tok[:, t, 0:512], ps[:, 3, :])
                nc.scalar.copy(h2_tok[:, t, 512:1024], ps[:, 4, :]).then_inc(h2t_ready, 1)
                if t == 0:
                    act.wait_ge(gd_ready, 1)
                    nc.scalar.activation(g_exp, g_exp, ACT.Exp).then_inc(gexp_ready, 1)
                elif t == 1:
                    act.wait_ge(gd_ready, 2)
                    nc.scalar.activation(e_p2, e_p2, ACT.Exp).then_inc(gexp_ready, 1)
            for t in range(TT):
                act.wait_ge(x1t_mm, t + 1)
                nc.scalar.copy(x1_tok[:, t, 0:512], ps[:, 5, :])
                nc.scalar.copy(x1_tok[:, t, 512:1024], ps[:, 6, :]).then_inc(x1t_ready, 1)
            act.wait_ge(rows_mm, 1)
            for i in range(2):
                for n in range(2):
                    last = nc.scalar.copy(gt2_row[:, i, n * 512:(n + 1) * 512], ps[:, 2 + 2 * i + n, :])
            last.then_inc(rows_ready, 1)
            def turned_half(i):
                act.wait_ge(xgt_mm, i + 1)
                nc.scalar.copy(xg_t[:, 4:8, :], ps[:, 1, :].rearrange("p (k i) -> p k i", k=4)).then_inc(xgt_ready, 1)

            def expert_pair(i, more):
                act.wait_ge(gate_mm, i + 1)
                nc.scalar.activation(e_silu, ps[:, 2, :], ACT.Silu).then_inc(silu_done, 1)
                if more:
                    turned_half(i + 1)
                act.wait_ge(at_mm, i + 1)
                nc.scalar.copy(e_act_t, ps[:, 4, :].rearrange("p (f i) -> p f i", f=FK)).then_inc(at_ready, 1)
                act.wait_ge(down_mm, i + 1)
                nc.scalar.copy(e_y[:, 512:1024], ps[:, 6, :]).then_inc(y_half, 1)

            turned_half(0)
            with act.Fori(0, NPAIR - 1) as i:
                expert_pair(i, True)
            expert_pair(NPAIR - 1, False)
            with act.If(more_than_cap(act)):
                with act.Fori(0, N_EXPERTS) as e:
                    for t in range(TT):
                        act.wait_ge(rest_up_mm, e * TT + t + 1)
                        nc.scalar.activation(e_silu, ps[:, 0, :], ACT.Silu).then_inc(rest_silu, 1)
                        act.wait_ge(rest_at_mm, e * TT + t + 1)
                        nc.scalar.copy(e_act_t, ps[:, 2, :].rearrange("p (f i) -> p f i", f=FK)).then_inc(rest_at, 1)
            nc.scalar.preload_act_table_set("natural_log_exp_and_others")
            for t in range(TT):
                act.wait_ge(x2_ready, t + 1)
                link(nc.scalar.activation(x2_sq, y_acc[:, t, :], ACT.Square, accum_out=ss[:, t:t + 1]))
                rsqrt(ss[:, 4 + t:5 + t], ss[:, t:t + 1], 1.0 / D_MODEL, ss[:, t:t + 1]).then_inc(x2_rs, 1)

        @block.vector
        def _(dve):
            steps = [0]

            def link(ins):
                steps[0] += 1
                ins.then_inc(dve_step, 1)
                dve.wait_ge(dve_step, steps[0])

            V = nc.vector
            V.memset(silu_c[:, :, :], 0.0).then_inc(silu_zero, 1)
            link(V.memset(pad, 0.0))
            dve.wait_ge(x_in, 48)
            V.tensor_tensor(x0_t[:, :, SEQ:TOK], x0_t[:, :, SEQ:TOK], k_t[:, :, 0:DEC_SEQ], ALU.add).then_inc(x_ready, 1)
            dve.wait_ge(pc_in, 16)
            dve.wait_ge(rs_ready, 1)
            link(V.tensor_tensor(h1_t, x0_t[:, :, :], rs1.unsqueeze(1).to_broadcast([P, KD, TOK]), ALU.mult))

            def mod_columns(g):
                dve.wait_ge(modp_ready, g + 1)
                b_ada = cols("b_ada")[:, 16 * g:16 * g + 16].rearrange("p (j b) -> p j b", j=4)
                for c in range(2):
                    last = V.tensor_tensor(mod[:, 16 * g:16 * g + 16, c].rearrange("p (j b) -> p j b", j=4),
                                           ps[:, 7, :].rearrange("p (b j r) -> p j b r", b=4, j=4)[:, :, :, c], b_ada, ALU.add)
                return last

            mod_columns(0).then_inc(mod_ready, 1)
            dve.wait_ge(mod_ready, 1)
            link(V.scalar_tensor_tensor(amp1[:, :, :], mod[:, KD:2 * KD, :], 1.0, cols("norm1").unsqueeze(2).to_broadcast([P, KD, 2]), ALU.add, ALU.mult))
            for k in range(KD):
                for c, (a, b) in enumerate(SEGS):
                    last = V.tensor_scalar(h1_t[:, k, a:b], h1_t[:, k, a:b], amp1[:, k, c:c + 1], mod[:, k, c:c + 1], ALU.mult, ALU.add)
                last.then_inc(h1_full, 1)
            for k in range(KD):
                dve.wait_ge(h1_hi_ready, k + 1)
                V.tensor_tensor(h1_lo[:, k, :], h1_t[:, k, :], h1_hi[:, k, :].bitcast(fp32), ALU.subtract).then_inc(h1_ready, 1)

            W5 = TOK + 4
            for i in range(CONV_BLOCKS):
                dve.wait_ge(block_out, i + 1)
                if i >= 2:
                    dve.wait_ge(conv_out, i - 1)
                c_acc, row = conv_acc[:, i % 2, :], pad[:, i % 2, :]
                link(V.tensor_scalar(c_acc, row[:, 0:W5], col("conv_w", CONV_W * i), col("conv_b", i), ALU.mult, ALU.add))
                for j in range(1, CONV_W):
                    ins = V.scalar_tensor_tensor(c_acc, row[:, j:j + W5], col("conv_w", CONV_W * i + j), c_acc, ALU.mult, ALU.add)
                    if j < CONV_W - 1:
                        link(ins)
                ins.then_inc(conv_done, 1)

            def square(i):
                if i >= 2:
                    dve.wait_ge(qk_sum, i - 1)
                x = (q_t, k_t)[i // KD][:, i % KD, :]
                V.tensor_tensor(sq[:, i % 2, :], x, x, ALU.mult).then_inc(qk_sq, 1)

            def scale(i):
                dve.wait_ge(qk_rs, i + 1)
                x = (q_t, k_t)[i // KD][:, i % KD, :]
                V.scalar_tensor_tensor(x, x, (DN_HEAD_DIM ** -0.5, 1.0)[i // KD], rs[:, i % 2, :], ALU.mult, ALU.mult).then_inc(qk_ready, 1)

            dve.wait_ge(conv_out, CONV_BLOCKS - 1)
            square(0)
            square(1)
            dve.wait_ge(tok_mm, 1)
            gp = ps[:, 5, 0:192].rearrange("p (t c) -> p t c", t=TT)
            link(V.tensor_tensor(sg[:, 0, :, :], gp[:, :, 0:48], cols("gate_bias").unsqueeze(1).to_broadcast([P, TT, 48]), ALU.add))
            V.scalar_tensor_tensor(sg[:, 1, :, :], sg[:, 0, :, :], -1.0, sg[:, 0, :, :], ALU.mult, ALU.min).then_inc(na_ready, 1)
            dve.wait_ge(ln_ready, 1)
            link(V.scalar_tensor_tensor(sg[:, 5, :, :], sg[:, 0, :, :], 0.0, sg[:, 3, :, :], ALU.max, ALU.add))
            V.tensor_copy(g_dt, sg[:, 5, :, 0:32])
            V.scalar_tensor_tensor(g_log, sg[:, 5, :, :], -1.0, sg[:, 4, 0:1, :].to_broadcast([P, TT, 48]), ALU.mult, ALU.mult).then_inc(log_ready, 1)
            link(V.tensor_scalar(g_beta, g_beta, 1.0, None, ALU.add))
            link(V.reciprocal(g_beta, g_beta))
            square(2)
            scale(0)
            square(3)
            scale(1)
            dve.wait_ge(cum_mm, 1)
            link(V.tensor_copy(cums[:, :, :], ps[:, 6, 0:TT * P].rearrange("p (t c) -> p t c", t=TT)))
            V.tensor_tensor(sg[:, 1, :, :], cums[:, :, 48:96], cums[:, :, 0:48], ALU.subtract).then_inc(cum_ready, 1)
            square(4)
            scale(2)
            dve.wait_ge(exps_ready, 1)
            V.tensor_tensor(g_dte, g_dt, sg[:, 0, :, 0:32], ALU.mult)
            V.tensor_tensor(g_be, g_beta, sg[:, 0, :, 32:48], ALU.mult)
            link(V.tensor_scalar(g_nec, g_nec, -1.0, None, ALU.mult))
            for i in range(5, 2 * KD):
                if i == 2 * KD - 1:
                    dve.wait_ge(conv_out, CONV_BLOCKS)
                square(i)
                scale(i - 2)
            scale(2 * KD - 2)
            scale(2 * KD - 1)

            def to_end(i):
                t, d = ENDS[i]
                dve.wait_ge(xt_ready, t + 1)
                if i >= 2:
                    dve.wait_ge(st_mm, i - 1)
                V.tensor_tensor(x_end[:, i % 2, :].rearrange("p (h c) -> p h c", c=64), x_tok[:, t, :].rearrange("p (h c) -> p h c", c=64),
                                g_dte[:, t, 16 * d:16 * d + 16].unsqueeze(2).to_broadcast([P, 16, 64]), ALU.mult).then_inc(xe_ready, 1)

            def second_start(d):
                dve.wait_ge(h0_in, 32)
                for g in range(2):
                    sl = slice(64 * g, 64 * g + 64)
                    last = V.tensor_tensor(h_st[sl, 2 * d + 1, :].rearrange("p (h c) -> p h c", c=64), h_st[sl, 2 * d, :].rearrange("p (h c) -> p h c", c=64),
                                           g_tot[sl, 1 + d, 16 * d + 8 * g:16 * d + 8 * g + 8].unsqueeze(2).to_broadcast([64, 8, 64]), ALU.mult)
                link(last)
                dve.wait_ge(st_mm, 3 + d)
                V.tensor_tensor(h_st[:, 2 * d + 1, :], h_st[:, 2 * d + 1, :], ps[:, 5, :], ALU.add).then_inc(h_ready, 1)

            def seg_part(n):
                t, u = SSD_UNITS[n]
                dve.wait_ge(seg_mm, n + 1)
                if n >= 3:
                    dve.wait_ge(y_mm, n - 2)
                for d in range(2):
                    for h in range(4):
                        hh = 16 * d + 4 * u + h
                        last = V.tensor_scalar(seg[n % 3][:, d, h, :], ps[:, 2 * (n % 2) + d, h * P:(h + 1) * P], cums[:, t, hh:hh + 1], 0.0,
                                               ALU.subtract, ALU.min)
                last.then_inc(seg_ready, 1)

            def m_part(n):
                t, u = SSD_UNITS[n]
                g = u // 2
                if u == 0:
                    dve.wait_ge(cb_mm, t + 1)
                    for d in range(2):
                        last = V.tensor_tensor(cbm[:, d, :, :], ps[:, 6:8, 0:P],
                                               mask(("upper", "lower")[d]).unsqueeze(1).to_broadcast([P, 2, P]), ALU.mult)
                    last.then_inc(cb_ready, 1)
                    dve.wait_ge(cb_ready, t + 1)
                dve.wait_ge(dec_ready, n + 1)
                for d in range(2):
                    for h in range(4):
                        hh = 16 * d + 4 * u + h
                        last = V.scalar_tensor_tensor(seg[n % 3][:, d, h, :], seg[n % 3][:, d, h, :], g_dt[:, t, hh:hh + 1], cbm[:, d, g, :],
                                                      ALU.mult, ALU.mult)
                last.then_inc(ssd_m_ready, 1)

            def y_out(n):
                t, u = SSD_UNITS[n]
                dve.wait_ge(y_mm, n + 1)
                if n >= 2:
                    dve.wait_ge(y_ready, n - 1)
                for b in range(2):
                    last = V.scalar_tensor_tensor(y_tmp[:, n % 2, b, :], x_ssd[:, 2 * u + b, t * P:(t + 1) * P], col("ssd_d", 2 * u + b),
                                                  ps[:, 4, b * P:(b + 1) * P], ALU.mult, ALU.add)
                link(last)
                if n == 0:
                    dve.wait_ge(z_ready, 1)
                V.tensor_tensor(mix[:, 2 * u:2 * u + 2, t * P:(t + 1) * P], mix[:, 2 * u:2 * u + 2, t * P:(t + 1) * P], y_tmp[:, n % 2, :, :],
                                ALU.mult).then_inc(y_ready, 1)

            dve.wait_ge(qk_ready, 2 * KD)
            seg_part(0)
            to_end(0)
            to_end(1)
            for n in range(len(SSD_UNITS)):
                if n + 1 < len(SSD_UNITS):
                    seg_part(n + 1)
                m_part(n)
                if n < 2:
                    to_end(2 + n)
                elif n < 4:
                    second_start(n - 2)
                if n:
                    y_out(n - 1)
            y_out(len(SSD_UNITS) - 1)
            def zero_states():
                V.memset(dn_s[:, 0, :, :], 0.0).then_inc(s_zero, 1)

            for t in range(TT):
                dve.wait_ge(kvt_mm, t + 1)
                V.tensor_copy(v_tok[:, t, :], ps[:, 2:4, :].rearrange("p b i -> p (b i)")).then_inc(kvt_ready, 1)
            dve.wait_ge(states_out, 32)
            zero_states()
            ident4 = mask("ident").unsqueeze(1).to_broadcast([P, 4, P])
            heads = lambda bank: ps[:, bank, :].rearrange("p (h i) -> p h i", h=4)

            def inverse_step(p, n):
                hq, kind, tile = dn_pair(p)
                if n == 0:
                    for a in range(2):
                        dve.wait_ge(dseg_mm[a], 2 * p + 1)
                        if p:
                            dve.wait_ge(off_ready[a], 5 * p)
                        for h in range(4):
                            c = 32 + 8 * a + 4 * hq + h
                            last = V.tensor_scalar(dn_m[a][:, h, :], ps[:, bank_a[a], h * P:(h + 1) * P], cums[:, tile[a], c:c + 1], 0.0,
                                                   ALU.subtract, ALU.min)
                        last.then_inc(dseg_ready[a], 1)
                    for a in range(2):
                        dve.wait_ge(dec_exp[a], 2 * p + 1)
                        if p >= 2:
                            dve.wait_ge(o_mm[a], p - 1)
                        link(V.tensor_tensor(dn_qk[a][p % 2], dn_m[a], mask(("upper64", "lower64")[a]).unsqueeze(1).to_broadcast([P, 4, P]), ALU.mult))
                        dve.wait_ge(dseg_mm[a], 2 * p + 2)
                        for h in range(4):
                            b = 8 * a + 4 * hq + h
                            last = V.scalar_tensor_tensor(dn_m[a][:, h, :], ps[:, bank_b[a], h * P:(h + 1) * P], g_beta[:, tile[a], b:b + 1],
                                                          dn_qk[a][p % 2][:, h, :], ALU.mult, ALU.mult)
                        last.then_inc(m_ready[a], 1)
                        dve.wait_ge(m_ready[a], 2 * p + 1)
                        V.tensor_tensor(dn_off[a][0], dn_m[a], mask(f"lev{a}_1").unsqueeze(1).to_broadcast([P, 4, P]), ALU.mult).then_inc(m_ready[a], 1)
                elif n == 1:
                    for a in range(2):
                        dve.wait_ge(kq_mm[a], p + 1)
                        V.tensor_tensor(dn_qk[a][p % 2], dn_qk[a][p % 2], heads(bank_a[a]), ALU.mult).then_inc(d_ready[a], 1)
                elif n == 2:
                    for a in range(2):
                        dve.wait_ge(m_ready[a], 2 * p + 2)
                        V.tensor_tensor(dn_dt[a][p % 2], ident4, dn_off[a][0], ALU.subtract)
                        dve.wait_ge(lev_mm1[a], 6 * p + 1)
                        V.tensor_tensor(dn_d[a], ident4, heads(bank_a[a]), ALU.subtract).then_inc(d_ready[a], 1)
                    for a in range(2):
                        dve.wait_ge(dec_exp[a], 2 * p + 2)
                        V.tensor_tensor(dn_e[a][p % 2], dn_e[a][p % 2], q_t[:, 4 * hq:4 * hq + 4, tile[a] * P:(tile[a] + 1) * P], ALU.mult)
                if p == 0 and n in (2, 4):
                    mod_columns(n // 2).then_inc(mod_ready, 1)
                if n % 2 == 0 and n >= 4:
                    lev = (n - 2) // 2
                    for a in range(2):
                        dve.wait_ge(lev_mm2[a], 5 * p + lev)
                        if lev < 5:
                            V.tensor_tensor(dn_d[a], dn_d[a], heads(bank_a[a]), ALU.subtract)
                        V.tensor_tensor(dn_dt[a][p % 2], dn_dt[a][p % 2], heads(bank_b[a]), ALU.subtract).then_inc(d_ready[a], 1)
                if p == 0 and n in (6, 8, 10, 12):
                    dve.wait_ge(rs_ready, 2)
                    for k in range(n - 6, n - 4):
                        V.scalar_tensor_tensor(mix[:, k, :], mix[:, k, :], col("ssd_norm", k), y_rs, ALU.mult, ALU.mult).then_inc(ynorm_ready, 1)

            def chunk_step(p, n):
                hq, kind, tile = dn_pair(p)
                step = n // 3
                if p == 2 and n == 3:
                    dve.wait_ge(states_out, 64)
                    zero_states()
                for a in range(2):
                    t = tile[a]
                    c, rows = dn_rows(step, a)
                    b = 8 * a + 4 * hq
                    X = ps[:, bank_x[a], :]
                    if n in (0, 3):
                        dve.wait_ge(ks_mm[a], 2 * p + step + 1)
                        for h in range(4):
                            last = V.scalar_tensor_tensor(dn_r[a][rows, h, :], X[rows, h * P:(h + 1) * P], g_nec[rows, t, b + h:b + h + 1],
                                                          v_tok[rows, t, (4 * hq + h) * P:(4 * hq + h + 1) * P], ALU.mult, ALU.add)
                        last.then_inc(r_ready[a], 1)
                    elif n in (1, 4):
                        dve.wait_ge(vn_mm[a], 2 * p + step + 1)
                        if p:
                            dve.wait_ge(o_mm[a], p)
                        v = heads(bank_x[a])[rows, :, :]
                        V.tensor_tensor(dn_vb[a][rows, :, :], v, g_be[rows, t, b:b + 4].unsqueeze(2).to_broadcast([64, 4, P]), ALU.mult)
                        V.tensor_tensor(dn_vo[a][rows, :, :], v, g_beta[rows, t, b:b + 4].unsqueeze(2).to_broadcast([64, 4, P]), ALU.mult).then_inc(vn_ready[a], 1)
                    elif n in (2, 5):
                        dve.wait_ge(ds_mm[a], 2 * p + step + 1)
                        st = dn_s[:, min(kind, 1), a, :]
                        for h in range(4):
                            cd = 48 + 16 * c + b + h
                            last = V.scalar_tensor_tensor(st[:, h * P:(h + 1) * P], st[:, h * P:(h + 1) * P], g_tot[:, t, cd:cd + 1],
                                                          X[:, h * P:(h + 1) * P], ALU.mult, ALU.add)
                        last.then_inc(s_ready[a], 1)
                    elif n == 6 and LAST_DIR_ADDS[kind][a]:
                        dve.wait_ge(o_mm[a], p + 1)
                        dve.wait_ge(o_out[0], p + 1 if kind == 0 else p)
                        dve.wait_ge(o_out[1], p)
                        o = o_t[:, 4 * hq:4 * hq + 4, t * P:(t + 1) * P]
                        V.tensor_tensor(o, o, heads(bank_o[a]), ALU.add).then_inc(o_out[a], 1)

            dn_rounds(chunk_step, inverse_step)
            for i in range(KD):
                dve.wait_ge(o_rs, i + 1)
                link(V.scalar_tensor_tensor(o_t[:, i, :], o_t[:, i, :], col("dn_norm"), o_rs_t[:, i % 2, :], ALU.mult, ALU.mult))
                V.tensor_tensor(mix[:, KD + i, :], mix[:, KD + i, :], o_t[:, i, :], ALU.mult).then_inc(o_ready, 1)
            V.scalar_tensor_tensor(amp2[:, :, :], mod[:, 4 * KD:5 * KD, :], 1.0, cols("norm2").unsqueeze(2).to_broadcast([P, KD, 2]), ALU.add,
                                   ALU.mult)
            dve.wait_ge(x_in, 96)
            V.tensor_tensor(x0_t[:, :, SEQ:TOK], x0_t[:, :, SEQ:TOK], k_t[:, :, 0:DEC_SEQ], ALU.add).then_inc(x_ready, 1)
            dve.wait_ge(x_ready, 2)
            for b in range(KD):
                dve.wait_ge(out_mm, b + 1)
                for c, (lo, hi) in enumerate(SEGS):
                    last = V.scalar_tensor_tensor(x1_t[:, b, lo:hi], ps[:, 4 + b % 2, lo:hi], mod[:, 2 * KD + b, c:c + 1], x0_t[:, b, lo:hi], ALU.mult, ALU.add)
                last.then_inc(x1_ready, 1)
            dve.wait_ge(x1_ready, KD)
            dve.wait_ge(rs_ready, 3)
            link(V.tensor_tensor(h2_t[:, 0:4, :], x1_t[:, 0:4, :], rs2.unsqueeze(1).to_broadcast([P, 4, TOK]), ALU.mult))
            for k in range(4):
                for c, (lo, hi) in enumerate(SEGS):
                    last = V.tensor_scalar(h2_t[:, k, lo:hi], h2_t[:, k, lo:hi], amp2[:, k, c:c + 1], mod[:, 3 * KD + k, c:c + 1], ALU.mult, ALU.add)
                last.then_inc(h2_ready[0], 1)
            AX = mybir.AxisListType.X
            desc8 = cols("desc8")
            wide = lambda v, n: v.to_broadcast([P, TT, n])

            def pick_first(out, values, top, n):
                d = desc8[:, 0:n].unsqueeze(1).to_broadcast([P, TT, n])
                link(V.tensor_tensor(e_eq[:, :, 0:n], values, wide(top, n), ALU.is_equal))
                link(V.tensor_tensor(e_eq[:, :, 0:n], e_eq[:, :, 0:n], d, ALU.mult))
                link(V.tensor_reduce(e_pick, e_eq[:, :, 0:n], AX, ALU.max))
                link(V.tensor_tensor(out, d, wide(e_pick, n), ALU.is_equal))

            dve.wait_ge(lg_mm, 1)
            link(V.tensor_tensor(lg, ps[:, 5:8, 0:N_ROUTE],
                                 cols("route_bias").unsqueeze(1).to_broadcast([P, TT, N_ROUTE]), ALU.add))
            link(V.tensor_reduce(gmax, lg[:, :, 0:4], AX, ALU.max))
            V.tensor_tensor(g_exp, lg[:, :, 0:4], wide(gmax, 4), ALU.subtract).then_inc(gd_ready, 1)
            pick_first(gpick, lg[:, :, 0:4], gmax, 4)
            ge = lambda v: v.rearrange("p t (g e) -> p t g e", g=N_GROUPS)
            of_g = lambda v: v.unsqueeze(3).to_broadcast([P, TT, N_GROUPS, PER_GROUP])
            of_e = lambda v: v.unsqueeze(2).to_broadcast([P, TT, N_GROUPS, PER_GROUP])
            link(V.tensor_tensor(ge(spread), ge(lg[:, :, 4:N_ROUTE]), of_g(gpick), ALU.mult))
            link(V.tensor_reduce(es, spread.rearrange("p t (g e) -> p t e g", g=N_GROUPS), AX, ALU.add))
            link(V.tensor_reduce(e_top[:, :, 0:1], es, AX, ALU.max))
            pick_first(pick1, es, e_top[:, :, 0:1], 8)
            link(V.scalar_tensor_tensor(es_rest, pick1, -1e30, es, ALU.mult, ALU.add))
            link(V.tensor_reduce(e_top[:, :, 1:2], es_rest, AX, ALU.max))
            V.tensor_tensor(e_p2, e_top[:, :, 1:2], e_top[:, :, 0:1], ALU.subtract).then_inc(gd_ready, 1)
            pick_first(pick2, es_rest, e_top[:, :, 1:2], 8)
            V.tensor_tensor(ge(a1), of_g(gpick), of_e(pick1), ALU.mult)
            link(V.tensor_tensor(ge(a2), of_g(gpick), of_e(pick2), ALU.mult))
            V.tensor_tensor(any_e, a1, a2, ALU.add).then_inc(any_ready, 1)
            dve.wait_ge(gexp_ready, 1)
            link(V.tensor_reduce(g_w, g_exp, AX, ALU.add))
            dve.wait_ge(gexp_ready, 2)
            link(V.scalar_tensor_tensor(g_w, e_p2, 1.0, g_w, ALU.add, ALU.mult))
            link(V.reciprocal(e_w1, g_w))
            link(V.tensor_tensor(e_w2, e_w1, e_p2, ALU.mult))
            V.tensor_tensor(wsum, pick1, wide(e_w1, 8), ALU.mult)
            link(V.tensor_tensor(es, pick2, wide(e_w2, 8), ALU.mult))
            link(V.tensor_tensor(wsum, wsum, es, ALU.add))
            link(V.tensor_tensor(ge(comb), of_g(gpick), of_e(wsum), ALU.mult))
            comb_jx = comb.rearrange("p t (j x) -> p t j x", x=2)
            tg_hi = tg[:, :, :, 1:5].rearrange("p t j (x y) -> p t j x y", y=2)
            link(V.tensor_copy(tg_hi[:, :, :, :, 0], comb_jx))
            V.tensor_tensor(tg_hi[:, :, :, :, 1], comb_jx, tg_hi[:, :, :, :, 0].bitcast(fp32), ALU.subtract)
            for x in (0, 5):
                V.tensor_copy(tg[:, :, :, x:x + 1], cols("tok_id").unsqueeze(2).unsqueeze(3).to_broadcast([P, TT, NPAIR, 1]))
            dve.wait_ge(rank_mm, 1)
            rp = ps[:, 7, 0:TT * N_EXPERTS].rearrange("p (t e) -> p t e", t=TT)
            V.tensor_copy(counts, ps[:, 7, TT * N_EXPERTS:(TT + 1) * N_EXPERTS])
            link(V.tensor_copy(rank, rp))
            link(V.scalar_tensor_tensor(rank_only, any_e, -1000.0, rank, ALU.mult, ALU.add))
            link(V.tensor_scalar(rank_only, rank_only, 1000.0, None, ALU.add))
            iota = masks_sb[:, MI["iota"], 0:CAP].unsqueeze(1).to_broadcast([P, N_EXPERTS, CAP])
            for t in range(TT):
                last = V.tensor_tensor(sel[:, t, :, :], iota, rank_only[:, t, :].unsqueeze(2).to_broadcast([P, N_EXPERTS, CAP]), ALU.is_equal)
            last.then_inc(sel_ready, 1)
            V.scalar_tensor_tensor(over, rank, float(CAP), comb, ALU.is_ge, ALU.mult)
            dve.wait_ge(info_mm, 1)
            link(V.tensor_copy(slot_info[:, :, :], ps[:, 0, 0:8 * NPAIR].rearrange("p (j x) -> p j x", x=8)[:, :, 0:5]))
            V.tensor_tensor(slot_gate[0:64, :], slot_info[0:64, :, 1], slot_info[0:64, :, 2], ALU.add)
            V.tensor_tensor(slot_gate[64:128, :], slot_info[64:128, :, 3], slot_info[64:128, :, 4], ALU.add)
            V.tensor_copy(slot_tok[:, :], slot_info[:, :, 0]).then_inc(slots_ready, 1)
            dve.wait_ge(slots_ready, 1)
            link(V.tensor_reduce(most_f, counts, AX, ALU.max))
            V.tensor_copy(most[:, 0:1], most_f).then_inc(most_ready, 1)

            def turned_half(i):
                dve.wait_ge(xgt_mm, i + 1)
                V.tensor_copy(xg_t[:, 0:4, :], ps[:, 0, :].rearrange("p (k i) -> p k i", k=4)).then_inc(xgt_ready, 1)

            def expert_pair(i, more):
                tok = slot_info[:, bass.ds(i, 1), 0] if more else slot_info[:, i, 0:1]
                gate = slot_gate[:, bass.ds(i, 1)] if more else slot_gate[:, i:i + 1]
                dve.wait_ge(gate_mm, i + 1)
                V.tensor_scalar(sel_t, iota_w, tok, None, ALU.is_equal)
                dve.wait_ge(up_mm, i + 1)
                dve.wait_ge(silu_done, i + 1)
                V.scalar_tensor_tensor(e_act, e_silu, gate, ps[:, 3, :], ALU.mult, ALU.mult).then_inc(hact_ready, 1)
                if more:
                    turned_half(i + 1)
                dve.wait_ge(down_mm, i + 1)
                V.tensor_copy(e_y[:, 0:512], ps[:, 5, :]).then_inc(y_half, 1)
                for m in range(2 * TT):
                    t, n = m // 2, m % 2
                    dve.wait_ge(spread_mm, i * 6 + m + 1)
                    a = y_acc[:, t, n * 512:(n + 1) * 512]
                    V.tensor_tensor(a, a, ps[:, (7, 4)[n], :], ALU.add).then_inc(acc_added, 1)

            turned_half(0)
            dve.wait_ge(h2_stored, 16 * TT)
            V.memset(y_acc, 0.0).then_inc(acc_added, 1)
            for t in range(TT):
                last = V.tensor_scalar(iota_w[:, t * P:(t + 1) * P], masks_sb[:, MI["iota"], :], float(t * P), None, ALU.add)
            last.then_inc(acc_added, 1)
            dve.wait_ge(acc_added, 2)
            with dve.Fori(0, NPAIR - 1) as i:
                expert_pair(i, True)
            expert_pair(NPAIR - 1, False)

            def finish(t):
                dve.wait_ge(x2_rs, t + 1)
                V.scalar_tensor_tensor(y_acc[:, t, :], y_acc[:, t, :], ss[:, 4 + t:5 + t], final_row, ALU.mult, ALU.mult).then_inc(out_ready, 1)

            with dve.If(more_than_cap(dve)):
                dve.sem_inc(rest_added, 1)
                with dve.Fori(0, N_EXPERTS) as e:
                    for t in range(TT):
                        dve.wait_ge(rest_silu, e * TT + t + 1)
                        V.scalar_tensor_tensor(e_act, e_silu, over[:, t, bass.ds(e, 1)], ps[:, 1, :], ALU.mult, ALU.mult).then_inc(rest_act, 1)
                        dve.wait_ge(rest_down_mm, e * TT + t + 1)
                        V.tensor_tensor(o_scaled, ps[:, 3:5, :].rearrange("p n d -> p (n d)"), gt2_row[:, min(t, 1), :], ALU.mult).then_inc(rest_scaled, 1)
                        dve.wait_ge(rest_scaled, e * TT + t + 1)
                        V.tensor_tensor(x1_tok[:, t, :], x1_tok[:, t, :], o_scaled, ALU.add).then_inc(rest_added, 1)

            for t in range(TT):
                link(V.tensor_tensor(y_acc[:, t, :], y_acc[:, t, :], gt2_row[:, min(t, 1), :], ALU.mult))
                V.tensor_tensor(y_acc[:, t, :], y_acc[:, t, :], x1_tok[:, t, :], ALU.add).then_inc(x2_ready, 1)
                if t == 1:
                    dve.wait_ge(pc_in, 32)
                if t:
                    finish(t - 1)
            finish(TT - 1)


def _masks():
    import numpy as np
    p, f = np.arange(P)[:, None], np.arange(P)[None, :]
    same = (p // 64) == (f // 64)
    out = {"ident": p == f, "ones": p >= 0 * f, "upper": p <= f, "lower": p >= f, "upper64": (p <= f) & same, "lower64": (p >= f) & same,
           "ones64": same, "first64": (p < 64) & (f >= 0), "last64": (p >= 64) & (f >= 0), "strict_up": p < f, "iota": f + 0 * p}
    for m in LEVELS:
        pair = (p // (2 * m)) == (f // (2 * m))
        p_odd, f_odd = (p // m) % 2 == 1, (f // m) % 2 == 1
        out[f"lev0_{m}"] = pair & ~p_odd & f_odd
        out[f"lev1_{m}"] = pair & p_odd & ~f_odd
    return np.ascontiguousarray(np.stack([out[n] for n in MASKS], 1), dtype=np.float32)


def _positions():
    import numpy as np
    quarter = D_MODEL // 4
    omega = (1.0 / (np.float32(10000.0) ** (np.arange(quarter, dtype=np.float32) / np.float32(quarter)))).astype(np.float32)
    n = np.arange(DEC_SEQ)
    ar = (n // 64).astype(np.float32)[:, None] * omega
    ac = (n % 64).astype(np.float32)[:, None] * omega
    return np.ascontiguousarray(np.concatenate([np.sin(ar), np.cos(ar), np.sin(ac), np.cos(ac)], -1).T, dtype=np.float32)


def _layout(inputs):
    import numpy as np
    g = {k: np.asarray(v) for k, v in inputs.items()}

    def on_partitions(v):
        return np.reshape(v, (-1, P)).T

    def on_all(v):
        return np.broadcast_to(np.reshape(v, (1, -1)), (P, np.size(v)))

    conv_w = np.concatenate([g["conv_ssd_w"][0], g["conv_dn_w"][0]], 1)
    parts = {
        "c": np.stack([on_partitions(g["c_ctx"]), on_partitions(g["c"][0])], 2).reshape(P, -1),
        "b_ada": on_partitions(g["b_ada"][0]),
        "norm1": on_partitions(g["norm1_w"][0]), "norm2": on_partitions(g["norm2_w"][0]), "final": on_partitions(g["final_norm_w"]),
        "ssd_norm": on_partitions(g["ssd_norm_w"][0]), "dn_norm": on_partitions(g["dn_norm_w"][0]),
        "ssd_d": on_partitions(np.repeat(g["ssd_d"][0], SSD_HEAD_DIM)),
        "conv_w": conv_w.reshape(CONV_W, -1, P).transpose(2, 1, 0).reshape(P, -1),
        "conv_b": on_partitions(np.concatenate([g["conv_ssd_b"][0], g["conv_dn_b"][0]])),
        "gate_bias": on_all(np.concatenate([g["ssd_dt_bias"].ravel(), g["dn_dt_bias"].ravel()])),
        "a_log": on_all(np.concatenate([g["ssd_a_log"].ravel(), g["dn_a_log"].ravel()])),
        "route_bias": on_all(np.concatenate([g["b_router_group"].ravel(), g["b_router_expert"].ravel()])),
    }
    parts["desc8"] = on_all(np.arange(8, 0, -1, dtype=np.float32))
    parts["tok_id"] = on_partitions(np.arange(TOK, dtype=np.float32))
    parts["eps"] = np.full((P, 1), EPS, np.float32)
    params = np.concatenate([parts[n] for n in PC], 1)
    h0 = np.stack([g["state_ssd_fwd"][0, 0], g["state_ssd_bwd"][0, 0]])
    h0 = h0.reshape(2, SSD_GROUPS, 8, SSD_HEAD_DIM, SSD_STATE).transpose(0, 1, 4, 2, 3).reshape(2, P, 512)
    s0 = np.stack([g["state_dn_fwd"][0, 0], g["state_dn_bwd"][0, 0]]).transpose(0, 2, 1, 3)
    router = np.concatenate([g["w_router_group"][0], g["w_router_expert"][0]], 1).reshape(KD, P, N_ROUTE).transpose(1, 0, 2)
    c = np.ascontiguousarray
    return {"x_t": c(g["x_prompt"][0].T), "xs_t": c(g["x_sample"][0].T), "pos_t": _positions(), "params": c(params), "masks": _masks(),
            "w_ada": g["w_ada"][0], "w_in": g["w_in"][0], "w_out": g["w_out"][0], "h0_ssd": c(h0), "s0_dn": c(s0), "router": c(router), "final_rows": c(on_all(g["final_norm_w"])),
            "w_gate": g["w_gate"][0], "w_up": g["w_up"][0], "w_down": g["w_down"][0]}


_INS = ["x_t", "xs_t", "pos_t", "params", "masks", "w_ada", "w_in", "w_out", "h0_ssd", "s0_dn", "router", "final_rows", "w_gate", "w_up", "w_down"]
_OUTS = [(SEQ, D_MODEL), (DEC_SEQ, D_MODEL), (SSD_WIDTH, SSD_STATE), (SSD_WIDTH, SSD_STATE), (P, DN_HEADS, P), (P, DN_HEADS, P)]


def kernel(**inputs):
    import numpy as np
    import concourse.bacc as _bacc
    from concourse import mybir as _mybir
    from concourse.bass_utils import run_bass_kernel_spmd as _run

    nc = _bacc.Bacc("TRN2", target_bir_lowering=False, num_devices=1)
    given = _layout(inputs)
    f32 = _mybir.dt.float32
    arrays = {f"in_{n}": given[n] for n in _INS}
    args = [nc.dram_tensor(f"in_{n}", given[n].shape, f32, kind="ExternalInput").ap() for n in _INS]
    h2_dram = nc.dram_tensor("h2_rows", (TOK, D_MODEL), f32, kind="Internal").ap()
    outs = [nc.dram_tensor(f"out_{i}", s, f32, kind="ExternalOutput").ap() for i, s in enumerate(_OUTS)]
    hybrid_step(nc, *args, h2_dram, outs)
    r = _run(nc, [arrays], core_ids=[0])
    y_p, y_s, s_f, s_b, d_f, d_b = (r.results[0][f"out_{i}"] for i in range(len(_OUTS)))
    ssd = (1, 1, SSD_HEADS, SSD_HEAD_DIM, SSD_STATE)
    return (y_p.reshape(1, SEQ, D_MODEL), y_s.reshape(1, DEC_SEQ, D_MODEL), s_f.reshape(ssd), s_b.reshape(ssd),
            np.ascontiguousarray(d_f.transpose(1, 0, 2))[None, None], np.ascontiguousarray(d_b.transpose(1, 0, 2))[None, None])
```
